# Optimizing a Trainium2 kernel written in Bass

```python
import math
import jax, jax.numpy as jnp
from jax import lax
import numpy as np

D_MODEL = 1024
BATCH = 1
SEQ = 256
DEPTH = 1

HEAD_DIM = 64
N_HEADS_A = 8
N_KV_A = 2
GROUP_A = N_HEADS_A // N_KV_A
WINDOW_A = 128
N_HEADS_B = 8
DILATED_PATTERNS = ((128, 1), (512, 4), (2048, 16))
WIDTH_A = N_HEADS_A * HEAD_DIM
WIDTH_B = N_HEADS_B * HEAD_DIM
D_MIX = WIDTH_A + WIDTH_B
KV_WIDTH_A = N_KV_A * HEAD_DIM
D_IN_PROJ = WIDTH_A + 2 * KV_WIDTH_A + 3 * WIDTH_B
N_BIAS_HEADS = N_HEADS_A + N_HEADS_B
NUM_BUCKETS = 32
MAX_DISTANCE = 1024
D_FF = 4 * D_MODEL
PLE_DIM = 256
EPS = 1e-6
NEG = -1e30


def rmsnorm(x, g):
    xf = x.astype(jnp.float32)
    y = xf * lax.rsqrt(jnp.mean(xf * xf, axis=-1, keepdims=True) + EPS)
    return (y * g.astype(jnp.float32)).astype(x.dtype)

def t5_bucket(rel):
    half = NUM_BUCKETS // 2
    max_exact = half // 2
    sign = jnp.where(rel > 0, half, 0)
    n = jnp.abs(rel)
    nf = jnp.maximum(n, 1).astype(jnp.float32)
    large = max_exact + (jnp.log(nf / max_exact) / math.log(MAX_DISTANCE / max_exact)
                         * (half - max_exact)).astype(jnp.int32)
    large = jnp.minimum(large, half - 1)
    return sign + jnp.where(n < max_exact, n, large)

def band_rel(block):
    qi = jnp.arange(block)[:, None]
    ki = jnp.arange(3 * block)[None, :]
    return ki - block - qi

def banded_attention(q, k, v, bias, half_window, block, sink):
    b_, hk, g, L, dh = q.shape
    nb = -(-L // block)
    lp = nb * block
    q = jnp.pad(q, ((0, 0), (0, 0), (0, 0), (0, lp - L), (0, 0)))
    kv_pad = ((0, 0), (0, 0), (block, lp - L + block), (0, 0))
    kp = jnp.pad(k, kv_pad).reshape(b_, hk, nb + 2, block, dh)
    vp = jnp.pad(v, kv_pad).reshape(b_, hk, nb + 2, block, dh)
    kw = jnp.concatenate([kp[:, :, :-2], kp[:, :, 1:-1], kp[:, :, 2:]], axis=3)
    vw = jnp.concatenate([vp[:, :, :-2], vp[:, :, 1:-1], vp[:, :, 2:]], axis=3)
    qb = q.reshape(b_, hk, g, nb, block, dh)
    s = jnp.einsum('bhgnqd,bhnkd->bhgnqk', qb, kw).astype(jnp.float32) * (dh ** -0.5)
    s = s + bias[:, :, None]
    rel = band_rel(block)
    kpos = jnp.arange(nb)[:, None, None] * block + jnp.arange(3 * block)[None, None, :] - block
    valid = (jnp.abs(rel) <= half_window)[None] & (kpos >= 0) & (kpos < L)
    s = jnp.where(valid, s, NEG)
    m = jnp.max(s, axis=-1, keepdims=True)
    if sink is not None:
        sinkb = sink.astype(jnp.float32)[None, :, :, None, None, None]
        m = jnp.maximum(m, sinkb)
    e = jnp.exp(s - m)
    denom = jnp.sum(e, axis=-1, keepdims=True)
    if sink is not None:
        denom = denom + jnp.exp(sinkb - m)
    o = jnp.einsum('bhgnqk,bhnkd->bhgnqd', e, vw.astype(jnp.float32)) / denom
    lse = (jnp.log(denom) + m)[..., 0]
    o = o.reshape(b_, hk, g, lp, dh)[:, :, :, :L].astype(k.dtype)
    lse = lse.reshape(b_, hk, g, lp)[..., :L]
    return o, lse

def windowed_gqa_sink(qa, ka, va, bias_table, sink):
    b_, s_, _ = qa.shape
    q = qa.reshape(b_, s_, N_KV_A, GROUP_A, HEAD_DIM).transpose(0, 2, 3, 1, 4)
    k = ka.reshape(b_, s_, N_KV_A, HEAD_DIM).transpose(0, 2, 1, 3)
    v = va.reshape(b_, s_, N_KV_A, HEAD_DIM).transpose(0, 2, 1, 3)
    bias = bias_table[t5_bucket(band_rel(WINDOW_A))][..., :N_HEADS_A]
    bias = bias.transpose(2, 0, 1).reshape(N_KV_A, GROUP_A, WINDOW_A, 3 * WINDOW_A)
    o, _ = banded_attention(q, k, v, bias.astype(jnp.float32), WINDOW_A, WINDOW_A,
                            sink.reshape(N_KV_A, GROUP_A))
    return o.transpose(0, 3, 1, 2, 4).reshape(b_, s_, WIDTH_A)

def dilated_mixture(qb_, kb_, vb_, bias_table):
    b_, s_, _ = qb_.shape
    to_heads = lambda t: t.reshape(b_, s_, N_HEADS_B, HEAD_DIM).transpose(0, 2, 1, 3)
    q, k, v = to_heads(qb_), to_heads(kb_), to_heads(vb_)
    outs, lses = [], []
    for window, dil in DILATED_PATTERNS:
        half = window // (2 * dil)
        ls = s_ // dil
        sub = lambda t: t.reshape(b_, N_HEADS_B, ls, dil, HEAD_DIM).transpose(0, 1, 3, 2, 4) \
                         .reshape(b_, N_HEADS_B * dil, ls, HEAD_DIM)
        bias = bias_table[t5_bucket(band_rel(half) * dil)][..., N_HEADS_A:]
        bias = jnp.repeat(bias.transpose(2, 0, 1), dil, axis=0)[:, None]
        o, lse = banded_attention(sub(q)[:, :, None], sub(k), sub(v),
                                  bias.astype(jnp.float32), half, half, None)
        o = o.reshape(b_, N_HEADS_B, dil, ls, HEAD_DIM).transpose(0, 1, 3, 2, 4) \
             .reshape(b_, N_HEADS_B, s_, HEAD_DIM)
        lse = lse.reshape(b_, N_HEADS_B, dil, ls).transpose(0, 1, 3, 2).reshape(b_, N_HEADS_B, s_)
        outs.append(o)
        lses.append(lse)
    w = jax.nn.softmax(jnp.stack(lses, axis=0), axis=0)
    o = jnp.sum(w[..., None] * jnp.stack(outs, axis=0).astype(jnp.float32), axis=0).astype(q.dtype)
    return o.transpose(0, 2, 1, 3).reshape(b_, s_, WIDTH_B)

def first_inputs(seed: int = 0) -> dict:
    key = jax.random.key(seed)
    ks = jax.random.split(key, 20)
    nrm = lambda k, shape, scale: (jax.random.normal(k, shape, jnp.float32) * scale)
    gain = lambda k, n: 1.0 + nrm(k, (DEPTH, n), 0.02)
    return {
        "x": nrm(ks[0], (BATCH, SEQ, D_MODEL), 1.0),
        "p": nrm(ks[1], (DEPTH, BATCH, SEQ, PLE_DIM), 1.0),
        "rel_bias_table": nrm(ks[2], (NUM_BUCKETS, N_BIAS_HEADS), 0.5),
        "g_pre_mix": gain(ks[3], D_MODEL),
        "w_in": nrm(ks[4], (DEPTH, D_MODEL, D_IN_PROJ), D_MODEL ** -0.5),
        "sink_a": nrm(ks[5], (DEPTH, N_HEADS_A), 0.5),
        "g_out_a": gain(ks[6], WIDTH_A),
        "g_out_b": gain(ks[7], WIDTH_B),
        "w_o": nrm(ks[8], (DEPTH, D_MIX, D_MODEL), D_MIX ** -0.5),
        "g_post_mix": gain(ks[9], D_MODEL),
        "g_pre_mlp": gain(ks[10], D_MODEL),
        "w_up": nrm(ks[11], (DEPTH, D_MODEL, D_FF), D_MODEL ** -0.5),
        "w_down": nrm(ks[12], (DEPTH, D_FF, D_MODEL), D_FF ** -0.5),
        "g_post_mlp": gain(ks[13], D_MODEL),
        "w_ple_proj": nrm(ks[14], (DEPTH, PLE_DIM, D_MODEL), PLE_DIM ** -0.5),
        "w_ple_gate": nrm(ks[15], (DEPTH, D_MODEL, D_MODEL), D_MODEL ** -0.5),
        "b_ple_gate": nrm(ks[16], (DEPTH, D_MODEL), 0.02),
        "g_post_ple": gain(ks[17], D_MODEL),
    }

def first_block(x, p, rel_bias_table, g_pre_mix, w_in, sink_a, g_out_a, g_out_b, w_o,
              g_post_mix, g_pre_mlp, w_up, w_down, g_post_mlp, w_ple_proj, w_ple_gate,
              b_ple_gate, g_post_ple):
    h = x
    offs = np.cumsum([0, WIDTH_A, KV_WIDTH_A, KV_WIDTH_A, WIDTH_B, WIDTH_B, WIDTH_B])
    for i in range(DEPTH):
        u = rmsnorm(h, g_pre_mix[i])
        proj = jnp.einsum('bsd,de->bse', u, w_in[i])
        qa, ka, va, qb, kb, vb = [proj[..., offs[j]:offs[j + 1]] for j in range(6)]
        o_a = rmsnorm(windowed_gqa_sink(qa, ka, va, rel_bias_table, sink_a[i]), g_out_a[i])
        o_b = rmsnorm(dilated_mixture(qb, kb, vb, rel_bias_table), g_out_b[i])
        mix = jnp.einsum('bse,ed->bsd', jnp.concatenate([o_a, o_b], axis=-1), w_o[i])
        h = h + rmsnorm(mix, g_post_mix[i])
        v_ = rmsnorm(h, g_pre_mlp[i])
        a = jax.nn.relu(jnp.einsum('bsd,df->bsf', v_, w_up[i]))
        ff = jnp.einsum('bsf,fd->bsd', a * a, w_down[i])
        h = h + rmsnorm(ff, g_post_mlp[i])
        gate = jax.nn.sigmoid(jnp.einsum('bsd,de->bse', h, w_ple_gate[i]) + b_ple_gate[i])
        ple = jnp.einsum('bsk,kd->bsd', p[i], w_ple_proj[i])
        h = h + rmsnorm(gate * ple, g_post_ple[i])
    return h


DEPTH_2 = 2

GRID_W = 64
CTX_LEN = 256
ATTN_QBLOCK = 128
ROPE_BASE = 10000.0

MLA_HEADS = 8
MLA_Q_RANK = 384
MLA_KV_RANK = 256
MLA_NOPE = 64
MLA_ROPE = 32
MLA_V = 64
ROPE_PAIRS = MLA_ROPE // 4
MLSTM_HEADS = 4
MLSTM_DH = 128
MLSTM_CONV = 3
MLSTM_CHUNK = 64
GLA_HEADS = 4
GLA_DK = 64
GLA_DV = 128
GLA_GATE_RANK = 16
GLA_TAU = 16.0
GLA_CHUNK = 64
NA_HEADS = 8
NA_DH = 64
NA_KH = 8
NA_KW = 16

BRANCH_A = MLA_HEADS * MLA_V
BRANCH_B = MLSTM_HEADS * MLSTM_DH
BRANCH_C = GLA_HEADS * GLA_DV
BRANCH_D = NA_HEADS * NA_DH
EVEN_SPLITS = (MLA_Q_RANK, MLA_KV_RANK, MLA_ROPE, BRANCH_B, BRANCH_B, BRANCH_B, BRANCH_B, 4 * MLSTM_HEADS, BRANCH_A + BRANCH_B)
ODD_SPLITS = (GLA_HEADS * GLA_DK, GLA_HEADS * GLA_DK, BRANCH_C, 2 * GLA_GATE_RANK, BRANCH_D, BRANCH_D, BRANCH_D, BRANCH_C + BRANCH_D)
EVEN_IN = sum(EVEN_SPLITS)
ODD_IN = sum(ODD_SPLITS)


def split_cols(a, sizes):
    return jnp.split(a, np.cumsum(sizes)[:-1].tolist(), axis=-1)

def rmsnorm_2(x, g):
    xf = x.astype(jnp.float32)
    xf = xf * lax.rsqrt(jnp.mean(xf * xf, axis=-1, keepdims=True) + EPS)
    return xf.astype(x.dtype) * g

def head_rmsnorm(x, g, n_heads):
    B, T, W = x.shape
    return rmsnorm_2(x.reshape(B, T, n_heads, W // n_heads), g.reshape(n_heads, -1)).reshape(B, T, W)

def to_heads(a, n_heads):
    B, T, W = a.shape
    return a.reshape(B, T, n_heads, W // n_heads).transpose(0, 2, 1, 3)

def merge_heads(a):
    B, H, T, d = a.shape
    return a.transpose(0, 2, 1, 3).reshape(B, T, H * d)

def centred_dwconv(x, w, b):
    K = w.shape[0]
    T = x.shape[1]
    pad = K // 2
    xp = jnp.pad(x, ((0, 0), (pad, K - 1 - pad), (0, 0)))
    y = xp[:, 0:T] * w[0]
    for j in range(1, K):
        y = y + xp[:, j:j + T] * w[j]
    return y + b

def rope2d_tables(S):
    t = jnp.arange(S)
    inv = 1.0 / (ROPE_BASE ** (jnp.arange(ROPE_PAIRS, dtype=jnp.float32) / ROPE_PAIRS))
    ang = jnp.concatenate([(t // GRID_W)[:, None] * inv, (t % GRID_W)[:, None] * inv], axis=-1)
    return jnp.cos(ang), jnp.sin(ang)

def apply_rope2d(x, cos, sin):
    cos = cos.astype(x.dtype)
    sin = sin.astype(x.dtype)
    parts = []
    for a in range(2):
        y = x[..., a * 2 * ROPE_PAIRS:(a + 1) * 2 * ROPE_PAIRS]
        y1, y2 = y[..., :ROPE_PAIRS], y[..., ROPE_PAIRS:]
        ca = cos[:, a * ROPE_PAIRS:(a + 1) * ROPE_PAIRS]
        sa = sin[:, a * ROPE_PAIRS:(a + 1) * ROPE_PAIRS]
        parts += [y1 * ca - y2 * sa, y2 * ca + y1 * sa]
    return jnp.concatenate(parts, axis=-1)

def to_chunks(a, L):
    B, H, T = a.shape[:3]
    return jnp.moveaxis(a.reshape(B, H, T // L, L, *a.shape[3:]), 2, 0)

def from_chunks(a):
    nc, B, H, L = a.shape[:4]
    return jnp.moveaxis(a, 0, 2).reshape(B, H, nc * L, *a.shape[4:])

def block_attention(q, k, v, scale):
    B, H, S, dq = q.shape
    nb = S // ATTN_QBLOCK
    qb = jnp.moveaxis(q.reshape(B, H, nb, ATTN_QBLOCK, dq), 2, 0)

    def one_block(qi):
        s = jnp.einsum('bhqd,bhkd->bhqk', qi, k).astype(jnp.float32) * scale
        p = jax.nn.softmax(s, axis=-1).astype(v.dtype)
        return jnp.einsum('bhqk,bhkd->bhqd', p, v)

    o = lax.map(one_block, qb)
    return jnp.moveaxis(o, 0, 2).reshape(B, H, S, v.shape[-1])

def mlstm_chunked(q, k, v, ig, lf, state):
    L = MLSTM_CHUNK
    causal = jnp.tril(jnp.ones((L, L), dtype=bool))

    def step(carry, xs):
        C, n, m = carry
        qc, kc, vc, ic, fc = xs
        b = jnp.cumsum(fc, axis=-1)
        logw = jnp.where(causal, b[..., :, None] - b[..., None, :] + ic[..., None, :], -jnp.inf)
        inter = b + m[..., None]
        m_t = jnp.maximum(inter, jnp.max(logw, axis=-1))
        w_intra = jnp.exp(logw - m_t[..., None])
        w_inter = jnp.exp(inter - m_t)
        qk = jnp.einsum('bhtd,bhsd->bhts', qc, kc) * w_intra
        num = jnp.einsum('bhts,bhsv->bhtv', qk, vc) + w_inter[..., None] * jnp.einsum('bhtd,bhdv->bhtv', qc, C)
        den = jnp.sum(qk, axis=-1) + w_inter * jnp.einsum('bhtd,bhd->bht', qc, n)
        h = num / jnp.maximum(jnp.abs(den), jnp.exp(-m_t))[..., None]
        b_last = b[..., -1]
        logk = b_last[..., None] - b + ic
        m_new = jnp.maximum(b_last + m, jnp.max(logk, axis=-1))
        carry_decay = jnp.exp(b_last + m - m_new)
        kw = jnp.exp(logk - m_new[..., None])[..., None] * kc
        C = carry_decay[..., None, None] * C + jnp.einsum('bhsd,bhsv->bhdv', kw, vc)
        n = carry_decay[..., None] * n + jnp.sum(kw, axis=2)
        return (C, n, m_new), h

    xs = tuple(to_chunks(a.astype(jnp.float32), L) for a in (q, k, v, ig, lf))
    state, h = lax.scan(step, state, xs)
    return from_chunks(h), state

def gla_chunked(q, k, v, lg, S0):
    L = GLA_CHUNK
    causal = jnp.tril(jnp.ones((L, L), dtype=bool))

    def step(S, xs):
        qc, kc, vc, gc = xs
        bcum = jnp.cumsum(gc, axis=2)
        rel = bcum[:, :, :, None, :] - bcum[:, :, None, :, :]
        decay = jnp.exp(jnp.where(causal[:, :, None], rel, -jnp.inf))
        att = jnp.einsum('bhtd,bhsd,bhtsd->bhts', qc, kc, decay)
        o = jnp.einsum('bhts,bhsv->bhtv', att, vc) + jnp.einsum('bhtd,bhdv->bhtv', qc * jnp.exp(bcum), S)
        b_last = bcum[:, :, -1:]
        S_new = jnp.exp(b_last[:, :, 0])[..., None] * S + jnp.einsum('bhsd,bhsv->bhdv', kc * jnp.exp(b_last - bcum), vc)
        return S_new, o

    xs = tuple(to_chunks(a.astype(jnp.float32), L) for a in (q, k, v, lg))
    S, o = lax.scan(step, S0, xs)
    return from_chunks(o), S

def bidirectional_scan(chunk_fn, init_state, shared_c, gates_c, shared_l, gates_l):
    outs_c, outs_l = [], []
    for d in range(2):
        if d == 0:
            f = lambda a: a
        else:
            f = lambda a: jnp.flip(a, axis=2)
        hc, st = chunk_fn(*[f(a) for a in shared_c], *[f(g[d]) for g in gates_c], init_state)
        hl, _ = chunk_fn(*[f(a) for a in shared_l], *[f(g[d]) for g in gates_l], st)
        outs_c.append(f(hc))
        outs_l.append(f(hl))
    return outs_c[0] + outs_c[1], outs_l[0] + outs_l[1]

def neighbourhood_attention(q, k, v, k_ctx, v_ctx, rpb, rows):
    B, H, S, d = q.shape
    kh = min(NA_KH, rows)
    qg = q.reshape(B, H, rows, GRID_W, d)
    kg = k.reshape(B, H, rows, GRID_W, d)
    vg = v.reshape(B, H, rows, GRID_W, d)
    r_idx = jnp.arange(rows)
    c_idx = jnp.arange(GRID_W)
    win_rows = jnp.clip(r_idx - kh // 2, 0, rows - kh)[:, None] + jnp.arange(kh)
    win_cols = jnp.clip(c_idx - NA_KW // 2, 0, GRID_W - NA_KW)[:, None] + jnp.arange(NA_KW)
    dcol = win_cols - c_idx[:, None] + (NA_KW - 1)
    scale = d ** -0.5
    n_loc = kh * NA_KW

    def one_row(r):
        rws = win_rows[r]
        drow = rws - r + (NA_KH - 1)
        bias = rpb[:, drow[None, :, None], dcol[:, None, :]].astype(jnp.float32)
        qr = qg[:, :, r]
        kw = kg[:, :, rws][:, :, :, win_cols]
        vw = vg[:, :, rws][:, :, :, win_cols]
        s_loc = jnp.einsum('bhcd,bhicjd->bhcij', qr, kw).astype(jnp.float32) * scale + bias
        s_ctx = jnp.einsum('bhcd,bhnd->bhcn', qr, k_ctx).astype(jnp.float32) * scale
        logits = jnp.concatenate([s_loc.reshape(B, H, GRID_W, n_loc), s_ctx], axis=-1)
        p = jax.nn.softmax(logits, axis=-1).astype(v.dtype)
        p_loc = p[..., :n_loc].reshape(B, H, GRID_W, kh, NA_KW)
        return jnp.einsum('bhcij,bhicjd->bhcd', p_loc, vw) + jnp.einsum('bhcn,bhnd->bhcd', p[..., n_loc:], v_ctx)

    o = lax.map(one_row, r_idx)
    return jnp.moveaxis(o, 0, 2).reshape(B, H, S, d)

def mla_mlstm_mixer(u_lat, u_ctx, cos, sin, w_in, q_norm, w_uq, kv_norm, w_ukv, conv_w, conv_b, b_i, b_f, h_norm, w_out, need_ctx):
    def project(u, rotate):
        B, T, _ = u.shape
        cq, ckv, k_rope, mq, mk, mv, mo, gates, z = split_cols(u @ w_in, EVEN_SPLITS)
        q = to_heads(rmsnorm_2(cq, q_norm) @ w_uq, MLA_HEADS)
        kv = to_heads(rmsnorm_2(ckv, kv_norm) @ w_ukv, MLA_HEADS)
        q_nope, q_rope = q[..., :MLA_NOPE], q[..., MLA_NOPE:]
        k_nope, v = kv[..., :MLA_NOPE], kv[..., MLA_NOPE:]
        k_rope = k_rope[:, None]
        if rotate:
            q_rope = apply_rope2d(q_rope, cos, sin)
            k_rope = apply_rope2d(k_rope, cos, sin)
        q = jnp.concatenate([q_nope, q_rope], axis=-1)
        k = jnp.concatenate([k_nope, jnp.broadcast_to(k_rope, (B, MLA_HEADS, T, MLA_ROPE))], axis=-1)
        qk = jax.nn.silu(centred_dwconv(jnp.concatenate([mq, mk], axis=-1), conv_w, conv_b))
        mq = to_heads(qk[..., :BRANCH_B], MLSTM_HEADS) * MLSTM_DH ** -0.5
        mk = to_heads(qk[..., BRANCH_B:], MLSTM_HEADS)
        mv = to_heads(mv, MLSTM_HEADS)
        g = gates.reshape(B, T, 2, 2, MLSTM_HEADS).astype(jnp.float32)
        ig = (g[:, :, :, 0] + b_i).transpose(2, 0, 3, 1)
        lf = jax.nn.log_sigmoid(g[:, :, :, 1] + b_f).transpose(2, 0, 3, 1)
        return (q, k, v), (mq, mk, mv), (ig, lf), mo, z

    (qa_l, ka_l, va_l), seq_l, gates_l, mo_l, z_l = project(u_lat, True)
    (qa_c, ka_c, va_c), seq_c, gates_c, mo_c, z_c = project(u_ctx, False)
    scale = (MLA_NOPE + MLA_ROPE) ** -0.5
    a_lat = block_attention(qa_l, jnp.concatenate([ka_c, ka_l], axis=2), jnp.concatenate([va_c, va_l], axis=2), scale)
    B = u_lat.shape[0]
    init = (jnp.zeros((B, MLSTM_HEADS, MLSTM_DH, MLSTM_DH), jnp.float32),
            jnp.zeros((B, MLSTM_HEADS, MLSTM_DH), jnp.float32),
            jnp.zeros((B, MLSTM_HEADS), jnp.float32))
    h_c, h_l = bidirectional_scan(mlstm_chunked, init, seq_c, gates_c, seq_l, gates_l)

    def combine(a, h, mo, z, dtype):
        hm = head_rmsnorm(jax.nn.sigmoid(mo.astype(jnp.float32)) * merge_heads(h), h_norm, MLSTM_HEADS).astype(dtype)
        return (jnp.concatenate([merge_heads(a), hm], axis=-1) * jax.nn.silu(z)) @ w_out

    y_lat = combine(a_lat, h_l, mo_l, z_l, u_lat.dtype)
    y_ctx = None
    if need_ctx:
        y_ctx = combine(block_attention(qa_c, ka_c, va_c, scale), h_c, mo_c, z_c, u_ctx.dtype)
    return y_lat, y_ctx

def gla_na_mixer(u_lat, u_ctx, rows, w_in, w_gate, b_gate, gla_norm, rpb, w_out, need_ctx):
    def project(u):
        B, T, _ = u.shape
        gq, gk, gv, ga, nq, nk, nv, z = split_cols(u @ w_in, ODD_SPLITS)
        ga = ga.reshape(B, T, 2, GLA_GATE_RANK)
        lg = jax.nn.log_sigmoid(jnp.einsum('btdr,drk->dbtk', ga, w_gate).astype(jnp.float32) + b_gate[:, None, None]) / GLA_TAU
        lg = lg.reshape(2, B, T, GLA_HEADS, GLA_DK).transpose(0, 1, 3, 2, 4)
        seq = (to_heads(gq, GLA_HEADS) * GLA_DK ** -0.5, to_heads(gk, GLA_HEADS), to_heads(gv, GLA_HEADS))
        na = (to_heads(nq, NA_HEADS), to_heads(nk, NA_HEADS), to_heads(nv, NA_HEADS))
        return seq, (lg,), na, z

    seq_l, gates_l, (nq_l, nk_l, nv_l), z_l = project(u_lat)
    seq_c, gates_c, (nq_c, nk_c, nv_c), z_c = project(u_ctx)
    B = u_lat.shape[0]
    init = jnp.zeros((B, GLA_HEADS, GLA_DK, GLA_DV), jnp.float32)
    o_c, o_l = bidirectional_scan(gla_chunked, init, seq_c, gates_c, seq_l, gates_l)
    na_l = neighbourhood_attention(nq_l, nk_l, nv_l, nk_c, nv_c, rpb, rows)

    def combine(o, na, z, dtype):
        g = head_rmsnorm(merge_heads(o), gla_norm, GLA_HEADS).astype(dtype)
        return (jnp.concatenate([g, merge_heads(na)], axis=-1) * jax.nn.silu(z)) @ w_out

    y_lat = combine(o_l, na_l, z_l, u_lat.dtype)
    y_ctx = None
    if need_ctx:
        y_ctx = combine(o_c, block_attention(nq_c, nk_c, nv_c, NA_DH ** -0.5), z_c, u_ctx.dtype)
    return y_lat, y_ctx

def second_inputs(seed: int = 0) -> dict:
    key = jax.random.key(seed)
    keys = iter(jax.random.split(key, 32))

    def rnd(shape, s):
        return jax.random.normal(next(keys), shape, jnp.float32) * s

    def gain(n):
        return 1.0 + rnd((n,), 0.05)

    D = D_MODEL
    return {
        'x': rnd((BATCH, SEQ, D), 1.0),
        'c': rnd((BATCH, D), 1.0),
        'ctx': rnd((BATCH, CTX_LEN, D), 1.0),
        'c_ctx': rnd((D,), 1.0),
        'l0_norm': gain(D),
        'l0_w_mod': rnd((D, 3 * D), 0.5 * D ** -0.5),
        'l0_b_mod': rnd((3 * D,), 0.02),
        'l0_w_in': rnd((D, EVEN_IN), D ** -0.5),
        'l0_mla_q_norm': gain(MLA_Q_RANK),
        'l0_mla_w_uq': rnd((MLA_Q_RANK, MLA_HEADS * (MLA_NOPE + MLA_ROPE)), MLA_Q_RANK ** -0.5),
        'l0_mla_kv_norm': gain(MLA_KV_RANK),
        'l0_mla_w_ukv': rnd((MLA_KV_RANK, MLA_HEADS * (MLA_NOPE + MLA_V)), MLA_KV_RANK ** -0.5),
        'l0_mlstm_conv_w': rnd((MLSTM_CONV, 2 * BRANCH_B), MLSTM_CONV ** -0.5),
        'l0_mlstm_conv_b': rnd((2 * BRANCH_B,), 0.02),
        'l0_mlstm_b_i': rnd((2, MLSTM_HEADS), 0.1),
        'l0_mlstm_b_f': jnp.linspace(3.0, 6.0, MLSTM_HEADS)[None] + rnd((2, MLSTM_HEADS), 0.1),
        'l0_mlstm_norm': gain(BRANCH_B),
        'l0_w_out': rnd((BRANCH_A + BRANCH_B, D), (BRANCH_A + BRANCH_B) ** -0.5),
        'l1_norm': gain(D),
        'l1_w_mod': rnd((D, 3 * D), 0.5 * D ** -0.5),
        'l1_b_mod': rnd((3 * D,), 0.02),
        'l1_w_in': rnd((D, ODD_IN), D ** -0.5),
        'l1_gla_w_gate': rnd((2, GLA_GATE_RANK, GLA_HEADS * GLA_DK), GLA_GATE_RANK ** -0.5),
        'l1_gla_b_gate': rnd((2, GLA_HEADS * GLA_DK), 0.5),
        'l1_gla_norm': gain(BRANCH_C),
        'l1_na_rpb': rnd((NA_HEADS, 2 * NA_KH - 1, 2 * NA_KW - 1), 0.1),
        'l1_w_out': rnd((BRANCH_C + BRANCH_D, D), (BRANCH_C + BRANCH_D) ** -0.5),
        'final_norm': gain(D),
    }

def second_block(x, c, ctx, c_ctx,
              l0_norm, l0_w_mod, l0_b_mod, l0_w_in, l0_mla_q_norm, l0_mla_w_uq, l0_mla_kv_norm, l0_mla_w_ukv,
              l0_mlstm_conv_w, l0_mlstm_conv_b, l0_mlstm_b_i, l0_mlstm_b_f, l0_mlstm_norm, l0_w_out,
              l1_norm, l1_w_mod, l1_b_mod, l1_w_in, l1_gla_w_gate, l1_gla_b_gate, l1_gla_norm, l1_na_rpb, l1_w_out,
              final_norm):
    S = x.shape[1]
    rows = S // GRID_W
    cos, sin = rope2d_tables(S)
    norms = (l0_norm, l1_norm)
    mods = ((l0_w_mod, l0_b_mod), (l1_w_mod, l1_b_mod))
    mixer_params = (
        (l0_w_in, l0_mla_q_norm, l0_mla_w_uq, l0_mla_kv_norm, l0_mla_w_ukv, l0_mlstm_conv_w, l0_mlstm_conv_b,
         l0_mlstm_b_i, l0_mlstm_b_f, l0_mlstm_norm, l0_w_out),
        (l1_w_in, l1_gla_w_gate, l1_gla_b_gate, l1_gla_norm, l1_na_rpb, l1_w_out),
    )
    h_lat, h_ctx = x, ctx
    for layer in range(DEPTH_2):
        need_ctx = layer < DEPTH_2 - 1
        w_mod, b_mod = mods[layer]
        shift_l, scale_l, gate_l = jnp.split(jax.nn.silu(c) @ w_mod + b_mod, 3, axis=-1)
        shift_c, scale_c, gate_c = jnp.split(jax.nn.silu(c_ctx) @ w_mod + b_mod, 3, axis=-1)
        u_lat = rmsnorm_2(h_lat, norms[layer]) * (1 + scale_l[:, None]) + shift_l[:, None]
        u_ctx = rmsnorm_2(h_ctx, norms[layer]) * (1 + scale_c) + shift_c
        if layer % 2 == 0:
            y_lat, y_ctx = mla_mlstm_mixer(u_lat, u_ctx, cos, sin, *mixer_params[layer], need_ctx=need_ctx)
        else:
            y_lat, y_ctx = gla_na_mixer(u_lat, u_ctx, rows, *mixer_params[layer], need_ctx=need_ctx)
        h_lat = h_lat + gate_l[:, None] * y_lat
        if need_ctx:
            h_ctx = h_ctx + gate_c * y_ctx
    return rmsnorm_2(h_lat, final_norm)


def setup_inputs(seed=0):
    out = dict(first_inputs(seed))
    for name, value in second_inputs(seed + 1).items():
        if name != "x":
            out[name + "_2"] = value
    return out


def reference(
    x, p, rel_bias_table, g_pre_mix, w_in, sink_a, g_out_a, g_out_b, w_o, g_post_mix, g_pre_mlp,
    w_up, w_down, g_post_mlp, w_ple_proj, w_ple_gate, b_ple_gate, g_post_ple, c_2, ctx_2,
    c_ctx_2, l0_norm_2, l0_w_mod_2, l0_b_mod_2, l0_w_in_2, l0_mla_q_norm_2, l0_mla_w_uq_2,
    l0_mla_kv_norm_2, l0_mla_w_ukv_2, l0_mlstm_conv_w_2, l0_mlstm_conv_b_2, l0_mlstm_b_i_2,
    l0_mlstm_b_f_2, l0_mlstm_norm_2, l0_w_out_2, l1_norm_2, l1_w_mod_2, l1_b_mod_2, l1_w_in_2,
    l1_gla_w_gate_2, l1_gla_b_gate_2, l1_gla_norm_2, l1_na_rpb_2, l1_w_out_2, final_norm_2,
):
    x = first_block(
        x, p, rel_bias_table, g_pre_mix, w_in, sink_a, g_out_a, g_out_b, w_o, g_post_mix,
        g_pre_mlp, w_up, w_down, g_post_mlp, w_ple_proj, w_ple_gate, b_ple_gate, g_post_ple,
    )
    return second_block(
        x, c_2, ctx_2, c_ctx_2, l0_norm_2, l0_w_mod_2, l0_b_mod_2, l0_w_in_2, l0_mla_q_norm_2,
        l0_mla_w_uq_2, l0_mla_kv_norm_2, l0_mla_w_ukv_2, l0_mlstm_conv_w_2, l0_mlstm_conv_b_2,
        l0_mlstm_b_i_2, l0_mlstm_b_f_2, l0_mlstm_norm_2, l0_w_out_2, l1_norm_2, l1_w_mod_2,
        l1_b_mod_2, l1_w_in_2, l1_gla_w_gate_2, l1_gla_b_gate_2, l1_gla_norm_2, l1_na_rpb_2,
        l1_w_out_2, final_norm_2,
    )


_drawn_inputs = setup_inputs


def setup_inputs(seed=0):
    import zlib

    import numpy as np

    out = dict(_drawn_inputs(seed))
    spreads = {}
    factors = {'sink_a': 8.0,
     'g_out_a': 5.811,
     'g_out_b': 5.776,
     'g_post_mix': 4.215,
     'g_pre_mlp': 4.786,
     'g_post_mlp': 5.174,
     'b_ple_gate': 8.0,
     'g_post_ple': 5.694,
     'ctx_2': 3.012,
     'l0_norm_2': 8.0,
     'l0_b_mod_2': 8.0,
     'l0_mla_q_norm_2': 8.0,
     'l0_mla_w_uq_2': 8.0,
     'l0_mla_kv_norm_2': 8.0,
     'l0_mla_w_ukv_2': 2.84,
     'l0_mlstm_conv_b_2': 64.0,
     'l0_mlstm_b_i_2': 64.0,
     'l0_mlstm_b_f_2': 2.682,
     'l0_mlstm_norm_2': 8.0,
     'l1_norm_2': 6.475,
     'l1_b_mod_2': 7.459,
     'l1_gla_w_gate_2': 3.41,
     'l1_gla_b_gate_2': 8.612,
     'l1_gla_norm_2': 35.781,
     'l1_na_rpb_2': 45.976}
    for name, (base, spread) in spreads.items():
        noise = np.random.default_rng([zlib.crc32(name.encode()), seed]).standard_normal(out[name].shape)
        drawn = base * np.exp(spread * noise) if base else spread * noise
        out[name] = __import__('jax').numpy.asarray(drawn.astype(out[name].dtype))
    for name, factor in factors.items():
        out[name] = (out[name] * factor).astype(out[name].dtype)
    return out
```

```python
import math
from contextlib import ExitStack

import numpy as np
import concourse.bass as bass
from concourse import mybir

ALU = mybir.AluOpType
ACT = mybir.ActivationFunctionType
F32 = mybir.dt.float32
U8 = mybir.dt.uint8
AX_X = mybir.AxisListType.X

P = 128
D = 1024
KT = D // P
S = 256
EPS = 1e-6
NEG = -1e30
BANK = 512

HD = 64
NHA, NKVA, NHB = 8, 2, 8
WINDOW_A = 128
DILATED = ((128, 1), (512, 4), (2048, 16))
WA, KVA, WB = NHA * HD, NKVA * HD, NHB * HD
D_FF = 4 * D
PLE = 256
NUM_BUCKETS, MAX_DISTANCE = 32, 1024

GRID_W = 64
ROWS = S // GRID_W
MLA_H, Q_RANK, KV_RANK, NOPE, ROPE, MLA_V = 8, 384, 256, 64, 32, 64
QK = NOPE + ROPE
PAIRS = ROPE // 4
ML_H, ML_D = 4, 128
GLA_H, GLA_DK, GLA_DV, GLA_RANK, GLA_TAU = 4, 64, 128, 16, 16.0
NA_H, NA_D, NA_KH, NA_KW = 8, 64, 8, 16
E_SIZES = (Q_RANK, KV_RANK, ROPE, 512, 512, 512, 512, 4 * ML_H, 1024)
O_SIZES = (256, 256, 512, 2 * GLA_RANK, 512, 512, 512, 1024)
E_OFF = [sum(E_SIZES[:i]) for i in range(len(E_SIZES) + 1)]
O_OFF = [sum(O_SIZES[:i]) for i in range(len(O_SIZES) + 1)]
GLA_LEVELS = [1 << i for i in range(7)]

COLS = {}
_n = 0
for _name, _w in (("g_pre_mix", 8), ("g_out_a", 4), ("g_out_b", 4), ("g_pre_mlp", 8), ("l0_norm", 8),
                  ("l1_norm", 8), ("l0_b_mod", 24), ("l1_b_mod", 24), ("q_norm", 3), ("kv_norm", 2),
                  ("h_norm", 4), ("gla_norm", 4), ("conv_b", 8), ("conv_w", 24), ("c", 16)):
    COLS[_name] = (_n, _w)
    _n += _w
NCOLS = _n
ROWS_ORDER = ("g_post_mix", "g_post_mlp", "b_ple_gate", "g_post_ple", "l0_b_gate", "l1_b_gate", "final_norm")
SQ = {n: i for i, n in enumerate(("ident", "ones", "tri_u", "tri_l", "tri_u16", "ones16a", "ones16b", "tri_l16",
                                  "neg_u", "neg_l"))}


class Engine:

    def __init__(self, e, sem):
        self.e, self.sem, self.count, self.seen = e, sem, 0, {}

    def wait(self, marks):
        for sem, value in marks:
            if self.seen.get(id(sem), 0) < value:
                self.e.wait_ge(sem, value)
                self.seen[id(sem)] = value

    def last(self):
        return [(self.sem, self.count)] if self.count else []


def step(eng, after, method, *args, **kw):
    eng.wait(after)
    method(*args, **kw).then_inc(eng.sem, 1)
    eng.count += 1
    return (eng.sem, eng.count)


def build(nc, ins, out, dump=None):
    ctx = ExitStack()
    with ctx:
        _build(nc, ctx, ins, out, dump)


def _build(nc, ctx, ins, out, dump):
    def sb(name, shape, dt=F32):
        return ctx.enter_context(nc.sbuf_tensor(name, shape, dt))

    def new_sem(name):
        return ctx.enter_context(nc.semaphore(name))

    PE = Engine(nc.tensor, new_sem("pe_done"))
    DV = Engine(nc.vector, new_sem("dve_done"))
    AC = Engine(nc.scalar, new_sem("act_done"))
    GP = Engine(nc.gpsimd, new_sem("pool_done"))
    SP = Engine(nc.sync, new_sem("sp_done"))
    COMPUTE = (PE, DV, AC, GP)
    v, a, g, t = nc.vector, nc.scalar, nc.gpsimd, nc.tensor

    sq = sb("sq", [P, len(SQ) * P])
    cols = sb("cols", [P, NCOLS])
    lnc = sb("lnc", [P, 384])
    selneg = sb("selneg", [4, 4 * P])
    sel2 = sb("sel2", [2, 2 * P])
    gla_mask = sb("gla_mask", [P, 14 * P], U8)
    rope = sb("rope", [P, 2, 2, 2 * PAIRS])
    small_rows = sb("small_rows", [P, 8 + 16])
    wgate = sb("wgate", [2 * GLA_RANK + 1, 512])
    H = sb("H", [P, 4, D])
    uT = sb("uT", [P, KT, 512])
    NSLOT = 3
    wslot = sb("wslot", [P, NSLOT, KT * 512])
    rowbuf = sb("rowbuf", [P, 4, D])
    probs = sb("probs", [P, 4, 512])
    probsT = sb("probsT", [P, 4, 512])
    xn = sb("xn", [P, 2, D])
    stats = sb("stats", [P, 1100])
    ARENA = 15616
    arena = sb("arena", [P, ARENA])
    banks = ctx.enter_context(nc.psum_tensor("banks", [P, 8, BANK], F32))

    def sqc(name):
        i = SQ[name]
        return sq[:, i * P:(i + 1) * P]

    ident = sqc("ident")

    def col(name, j0=0, n=None):
        c0, w = COLS[name]
        return cols[:, c0 + j0:c0 + (w if n is None else j0 + n)]

    stat_at = [0]

    def stat(n=1):
        stat_at[0] += n
        assert stat_at[0] <= 1100, stat_at
        return stats[:, stat_at[0] - n:stat_at[0]]

    def carve(base, *shape):
        n = int(np.prod(shape))
        assert base + n <= ARENA, (base, n)
        view = arena[:, base:base + n]
        if len(shape) == 2:
            view = view.rearrange("p (a b) -> p a b", a=shape[0])
        elif len(shape) == 3:
            view = view.rearrange("p (a b c) -> p a b c", a=shape[0], b=shape[1])
        elif len(shape) == 4:
            view = view.rearrange("p (a b c d) -> p a b c d", a=shape[0], b=shape[1], c=shape[2])
        return view, base + n

    def bc(ap, n):
        return ap.unsqueeze(len(ap.shape)).to_broadcast(list(ap.shape) + [n])

    bank_free = [[] for _ in range(8)]

    class Pool:

        def __init__(self, which):
            self.which, self.n = list(which), 0

        def take(self):
            b = self.which[self.n % len(self.which)]
            self.n += 1
            free = bank_free[b]
            assert free is not None, b
            bank_free[b] = None
            return b, banks[:, b, :], free

    def give(b, marks):
        bank_free[b] = list(marks)

    loads = {}
    def load(eng, name, dst, src, after=(), sem=None):
        eng.wait(after)
        s_ = sem or new_sem("ld_" + name)
        eng.e.dma_start(dst, src).then_inc(s_, 16)
        loads[name] = (s_, 16)
        return (s_, 16)

    def kview(w, k0, k1, c0, c1):
        return w[k0 * P:k1 * P, c0:c1].rearrange("(k p) n -> p k n", p=P)

    chunks = []

    def chunk(name, *parts):
        chunks.append((name, parts))

    w_in = "w_in"
    chunk("qa", (w_in, 0, 8, 0, 512))
    chunk("kva", (w_in, 0, 8, 512, 768))
    chunk("qb", (w_in, 0, 8, 768, 1280))
    chunk("kb", (w_in, 0, 8, 1280, 1792))
    chunk("vb", (w_in, 0, 8, 1792, 2304))
    for c in range(2):
        chunk(f"wo{c}", ("w_o", 0, 8, c * 512, c * 512 + 512))
    for c in range(8):
        chunk(f"up{c}", ("w_up", 0, 8, c * 512, c * 512 + 512))
    for c in range(2):
        for k in range(4):
            chunk(f"down{c}{k}", ("w_down", 8 * k, 8 * k + 8, c * 512, c * 512 + 512))
    chunk("ple", ("w_ple_proj", 0, 2, 0, 1024))
    for c in range(2):
        chunk(f"pg{c}", ("w_ple_gate", 0, 8, c * 512, c * 512 + 512))
    for c in range(6):
        chunk(f"mod0{c}", ("l0_w_mod", 0, 8, c * 512, c * 512 + 512))
    eo = E_OFF
    chunk("cq", ("l0_w_in", 0, 8, eo[0], eo[1]))
    chunk("ckv", ("l0_w_in", 0, 8, eo[1], eo[3]), ("l0_w_in", 0, 8, eo[7], eo[8]))
    chunk("uq", ("w_uq", 0, 3, 0, 768))
    chunk("ukv", ("w_ukv", 0, 2, 0, 1024))
    for i, n in ((3, "mq"), (4, "mk"), (5, "mv"), (6, "mo")):
        chunk(n, ("l0_w_in", 0, 8, eo[i], eo[i + 1]))
    for c in range(2):
        chunk(f"z0{c}", ("l0_w_in", 0, 8, eo[8] + 512 * c, eo[8] + 512 * c + 512))
    for c in range(2):
        chunk(f"out0{c}", ("l0_w_out", 0, 8, c * 512, c * 512 + 512))
    for c in range(6):
        chunk(f"mod1{c}", ("l1_w_mod", 0, 8, c * 512, c * 512 + 512))
    oo = O_OFF
    chunk("gqk", ("l1_w_in", 0, 8, 0, 512))
    chunk("gv", ("l1_w_in", 0, 8, oo[2], oo[3]))
    chunk("ga", ("l1_w_in", 0, 8, oo[3], oo[4]))
    for i, n in ((4, "nq"), (5, "nk"), (6, "nv")):
        chunk(n, ("l1_w_in", 0, 8, oo[i], oo[i + 1]))
    for c in range(2):
        chunk(f"z1{c}", ("l1_w_in", 0, 8, oo[7] + 512 * c, oo[7] + 512 * c + 512))
    for c in range(2):
        chunk(f"out1{c}", ("l1_w_out", 0, 8, c * 512, c * 512 + 512))

    slot_sem = [new_sem(f"weights_in_slot{i}") for i in range(NSLOT)]
    slot_count = [0] * NSLOT
    chunk_mark = {}

    def slot_view(i):
        parts = chunks[i][1]
        kt = parts[0][2] - parts[0][1]
        n = sum(p[4] - p[3] for p in parts)
        return wslot[:, i % NSLOT, 0:kt * n].rearrange("p (k n) -> p k n", k=kt)

    def load_chunk(i, after):
        if i >= len(chunks):
            return
        SP.wait(after)
        view, at, k = slot_view(i), 0, i % NSLOT
        for name, k0, k1, c0, c1 in chunks[i][1]:
            SP.e.dma_start(view[:, :, at:at + c1 - c0], kview(ins[name], k0, k1, c0, c1)).then_inc(slot_sem[k], 16)
            slot_count[k] += 16
            at += c1 - c0
        chunk_mark[i] = loads[f"slot{k}"] = (slot_sem[k], slot_count[k])

    chunk_at = [0]

    def weights(name):
        i = chunk_at[0]
        assert chunks[i][0] == name, (chunks[i][0], name)
        chunk_at[0] += 1
        return slot_view(i), [chunk_mark[i]], i

    def used(i, mark):
        load_chunk(i + NSLOT, [mark])

    def products(after, terms):
        PE.wait(after)
        for i, (o, l, r) in enumerate(terms):
            m = t.matmul(o, l, r, start=(i == 0), stop=(i == len(terms) - 1))
        m.then_inc(PE.sem, 1)
        PE.count += 1
        return (PE.sem, PE.count)

    def project_tm(pool, name, srcT, src_marks, tiles, evac, c0=0, n=None, kt=KT, last=True, view=None):
        w, wm, i = view or weights(name)
        n = n or min(512, w.shape[2] - c0)
        for tile in tiles:
            b, ps, free = pool.take()
            m = products(free + wm + list(src_marks(tile)),
                         [(ps[:, 0:n], srcT[:, k, tile * P:(tile + 1) * P], w[:, k, c0:c0 + n]) for k in range(kt)])
            give(b, evac(tile, ps, m))
        if last:
            used(i, m)
        return (w, wm, i)

    def project_fm(pool, name, srcT, src_marks, t0, nt, fts, lhs, evac, last=True, view=None):
        w, wm, i = view or weights(name)
        for ft in fts:
            b, ps, free = pool.take()
            m = products(free + wm + src_marks, [(ps[:, 0:nt], lhs(w, k, ft), srcT[:, k, t0:t0 + nt]) for k in range(KT)])
            give(b, evac(ft, ps, m))
        if last:
            used(i, m)
        return (w, wm, i)

    junk_mark = [[]]

    def rstd_of(srcs, width, after, junk=None):
        n = len(srcs)
        ss, r = stat(n), stat(n)
        ms = []
        for i, s_ in enumerate(srcs):
            j = junk if junk is not None else probs[:, 0:2, :].rearrange("p a b -> p (a b)")
            m = step(AC, list(after[i]) + junk_mark[0], a.activation, j[:, 0:width], s_, ACT.Square, accum_out=ss[:, i:i + 1])
            junk_mark[0] = [m]
            ms.append(m)
        m = step(AC, ms, a.activation, ss, ss, ACT.Ln, scale=1.0 / width, bias=eps_col[:, 0:1])
        m = step(AC, [m], a.activation, r, ss, ACT.Exp, scale=-0.5)
        return r, m, ms

    xn_free = [[], []]
    xn_n = [0]

    def into_T(pool, src, width, dst, tok, after, gain=None, shift=None, dst_free=()):
        marks, reads = [], []
        nj = width // P
        for j0 in range(0, nj, 4):
            nb = min(4, nj - j0)
            b, ps, free = pool.take()
            PE.wait(free + list(after))
            for j in range(nb):
                m = t.transpose(ps[:, j * P:(j + 1) * P], src[:, (j0 + j) * P:(j0 + j + 1) * P], ident)
            m.then_inc(PE.sem, 1)
            PE.count += 1
            m = (PE.sem, PE.count)
            reads = [m]
            psv = ps[:, 0:nb * P].rearrange("p (j q) -> p j q", j=nb)
            d = dst[:, j0:j0 + nb, tok:tok + P]
            if gain is None:
                if (j0 // 4) % 2:
                    m2 = step(AC, [m] + list(dst_free), a.copy, d, psv)
                else:
                    m2 = step(DV, [m] + list(dst_free), v.tensor_copy, d, psv)
            else:
                m2 = step(DV, [m] + list(dst_free), v.tensor_tensor, d, psv, bc(gain[:, j0:j0 + nb], P), ALU.mult)
            give(b, [m2])
            if shift is not None:
                m2 = step(GP, [m2], g.tensor_tensor, d, d, bc(shift[:, j0:j0 + nb], P), ALU.add)
            marks.append(m2)
        return marks, reads

    def norm_into_T(pool, srcs, width, dst, toks, after, gain=None, shift=None, dst_free=()):
        r, rm, _ = rstd_of(srcs, width, after)
        marks = {}
        for i, s_ in enumerate(srcs):
            k = xn_n[0] % 2
            xn_n[0] += 1
            x_ = xn[:, k, 0:width]
            m = step(DV, [rm] + list(after[i]) + xn_free[k], v.tensor_scalar, x_, s_, r[:, i:i + 1], None, ALU.mult)
            mk, rd = into_T(pool, x_, width, dst, toks[i], [m], gain(i) if gain else None,
                            shift(i) if shift else None, dst_free)
            xn_free[k] = rd
            marks[i] = mk
        return marks

    def fence():
        return [m for e in COMPUTE for m in e.last()]

    def fence_all():
        f = fence()
        for e in COMPUTE:
            e.wait(f)
        return f

    def dbg(name, ap, after):
        if dump is not None and name in dump:
            AC.wait(after)
            dump[name](a, ap, new_sem("dump_" + name), loads)

    x_m = [load(AC, "x", H[:, 2:4, :], ins["x"].rearrange("(t p) d -> p t d", p=P))]
    cols_m = [load(AC, "cols", cols[:, :], ins["cols"])]
    sq_m = [load(AC, "sq", sq[:, :], ins["sq"])]
    bias_t5, _ = carve(0, 16, 384)
    for i in range(NSLOT):
        load_chunk(i, [])
    bias_m = [load(AC, "bias_t5", bias_t5, ins["bias_t5"])]
    lnc_m = [load(AC, "lnc", lnc[:, :], ins["lnc"])]
    small_m = [load(AC, "small_rows", small_rows[:, :], ins["small_rows"].partition_broadcast(P))]
    row_m = {}

    def load_row(slot, name, after=()):
        i = ROWS_ORDER.index(name)
        row_m[name] = [load(AC, name, rowbuf[:, slot, :], ins["rows"][i, :].partition_broadcast(P), after)]
        return rowbuf[:, slot, :]

    g_post_mix = load_row(0, "g_post_mix")
    g_post_mlp = load_row(1, "g_post_mlp")
    b_ple = load_row(2, "b_ple_gate")
    g_post_ple = load_row(3, "g_post_ple")
    ctx_m = [load(AC, "ctx", H[:, 0:2, :], ins["ctx"].rearrange("(t p) d -> p t d", p=P))]
    misc_m = [load(AC, "selneg", selneg[:, :], ins["selneg"]), load(AC, "sel2", sel2[:, :], ins["sel2"]),
              load(AC, "gla_mask", arena[:, ARENA - 14 * P:], ins["gla_mask"]), load(AC, "rope", rope[:, :, :, :], ins["rope"]),
              load(AC, "wgate", wgate[:, :], ins["wgate"])]
    eps_col = sb("eps_col", [P, 1])
    eps_m = step(DV, [], v.memset, eps_col[:, :], EPS)
    AC.wait([eps_m])
    one_col = sb("one_col", [P, 1])
    one_m = step(DV, [], v.memset, one_col[:, :], 1.0)
    AC.wait([one_m])

    gemm = Pool([0, 1, 2, 3])
    turn = Pool([4, 5])
    outp = Pool([6, 7])

    probs_free = [[] for _ in range(4)]
    probsT_free = [[] for _ in range(4)]
    att_n = [0]

    def attention(qtiles, heads, q, k, nk, val, marks, finish, bias=None, b0=0, nbias=0, sink=None, dv=64):
        scores = Pool([0, 1, 2])
        items = [(qt, h) for qt in qtiles for h in range(heads)]
        state = {}
        outs = {}
        rsum = {qt: stat(heads) for qt in qtiles}
        esink = {qt: stat(heads) for qt in qtiles} if sink is not None else None
        summed = {qt: [] for qt in qtiles}

        def head_scores(qt, h):
            n = nk(qt)
            b, ps, free = scores.take()
            m = products(free + marks, [(ps[:, 0:n], q(h, qt), k(h, n))])
            mx = stat(1)
            if bias is not None:
                if nbias == n:
                    m = step(DV, [m] + bias_marks, v.tensor_tensor_reduce, ps[:, 0:n], ps[:, 0:n], bias(h, qt),
                             1.0, -3e38, ALU.add, ALU.max, mx)
                else:
                    m = step(DV, [m] + bias_marks, v.tensor_tensor, ps[:, b0:b0 + nbias], ps[:, b0:b0 + nbias],
                             bias(h, qt), ALU.add)
            if bias is None or nbias != n:
                m = step(DV, [m], v.tensor_reduce, mx, ps[:, 0:n], AX_X, ALU.max)
            if sink is not None:
                m = step(DV, [m], v.tensor_scalar, mx, mx, sink(h), -1.0, ALU.max, ALU.mult)
            else:
                m = step(DV, [m], v.tensor_scalar, mx, mx, -1.0, None, ALU.mult)
            i = att_n[0] % 4
            att_n[0] += 1
            pr = probs[:, i, 0:n]
            me = step(AC, [m] + probs_free[i] + junk_mark[0], a.activation, pr, ps[:, 0:n], ACT.Exp, bias=mx,
                      accum_out=rsum[qt][:, h:h + 1])
            give(b, [me])
            summed[qt].append(me)
            if sink is not None:
                summed[qt].append(step(AC, [m], a.activation, esink[qt][:, h:h + 1], sink(h), ACT.Exp, bias=mx))
            state[(qt, h)] = (i, pr, me, n)

        def head_values(qt, h):
            i, pr, me, n = state.pop((qt, h))
            b, ps, free = turn.take()
            PE.wait(free + [me])
            for j in range(n // P):
                m = t.transpose(ps[:, j * P:(j + 1) * P], pr[:, j * P:(j + 1) * P], ident)
            m.then_inc(PE.sem, 1)
            PE.count += 1
            m = (PE.sem, PE.count)
            probs_free[i] = [m]
            pT = probsT[:, i, 0:n]
            if (h + qt) % 2:
                me = step(AC, [m] + probsT_free[i], a.copy, pT, ps[:, 0:n])
            else:
                me = step(DV, [m] + probsT_free[i], v.tensor_copy, pT, ps[:, 0:n])
            give(b, [me])
            state[(qt, h, "T")] = (i, pT, me, n)

        def head_out(qt, h):
            i, pT, me, n = state.pop((qt, h, "T"))
            if h == 0:
                outs[qt] = outp.take()
            b, po, free = outs[qt]
            m = products(free + [me] + marks, [(po[:, h * dv:(h + 1) * dv], pT[:, j * P:(j + 1) * P], val(h, j))
                                              for j in range(n // P)])
            probsT_free[i] = [m]
            if h == heads - 1:
                r = rsum[qt]
                dm = summed[qt]
                if sink is not None:
                    dm = [step(DV, dm, v.tensor_tensor, r, r, esink[qt], ALU.add)]
                dm = [step(DV, dm, v.reciprocal, r, r)]
                give(b, finish(qt, po, [m] + dm, r))

        for n in range(len(items) + 3):
            if n < len(items):
                head_scores(*items[n])
            if 2 <= n < len(items) + 2:
                head_values(*items[n - 2])
            if n >= 3:
                head_out(*items[n - 3])
        for i in range(4):
            junk_mark[0] = junk_mark[0] + probs_free[i]

    bias_marks = []

    misc_m.append(step(GP, misc_m, g.tensor_copy, gla_mask[:, :], arena[:, ARENA - 14 * P:]))
    m = step(GP, bias_m + lnc_m, g.tensor_tensor, bias_t5[:, 8:16, :], bias_t5[:, 8:16, :],
             lnc[:, :].unsqueeze(1).to_broadcast([P, 8, 384]), ALU.add)
    bias_marks = bias_m + [m]
    for e in (PE, DV):
        e.wait(sq_m + cols_m)

    base = 16 * 384
    qaT, base = carve(base, 4, S)
    kaT, base = carve(base, 1, S)
    qbT, base = carve(base, 4, S)
    kbT, base = carve(base, 4, S)
    va, base = carve(base, 2, 128)
    vb, base = carve(base, 2, 512)
    o_tm, base = carve(base, 2, D)
    mix, _ = carve(0, 2, D)

    lat = [2, 3]
    m = norm_into_T(turn, [H[:, i, :] for i in lat], D, uT, [0, P], [x_m, x_m], gain=lambda i: col("g_pre_mix"))
    u_m = m[0] + m[1]

    def copy_out(dst, scale=None):
        def f(i, ps, mk):
            d = dst(i)
            n = d.shape[-1]
            mk = step(AC, [mk], a.activation, d, ps[:, 0:n], ACT.Copy, scale=1.0 if scale is None else scale)
            kept.append(mk)
            return [mk]
        return f

    def copy_out_v(dst):
        def f(i, ps, mk):
            d = dst(i)
            mk = step(DV, [mk], v.tensor_copy, d, ps[:, 0:d.shape[-1]])
            kept.append(mk)
            return [mk]
        return f

    kept = []
    plain = lambda w, k, ft: w[:, k, ft * P:(ft + 1) * P]
    project_fm(gemm, "qa", uT, u_m, 0, S, range(4), plain,
               copy_out(lambda ft: qaT[:, ft, :], 0.125))
    view = project_fm(gemm, "kva", uT, u_m, 0, S, [0], lambda w, k, ft: w[:, k, 0:128],
                      copy_out_v(lambda ft: kaT[:, 0, :]), last=False)
    project_tm(gemm, "kva", uT, lambda i: u_m, [0, 1], copy_out_v(lambda i: va[:, i, :]), c0=128, n=128, view=view)
    project_fm(gemm, "qb", uT, u_m, 0, S, range(4), plain, copy_out(lambda ft: qbT[:, ft, :], 0.125))
    project_fm(gemm, "kb", uT, u_m, 0, S, range(4), plain, copy_out_v(lambda ft: kbT[:, ft, :]))
    project_tm(gemm, "vb", uT, lambda i: u_m, [0, 1], copy_out_v(lambda i: vb[:, i, :]))
    proj_m = kept[:]

    o_marks = {0: [], 1: []}

    def finish_to(dst, sink_marks):
        def f(qt, po, mk, r):
            n = r.shape[-1]
            dm = step(DV, mk, v.tensor_tensor, dst(qt).rearrange("p (h d) -> p h d", h=n),
                      po[:, 0:n * 64].rearrange("p (h d) -> p h d", h=n), bc(r, 64), ALU.mult)
            sink_marks(qt).append(dm)
            return [dm]
        return f

    def t5(h, qt):
        return bias_t5[:, h, (128 if qt == 0 else 0):(128 if qt == 0 else 0) + S]

    hp = lambda h: slice(64 * h, 64 * h + 64)
    attention([0, 1], 8, lambda h, qt: qaT[hp(h // 4), h % 4, qt * P:(qt + 1) * P], lambda h, n: kaT[hp(h // 4), 0, 0:n],
              lambda qt: S, lambda h, j: va[:, j, 64 * (h // 4):64 * (h // 4) + 64], proj_m + small_m,
              finish_to(lambda qt: o_tm[:, qt, 0:512], lambda qt: o_marks[qt]), bias=t5, nbias=S,
              sink=lambda h: small_rows[:, h:h + 1])
    attention([0, 1], 8, lambda h, qt: qbT[hp(h % 2), h // 2, qt * P:(qt + 1) * P], lambda h, n: kbT[hp(h % 2), h // 2, 0:n],
              lambda qt: S, lambda h, j: vb[:, j, 64 * h:64 * h + 64], proj_m,
              finish_to(lambda qt: o_tm[:, qt, 512:1024], lambda qt: o_marks[qt]), bias=lambda h, qt: t5(h + 8, qt), nbias=S)
    dbg("o_tm", o_tm, o_marks[0] + o_marks[1])

    dead_u = PE.last()
    ob = [o_marks[0], o_marks[1]]
    m1 = norm_into_T(turn, [o_tm[:, i, 0:512] for i in range(2)], 512, uT[:, 0:4, :], [0, P], ob,
                     gain=lambda i: col("g_out_a"), dst_free=dead_u)
    m2 = norm_into_T(turn, [o_tm[:, i, 512:1024] for i in range(2)], 512, uT[:, 4:8, :], [0, P], ob,
                     gain=lambda i: col("g_out_b"), dst_free=dead_u)
    oT_m = [m1[0] + m2[0], m1[1] + m2[1]]

    def project_1024(names, srcT, src_marks, tiles, evac):
        for c, name in enumerate(names):
            project_tm(gemm, name, srcT, src_marks, tiles, lambda i, ps, mk, c=c: evac(i, c, ps, mk))

    def half(ap, c):
        return ap[:, c * 512:(c + 1) * 512]

    def residual_norm(src, src_marks, gain, gain_marks):
        r, rm, _ = rstd_of([src[:, i, :] for i in range(2)], D, [src_marks[i] for i in range(2)])
        res = []
        for i in range(2):
            mk = step(DV, [rm] + src_marks[i] + gain_marks, v.scalar_tensor_tensor, src[:, i, :], src[:, i, :],
                      r[:, i:i + 1], gain, ALU.mult, ALU.mult)
            res.append([step(GP, [mk], g.tensor_tensor, H[:, 2 + i, :], H[:, 2 + i, :], src[:, i, :], ALU.add)])
        return res

    mix_marks = [[], []]
    bias_dead = DV.last()

    def mix_evac(i, c, ps, mk):
        mk = step(DV if c else AC, [mk] + bias_dead, v.tensor_copy if c else a.copy, half(mix[:, i, :], c), ps)
        mix_marks[i].append(mk)
        return [mk]

    project_1024(["wo0", "wo1"], uT, lambda i: oT_m[i], [0, 1], mix_evac)
    h_m = residual_norm(mix, mix_marks, g_post_mix, row_m["g_post_mix"])
    dbg("h1", H[:, 2:4, :], h_m[0] + h_m[1])

    dead = PE.last()
    m = norm_into_T(turn, [H[:, i, :] for i in lat], D, uT, [0, P], h_m, gain=lambda i: col("g_pre_mlp"), dst_free=dead)
    v_m = m[0] + m[1]
    hidden, _ = carve(2 * D, D_FF // P, S)
    hid_free = fence()
    hid_m = {}
    for c in range(8):
        w, wm, wi = weights(f"up{c}")
        for pair in range(2):
            b, ps, free = gemm.take()
            for f in range(2):
                ft = 2 * pair + f
                pm = products(free + wm + v_m, [(ps[:, f * S:(f + 1) * S], w[:, k, ft * P:(ft + 1) * P], uT[:, k, 0:S])
                                               for k in range(KT)])
            dst = hidden[:, 4 * c + 2 * pair:4 * c + 2 * pair + 2, :].rearrange("p a b -> p (a b)")
            rm = step(AC, [pm] + hid_free, a.activation, dst, ps, ACT.Relu)
            give(b, [rm])
            sm = step(GP if pair else DV, [rm], (g if pair else v).tensor_tensor, dst, dst, dst, ALU.mult)
            hid_m[2 * c + pair] = sm
        used(wi, pm)
    mix_marks = [[], []]
    mix_dead = fence()
    for c in range(2):
        taken = [gemm.take(), gemm.take()]
        for kc in range(4):
            w, wm, wi = weights(f"down{c}{kc}")
            for i in range(2):
                b, ps, free = taken[i]
                PE.wait(free + wm + [hid_m[4 * kc + j] for j in range(4)])
                for k in range(KT):
                    ins_ = t.matmul(ps, hidden[:, 8 * kc + k, i * P:(i + 1) * P], w[:, k, :],
                                    start=(kc == 0 and k == 0), stop=(kc == 3 and k == KT - 1))
                ins_.then_inc(PE.sem, 1)
                PE.count += 1
                pm = (PE.sem, PE.count)
                if kc == 3:
                    mk = step(DV if i else AC, [pm] + mix_dead, v.tensor_copy if i else a.copy, half(mix[:, i, :], c), ps)
                    give(b, [mk])
                    mix_marks[i].append(mk)
            used(wi, pm)
    h_m = residual_norm(mix, mix_marks, g_post_mlp, row_m["g_post_mlp"])
    dbg("h2", H[:, 2:4, :], h_m[0] + h_m[1])

    pT, base = carve(2 * D, 2, S)
    gate_tm, base = carve(base, 2, D)
    ple_tm, base = carve(base, 2, D)
    arena_free = fence()
    pT_m = [load(AC, "pT", pT, ins["pT"].rearrange("(k p) t -> p k t", p=P), arena_free)]
    w, wm, wi = weights("ple")
    ple_marks = [[], []]
    for i in range(2):
        for c in range(2):
            b, ps, free = gemm.take()
            pm = products(free + wm + pT_m, [(ps, pT[:, k, i * P:(i + 1) * P], w[:, k, c * 512:c * 512 + 512])
                                            for k in range(2)])
            mk = step(DV, [pm] + arena_free, v.tensor_copy, half(ple_tm[:, i, :], c), ps)
            give(b, [mk])
            ple_marks[i].append(mk)
    used(wi, pm)
    hT_m = []
    for i in range(2):
        mk, _ = into_T(turn, H[:, 2 + i, :], D, uT, i * P, h_m[i], dst_free=dead)
        hT_m.append(mk)
    mix_marks = [[], []]

    def gate_evac(i, c, ps, mk):
        gsl = half(gate_tm[:, i, :], c)
        m1 = step(DV, [mk] + row_m["b_ple_gate"], v.tensor_tensor, gsl, ps, half(b_ple, c), ALU.add)
        m2 = step(AC, [m1], a.activation, gsl, gsl, ACT.Sigmoid)
        mix_marks[i].append(step(GP, [m2] + ple_marks[i] + arena_free, g.tensor_tensor, half(mix[:, i, :], c), gsl,
                                 half(ple_tm[:, i, :], c), ALU.mult))
        return [m1]

    project_1024(["pg0", "pg1"], uT, lambda i: hT_m[i], [0, 1], gate_evac)
    h_m = residual_norm(mix, mix_marks, g_post_ple, row_m["g_post_ple"])
    dbg("h3", H[:, 2:4, :], h_m[0] + h_m[1])

    row_free = fence()
    load_row(0, "final_norm", row_free)
    gateB = {0: rowbuf[:, 2, :], 1: rowbuf[:, 3, :]}
    scT = sb("scT", [P, KT, 2])
    modrow = probsT[0:2, 0:2, :]
    mod_shift, mod_gain = sb("mod_shift", [P, KT, 2]), sb("mod_gain", [P, KT, 2])
    sc_m = step(AC, cols_m, a.activation, scT[:, :, :].rearrange("p a b -> p (a b)"), col("c"), ACT.Silu)
    modrow_free = [[], []]

    def modulation(layer, readers):
        bname = f"l{layer}_b_gate"
        load_row(1, bname, readers)
        res = []
        for c in range(6):
            w, wm, wi = weights(f"mod{layer}{c}")
            b, ps, free = gemm.take()
            pm = products(free + wm + [sc_m], [(ps[0:2, :], scT[:, k, :], w[:, k, :]) for k in range(KT)])
            used(wi, pm)
            row = modrow[:, c % 2, :]
            mk = step(DV, [pm] + readers + modrow_free[c % 2], v.tensor_copy, row, ps[0:2, :])
            give(b, [mk])
            if c < 4:
                b, ps, free = turn.take()
                PE.wait(free + [mk])
                for j in range(4):
                    m = t.transpose(ps[:, 2 * j:2 * j + 2], row[:, j * P:(j + 1) * P], sq[0:2, 0:2])
                m.then_inc(PE.sem, 1)
                PE.count += 1
                modrow_free[c % 2] = PE.last()
                dst = (mod_shift if c < 2 else mod_gain)[:, 4 * (c % 2):4 * (c % 2) + 4, :]
                bcol = col(f"l{layer}_b_mod", 4 * c, 4)
                mk = step(DV, PE.last() + readers + cols_m, v.tensor_tensor, dst,
                          ps[:, 0:8].rearrange("p (j r) -> p j r", j=4), bc(bcol, 2), ALU.add)
                give(b, [mk])
                if c >= 2:
                    mk = step(DV, [mk], v.tensor_scalar, dst, dst, 1.0, None, ALU.add)
                    mk = step(DV, [mk], v.tensor_tensor, dst, dst, bc(col(f"l{layer}_norm", 4 * (c % 2), 4), 2), ALU.mult)
                res.append(mk)
            else:
                for r in range(2):
                    b, ps, free = turn.take()
                    pm = products(free + [mk] + misc_m, [(ps, sel2[:, r * P:(r + 1) * P], row)])
                    m2 = step(DV, [pm] + readers + row_m[bname], v.tensor_tensor, half(gateB[r], c % 2), ps,
                              half(rowbuf[:, 1, :], c % 2), ALU.add)
                    give(b, [m2])
                    res.append(m2)
                modrow_free[c % 2] = [pm]
        probsT_free[0], probsT_free[1] = modrow_free
        return res

    def modulated_norm(tiles, marks, mod_m, dst_free):
        stream = lambda tile: 0 if tile < 2 else 1
        m = norm_into_T(turn, [H[:, i, :] for i in tiles], D, uT, [i * P for i in tiles],
                        [marks[i] + mod_m for i in tiles],
                        gain=lambda i: mod_gain[:, :, stream(tiles[i])],
                        shift=lambda i: mod_shift[:, :, stream(tiles[i])], dst_free=dst_free)
        return {tile: m[i] for i, tile in enumerate(tiles)}

    def gate_and_out(names, tiles, tile0, catT, cat_marks, H_marks, release):
        res = {i: [] for i in tiles}

        def evac(i, c, ps, mk):
            k = (2 * c + i) % 4
            tile = i + tile0
            tmp = probsT[:, k, :]
            m1 = step(DV, [mk] + probsT_free[k], v.tensor_tensor, tmp, ps, half(gateB[0 if tile < 2 else 1], c), ALU.mult)
            m2 = step(GP, [m1] + H_marks[tile], g.tensor_tensor, half(H[:, tile, :], c), half(H[:, tile, :], c), tmp, ALU.add)
            probsT_free[k] = [m2]
            res[i].append(m2)
            return [m1]

        project_1024(names, catT, lambda i: cat_marks[i], tiles, evac)
        return {i + tile0: res[i] for i in tiles}

    mod_m = modulation(0, row_free)
    ctx_marks = {0: ctx_m, 1: ctx_m, 2: h_m[0], 3: h_m[1]}
    um = modulated_norm([0, 1, 2, 3], ctx_marks, mod_m, PE.last())
    u_all = [x for i in range(4) for x in um[i]]
    dbg("u0", uT[:, :, :], u_all)
    stage0 = fence_all()
    all4 = range(4)
    cat, base = carve(0, 4, D)
    qT, base = carve(base, 8, 512)
    kT, base = carve(base, 8, 512)
    v_tm, base = carve(base, 4, 512)
    cqT, b2 = carve(0, 3, 512)
    ckvT, b2 = carve(b2, 2, 512)
    q_tm, b2 = carve(b2, 8, QK)
    assert b2 <= 4 * D
    k_tm, base = carve(base, 8, QK)
    kr_tm, base = carve(base, 4, ROPE)
    g_tm = sb("g_tm", [P, 4, 16])
    rtmp = sb("rtmp", [P, 4, 128])

    cq_m, ckv_m, kr_m, gt_m = {}, {}, {}, {}

    def cq_evac(i, ps, mk):
        m = norm_into_T(turn, [ps[:, 0:Q_RANK]], Q_RANK, cqT, [i * P], [[mk]], gain=lambda _: col("q_norm"))
        cq_m[i] = m[0]
        return DV.last() + AC.last()

    project_tm(gemm, "cq", uT, lambda i: um[i], all4, cq_evac)

    def ckv_evac(i, ps, mk):
        kr_m[i] = [step(DV, [mk], v.tensor_copy, kr_tm[:, i, :], ps[:, KV_RANK:KV_RANK + ROPE])]
        gt_m[i] = step(DV, kr_m[i] + small_m, v.tensor_tensor, g_tm[:, i, :], ps[:, KV_RANK + ROPE:KV_RANK + ROPE + 16],
                       small_rows[:, 8:24], ALU.add)
        m = norm_into_T(turn, [ps[:, 0:KV_RANK]], KV_RANK, ckvT, [i * P], [[gt_m[i]]], gain=lambda _: col("kv_norm"))
        ckv_m[i] = m[0]
        return DV.last() + AC.last()

    project_tm(gemm, "ckv", uT, lambda i: um[i], all4, ckv_evac, n=KV_RANK + ROPE + 16)

    rt_free = [[]]

    def rotate(view, nh, tile, after):
        y = view.rearrange("p h (a two c) -> p h a two c", a=2, two=2)
        y1, y2 = y[:, :, :, 0, :], y[:, :, :, 1, :]

        def table(which):
            x_ = rope[:, tile, which, :].rearrange("p (a c) -> p a c", a=2)
            return x_.unsqueeze(1).to_broadcast([P, nh, 2, PAIRS])

        tmp = [rtmp[:, j, 0:nh * 16].rearrange("p (h a c) -> p h a c", h=nh, a=2) for j in range(4)]
        ms = []
        for j, (y_, w_) in enumerate(((y1, 0), (y2, 1), (y2, 0), (y1, 1))):
            ms.append(step(GP, after + rt_free[0] + misc_m, g.tensor_tensor, tmp[j], y_, table(w_), ALU.mult))
        m1 = step(GP, ms, g.tensor_tensor, y1, tmp[0], tmp[1], ALU.subtract)
        m2 = step(GP, ms, g.tensor_tensor, y2, tmp[2], tmp[3], ALU.add)
        rt_free[0] = [m1, m2]
        return [m1, m2]

    def heads_into_T(src, dst, tile, after):
        res = []
        for hh in range(2):
            b, ps, free = turn.take()
            PE.wait(free + after)
            for j in range(4):
                m = t.transpose(ps[0:QK, j * P:(j + 1) * P], src[:, 4 * hh + j, :], ident)
            m.then_inc(PE.sem, 1)
            PE.count += 1
            d = dst[0:QK, 4 * hh:4 * hh + 4, tile * P:(tile + 1) * P]
            psv = ps[0:QK, :].rearrange("p (j q) -> p j q", j=4)
            mk = step(DV, PE.last(), v.tensor_copy, d, psv) if hh else step(AC, PE.last(), a.copy, d, psv)
            give(b, [mk])
            res.append(mk)
        return res, PE.last()

    w, wm, wi = weights("uq")
    q_free, qT_m = [], []
    for i in all4:
        qf = q_tm.rearrange("p a b -> p (a b)")
        ms = []
        for c0, n in ((0, 512), (512, 256)):
            b, ps, free = gemm.take()
            pm = products(free + wm + cq_m[i], [(ps[:, 0:n], cqT[:, k, i * P:(i + 1) * P], w[:, k, c0:c0 + n]) for k in range(3)])
            mk = step(AC, [pm] + q_free, a.activation, qf[:, c0:c0 + n], ps[:, 0:n], ACT.Copy, scale=QK ** -0.5)
            give(b, [mk])
            ms.append(mk)
        if i >= 2:
            ms = ms + rotate(q_tm[:, :, NOPE:QK], 8, i - 2, ms)
        mk, q_free = heads_into_T(q_tm, qT, i, ms)
        qT_m += mk
    used(wi, pm)
    w, wm, wi = weights("ukv")
    k_free, kv_m = [], []
    for i in all4:
        ms = []
        for hh in range(2):
            b, ps, free = gemm.take()
            pm = products(free + wm + ckv_m[i], [(ps, ckvT[:, k, i * P:(i + 1) * P], w[:, k, hh * 512:hh * 512 + 512]) for k in range(2)])
            kvv = ps.rearrange("p (h d) -> p h d", h=4)
            m1 = step(DV, [pm] + k_free, v.tensor_copy, k_tm[:, 4 * hh:4 * hh + 4, 0:NOPE], kvv[:, :, 0:NOPE])
            m2 = step(AC, [m1], a.copy, v_tm[:, i, hh * 256:hh * 256 + 256].rearrange("p (h d) -> p h d", h=4), kvv[:, :, NOPE:])
            give(b, [m1, m2])
            kv_m.append(m2)
            ms.append(m1)
        krv = kr_tm[:, i, :].unsqueeze(1)
        if i >= 2:
            kr_m[i] = kr_m[i] + rotate(krv, 1, i - 2, kr_m[i])
        ms.append(step(DV, kr_m[i] + k_free, v.tensor_copy, k_tm[:, :, NOPE:QK], krv.to_broadcast([P, 8, ROPE])))
        mk, k_free = heads_into_T(k_tm, kT, i, ms)
        kv_m += mk
    used(wi, pm)
    cat_free = fence()
    for e in (DV, AC):
        e.wait(cat_free)
    a_m = {i: [] for i in all4}
    bias_marks = []
    attention(all4, 8, lambda h, qt: qT[0:QK, h, qt * P:(qt + 1) * P], lambda h, n: kT[0:QK, h, 0:n],
              lambda qt: 256 if qt < 2 else 512, lambda h, j: v_tm[:, j, 64 * h:64 * h + 64], qT_m + kv_m,
              finish_to(lambda qt: cat[:, qt, 0:512], lambda qt: a_m[qt]))
    dbg("mla", cat[:, :, 0:512], fence())

    stage1 = fence_all()
    mlT = []
    base = 4 * D
    for _ in range(2):
        w_, base = carve(base, 4, 512)
        mlT.append(w_)
    mv, base = carve(base, 4, 4, 132)
    nd, nd_end = carve(base, 4, 4, 2 * 132)
    pads = []
    b2 = base
    for _ in range(4):
        w_, b2 = carve(b2, 2, 384)
        pads.append(w_)
    Mrow, b2 = carve(b2, 2, 512)
    Mrow = xn
    assert b2 <= nd_end
    glog, gb, ga_ = sb("glog", [P, 4, 2, 4]), sb("gb", [P, 4, 2, 4]), sb("ga_", [P, 4, 2, 4])
    gem = sb("gem", [P, 4, 2, 4])
    ml_m = [[], []]
    for which, name in enumerate(("mq", "mk")):
        def conv_evac(ft, ps, mk, which=which):
            d = mlT[which][:, ft, :]
            cw = col("conv_w").rearrange("p (j f) -> p j f", j=3)
            f = 4 * which + ft
            dr, pr = (x_.rearrange("p (r s) -> p r s", r=2) for x_ in (d, ps))
            m = step(DV, [mk], v.tensor_scalar, d, ps, cw[:, 1, f:f + 1], col("conv_b", f, 1), ALU.mult, ALU.add)
            m = step(DV, [m], v.scalar_tensor_tensor, dr[:, :, 1:S], pr[:, :, 0:S - 1], cw[:, 0, f:f + 1], dr[:, :, 1:S], ALU.mult, ALU.add)
            m = step(DV, [m], v.scalar_tensor_tensor, dr[:, :, 0:S - 1], pr[:, :, 1:S], cw[:, 2, f:f + 1], dr[:, :, 0:S - 1], ALU.mult, ALU.add)
            ml_m[which].append(step(AC, [m], a.activation, d, d, ACT.Silu))
            return [m]
        project_fm(gemm, name, uT, u_all, 0, 512, range(4), plain, conv_evac)
    mv_ones = step(GP, [], g.memset, mv[:, :, :, 128:129], 1.0)
    mv_m = [mv_ones]

    def mv_evac(i, ps, mk):
        mk = step(DV, [mk], v.tensor_copy, mv[:, i, :, 0:128], ps.rearrange("p (h d) -> p h d", h=4))
        mv_m.append(mk)
        return [mk]

    project_tm(gemm, "mv", uT, lambda i: um[i], all4, mv_evac)
    mo_m = {}

    def mo_evac(i, ps, mk):
        mo_m[i] = step(AC, [mk], a.activation, cat[:, i, 512:1024], ps, ACT.Sigmoid)
        return [mo_m[i]]

    project_tm(gemm, "mo", uT, lambda i: um[i], all4, mo_evac)

    def log_sigmoid(x_, tmp, dst, after):
        m = step(AC, after, a.activation, tmp, x_, ACT.Abs)
        m = step(AC, [m], a.activation, tmp, tmp, ACT.Exp, scale=-1.0)
        m = step(AC, [m], a.activation, tmp, tmp, ACT.Ln, bias=one_col[:, 0:1])
        return step(DV, [m] + list(after), v.scalar_tensor_tensor, dst, x_, 0.0, tmp, ALU.min, ALU.subtract)

    gv5 = g_tm[:, :, :].rearrange("p t (d w h) -> p t d w h", d=2, w=2)
    gtm = list(gt_m.values())
    ftmp = rtmp[:, 0, 0:32].rearrange("p (t d h) -> p t d h", t=4, d=2)
    fin = rtmp[:, 1, 0:32].rearrange("p (t d h) -> p t d h", t=4, d=2)
    m = step(DV, gtm + rt_free[0], v.tensor_copy, fin, gv5[:, :, :, 1, :])
    fl = lambda x_: x_.rearrange("p t d h -> p (t d h)")
    lf_m = log_sigmoid(rtmp[:, 1, 0:32], rtmp[:, 0, 0:32], fl(glog[:, :, :, :]), [m])
    b, ps, free = gemm.take()
    gbp = ps[:, 0:32].rearrange("p (t d h) -> p t d h", t=4, d=2)
    for i in all4:
        for d in range(2):
            if d == 0:
                src = [(j, "ones") for j in range(i)] + [(i, "tri_u")]
            elif i < 2:
                src = [(i, "tri_l")] + [(j, "ones") for j in range(i + 1, 2)]
            else:
                src = [(0, "ones"), (1, "ones"), (i, "tri_l")] + [(j, "ones") for j in range(i + 1, 4)]
            pm = products(free + [lf_m], [(gbp[:, i, d, :], sqc(n_), glog[:, j, d, :]) for j, n_ in src])
    bm = step(DV, [pm], v.tensor_copy, gb[:, :, :, :], gbp)
    give(b, [bm])
    am = step(DV, [bm], v.tensor_tensor, ga_[:, :, :, :], gv5[:, :, :, 0, :], gb[:, :, :, :], ALU.subtract)
    zm = step(GP, [], g.memset, arena[0:4, base:base + 4 * 768], 0.0)
    for d in range(2):
        b, ps, free = gemm.take()
        PE.wait(free + [am])
        for i in all4:
            m = t.transpose(ps[0:4, i * P:(i + 1) * P], ga_[:, i, d, :], ident)
        m.then_inc(PE.sem, 1)
        PE.count += 1
        lo = 128 if d == 0 else 0
        own = pads[2 * d:2 * d + 2]
        m = step(DV, PE.last() + [zm], v.tensor_copy, own[0][0:4, :, lo:lo + S], ps[0:4, :].rearrange("p (r s) -> p r s", r=2))
        give(b, [m])
        cur = 0
        for sh in (1, 2, 4, 8, 16, 32, 64, 128):
            s_ = own[cur][0:4]
            o_ = own[1 - cur][0:4]
            off = lo - sh if d == 0 else sh
            m = step(DV, [m], v.tensor_tensor, o_[:, :, lo:lo + S], s_[:, :, lo:lo + S], s_[:, :, off:off + S], ALU.max)
            cur = 1 - cur
        s_ = own[cur][0:4]
        carry = s_[:, 0, lo + S - 1:lo + S] if d == 0 else s_[:, 0, lo:lo + 1]
        m1 = step(DV, [m], v.tensor_scalar, Mrow[0:4, d, 0:S], s_[:, 0, lo:lo + S], 0.0, None, ALU.max)
        m2 = step(DV, [m], v.tensor_scalar, Mrow[0:4, d, S:2 * S], s_[:, 1, lo:lo + S], carry, 0.0, ALU.max, ALU.max)
        if d == 0:
            Mm = [m1, m2]
        else:
            Mm = Mm + [m1, m2]
    b, ps, free = gemm.take()
    PE.wait(free + Mm)
    mtp = ps[:, 0:32].rearrange("p (t d h) -> p t d h", t=4, d=2)
    for i in all4:
        for d in range(2):
            m = t.transpose(mtp[:, i, d, :], Mrow[0:4, d, i * P:(i + 1) * P], sq[0:4, 0:4])
    m.then_inc(PE.sem, 1)
    PE.count += 1
    m = step(DV, PE.last(), v.tensor_tensor, gem[:, :, :, :], mtp, gb[:, :, :, :], ALU.add)
    give(b, [m])
    m = step(DV, [m], v.tensor_scalar, gem[:, :, :, :], gem[:, :, :, :], -1.0, 80.0, ALU.mult, ALU.min)
    em_m = step(AC, [m], a.activation, fl(gem[:, :, :, :]), fl(gem[:, :, :, :]), ACT.Exp)
    pads_dead = fence()
    DV.wait(pads_dead)
    dbg("gem", gem[:, :, :, :], [em_m])

    reach = {0: [[0, 1, 2, 3], [1, 2, 3], [2, 3], [3]], 1: [[0, 2, 3], [0, 1, 2, 3], [2], [2, 3]]}
    ranges = {0: [[(0, 4)], [(1, 4)], [(2, 4)], [(3, 4)]], 1: [[(0, 1), (2, 4)], [(0, 4)], [(2, 3)], [(2, 4)]]}
    wdec = [uT, uT]
    dec, dend = carve(nd_end, 2, 512)
    pml, _ = carve(dend, 2, 512) if dend + 1024 <= ARENA else (None, None)
    nd_m = []
    prod_free = [[], []]
    dec_free = [[], []]
    wl_free = [[] for _ in range(4)]
    prodP = [probs, probsT]
    ap = Pool([0, 1])
    sp_ = Pool([2, 3, 4, 5])
    hp_ = Pool([6, 7])
    all_in = ml_m[0] + ml_m[1] + mv_m
    wtmp_free = [[], []]
    wtmp = xn[:, 1, :].rearrange("p (a b) -> p a b", a=2)
    for h in range(ML_H):
        decs = []
        for d in range(2):
            b, ps, free = ap.take()
            pm = products(free + Mm + misc_m, [(ps, selneg[:, h * P:(h + 1) * P], Mrow[0:4, d, 0:512])])
            dm = step(DV, [pm] + dec_free[d], v.tensor_tensor, dec[:, d, :].rearrange("p (j q) -> p j q", j=4),
                      ps.rearrange("p (j q) -> p j q", j=4),
                      sqc("neg_u" if d == 0 else "neg_l").unsqueeze(1).to_broadcast([P, 4, P]), ALU.add)
            decs.append((b, ps, pm, dm))
        st = []
        for s_ in range(4):
            b, ps, free = sp_.take()
            c0 = 0 if s_ < 2 else 256
            pm = products(free + all_in, [(ps[:, c0:512], mlT[1][:, h, s_ * P:(s_ + 1) * P], mlT[0][:, h, c0:512])])
            st.append((b, ps, pm, []))
        pmk = {}
        for d in range(2):
            bD, psD, pmD, dmD = decs[d]
            readers = []
            for s_ in range(4):
                wl = xn[:, (2 * d + s_) % 2, 512:1024]
                wk = (2 * d + s_) % 2
                ems = []
                for (c0, c1) in ranges[d][s_]:
                    for (x0, x1) in ((c0, min(c1, s_)), (max(c0, s_ + 1), c1)):
                        if x0 < x1:
                            m = step(AC, [dmD, am] + wtmp_free[wk], a.activation, wl[:, x0 * P:x1 * P], psD[:, x0 * P:x1 * P],
                                     ACT.Exp, bias=ga_[:, s_, d, h:h + 1])
                            ems.append(m)
                            readers.append(m)
                m = step(AC, [dmD, am] + wtmp_free[wk], a.activation, wl[:, s_ * P:(s_ + 1) * P], dec[:, d, s_ * P:(s_ + 1) * P],
                         ACT.Exp, bias=ga_[:, s_, d, h:h + 1])
                ems.append(m)
                dlast = m
                b, ps, pm, rd = st[s_]
                for (c0, c1) in ranges[d][s_]:
                    m = step(DV, ems + [pm] + prod_free[d], v.scalar_tensor_tensor, prodP[d][:, s_, c0 * P:c1 * P],
                             ps[:, c0 * P:c1 * P], ML_D ** -0.5, wl[:, c0 * P:c1 * P], ALU.mult, ALU.mult)
                    rd.append(m)
                wtmp_free[wk] = [m]
                pmk[(d, s_)] = m
            dec_free[d] = [dlast]
            give(bD, readers + [dmD])
        for b, ps, pm, rd in st:
            give(b, rd)
        for i in all4:
            b, ps, free = hp_.take()
            for d in range(2):
                srcs = [s_ for s_ in range(4) if i in reach[d][s_]]
                m = products(free + [pmk[(d, s_)] for s_ in srcs],
                             [(ps[:, d * 132:d * 132 + 129], prodP[d][:, s_, i * P:(i + 1) * P], mv[:, s_, h, 0:129]) for s_ in srcs])
            mk = step(AC if i % 2 else DV, [m], a.copy if i % 2 else v.tensor_copy,
                      nd[:, i, h, :].rearrange("p (d w) -> p d w", d=2)[:, :, 0:129],
                      ps[:, 0:264].rearrange("p (d w) -> p d w", d=2)[:, :, 0:129])
            give(b, [mk])
            nd_m.append(mk)
        prod_free = [[m], [m]]
    den = nd.rearrange("p t h (d w) -> p t d h w", d=2)[:, :, :, :, 128]
    dabs = rtmp[:, 2, 0:32].rearrange("p (t d h) -> p t d h", t=4, d=2)
    for i in all4:
        m = step(DV, nd_m, v.scalar_tensor_tensor, dabs[:, i], den[:, i], -1.0, den[:, i], ALU.mult, ALU.max)
        m = step(DV, [m, em_m], v.tensor_tensor, dabs[:, i], dabs[:, i], gem[:, i], ALU.max)
    m = step(DV, [m], v.reciprocal, rtmp[:, 2, 0:32], rtmp[:, 2, 0:32])
    ndv = nd.rearrange("p t h (d w) -> p t d h w", d=2)
    hm_m = {}
    hss = stat(16)
    for i in all4:
        E_, e_ = (DV, v) if i % 2 else (GP, g)
        for d in range(2):
            x_ = ndv[:, i, d, :, 0:128]
            mk = step(E_, [m], e_.tensor_tensor, x_, x_, bc(dabs[:, i, d], P), ALU.mult)
            if d:
                mk = step(E_, [mk, prev], e_.tensor_tensor, x_, x_, ndv[:, i, 0, :, 0:128], ALU.add)
            prev = mk
        ch = cat[:, i, 512:1024].rearrange("p (h w) -> p h w", h=4)
        mk = step(E_, [mk, mo_m[i]], e_.tensor_tensor, ch, x_, ch, ALU.mult)
        hm_m[i] = [mk]
    def head_norm(ap_, n, width, after, sq_buf, eng):
        E_, e_ = eng
        view = ap_.rearrange("p (h w) -> p h w", h=n)
        sqv = sq_buf.rearrange("p (h w) -> p h w", h=n)
        ss = stat(n)
        m = step(E_, after, e_.tensor_tensor, sqv, view, view, ALU.mult)
        m = step(DV, [m], v.tensor_reduce, ss, sqv, AX_X, ALU.add)
        m = step(AC, [m], a.activation, ss, ss, ACT.Ln, scale=1.0 / width, bias=eps_col[:, 0:1])
        m = step(AC, [m], a.activation, ss, ss, ACT.Exp, scale=-0.5)
        return [step(E_, [m], e_.tensor_tensor, view, view, bc(ss, width), ALU.mult)]

    for i in all4:
        x_ = nd[:, i, :, 0:128]
        flat = nd[:, i, :, :].rearrange("p h w -> p (h w)")[:, 0:512]
        hm_m[i] = head_norm(cat[:, i, 512:1024], 4, 128, hm_m[i], flat, (DV, v) if i % 2 else (GP, g))
    dbg("hm", cat[:, :, 512:1024], fence())

    def gated_cat_T(layer, tiles, tile0, cat_, cat_m, gain2, mul_free):
        zm = {i: [] for i in tiles}
        for c in range(2):
            def z_evac(i, ps, mk, c=c):
                k = i % 4
                tmp = probs[:, k, :]
                m1 = step(AC, [mk] + probs_free[k] + junk_mark[0], a.activation, tmp, ps, ACT.Silu)
                m2 = step(DV, [m1] + cat_m[i - tile0], v.tensor_tensor, half(cat_[:, i - tile0, :], c), half(cat_[:, i - tile0, :], c), tmp, ALU.mult)
                probs_free[k] = [m2]
                zm[i].append(m2)
                return [m1]
            project_tm(gemm, f"z{layer}{c}", uT, lambda i: um[i], tiles, z_evac)
        dead = PE.last()
        res = {}
        for i in tiles:
            src = cat_[:, i - tile0, :]
            r = []
            for c in range(2):
                mk, _ = into_T(turn, half(src, c), 512, uT[:, 4 * c:4 * c + 4, :], (i - tile0) * P, zm[i],
                               gain=gain2 if c == (1 if layer == 0 else 0) else None, dst_free=dead)
                r += mk
            res[i - tile0] = r
        return res

    f = fence_all()
    for i in range(4):
        probs_free[i], probsT_free[i] = f, f
    catT_m = gated_cat_T(0, all4, 0, cat, {i: a_m[i] + hm_m[i] for i in all4}, col("h_norm"), None)
    Hm = gate_and_out(["out00", "out01"], all4, 0, uT, catT_m, ctx_marks, None)
    dbg("h4", H[:, :, :], fence())

    f = fence_all()
    mod_m = modulation(1, f)
    um = modulated_norm([0, 1, 2, 3], Hm, mod_m, f)
    u_all = [x for i in range(4) for x in um[i]]
    dbg("u1", uT[:, :, :], u_all)
    cat, base = carve(0, 2, D)
    gkT, base = carve(base, 2, 512)
    gqT, base = carve(base, 2, S)
    gv_tm, base = carve(base, 4, 512)
    BT = []
    for _ in range(2):
        w_, base = carve(base, 2, 512)
        BT.append(w_)
    lg, _ = carve(base, 4, 2, 256)
    attG, base = carve(base, 2, 2, 2, P)
    attX, base = carve(base, 2, 2, 2, P)
    attC, base = carve(base, 2, 2, 2, S)
    lev = []
    for _ in range(6):
        w_, base = carve(base, 2, S)
        lev.append(w_)
    na_bias, base2 = carve(base, 1)
    kept = []
    kept_q = []

    w, wm, wi = weights("gqk")
    for ft in range(4):
        t0, nt = (S, S) if ft < 2 else (0, 512)
        b, ps, free = gemm.take()
        pm = products(free + wm + u_all, [(ps[:, 0:nt], w[:, k, ft * P:(ft + 1) * P], uT[:, k, t0:t0 + nt]) for k in range(KT)])
        d = gqT[:, ft, :] if ft < 2 else gkT[:, ft - 2, :]
        mk = step(AC, [pm], a.activation, d, ps[:, 0:nt], ACT.Copy, scale=GLA_DK ** -0.5 if ft < 2 else 1.0)
        give(b, [mk])
        kept.append(mk)
    used(wi, pm)
    project_tm(gemm, "gv", uT, lambda i: um[i], all4, copy_out_v(lambda i: gv_tm[:, i, :]))
    gaT = sb("gaT", [2 * GLA_RANK + 1, 512])
    gone = step(DV, [], v.memset, gaT[2 * GLA_RANK:2 * GLA_RANK + 1, :], 1.0)
    w, wm, wi = weights("ga")
    b, ps, free = gemm.take()
    pm = products(free + wm + u_all, [(ps[0:32, :], w[:, k, :], uT[:, k, :]) for k in range(KT)])
    used(wi, pm)
    gaT_m = step(DV, [pm], v.tensor_copy, gaT[0:32, :], ps[0:32, :])
    give(b, [gaT_m])
    lg_m = {}
    for i in all4:
        b, ps, free = gemm.take()
        pm = products(free + [gaT_m, gone] + misc_m, [(ps, gaT[:, i * P:(i + 1) * P], wgate[:, :])])
        lg_m[i] = log_sigmoid(ps, probs[:, i, :], lg[:, i, :, :].rearrange("p d c -> p (d c)"), [pm])
        give(b, [lg_m[i]])
    BT_m = []
    for d in range(2):
        for dt_ in range(2):
            b, ps, free = gemm.take()
            for r in range(2):
                o_ = ps[:, r * S:(r + 1) * S]
                full = sq[:, SQ["tri_u16" if d == 0 else "ones16b"] * P:][:, 0:2 * P]
                first, second = (2 * r, 2 * r + 1) if d == 0 else (2 * r + 1, 2 * r)
                tri = sqc("tri_u16" if d == 0 else "tri_l16")
                sub = o_[:, P:2 * P] if d == 0 else o_[:, 0:P]
                pm = products(free + [lg_m[2 * r], lg_m[2 * r + 1]],
                              [(o_, lg[:, first, d, dt_ * P:(dt_ + 1) * P], full), (sub, lg[:, second, d, dt_ * P:(dt_ + 1) * P], tri)])
            mk = step(AC if dt_ else DV, [pm], a.copy if dt_ else v.tensor_copy, BT[d][:, dt_, :], ps)
            give(b, [mk])
            BT_m.append(mk)
    dbg("BT", BT[0], BT_m)
    gla_in = kept + BT_m
    E_ctx, Kc = lev[0], [lev[1], lev[2]]
    Ql, Qc = lev[3], [lev[4], lev[5]]
    qc_m, kc_m = [], []
    e_prev = []
    for d in range(2):
        for dt_ in range(2):
            end = BT[d][:, dt_, S - 1:S] if d == 0 else BT[d][:, dt_, 0:1]
            e_prev.append(step(AC, gla_in + kc_m + qc_m, a.activation, E_ctx[:, dt_, :], BT[d][:, dt_, 0:S], ACT.Exp, scale=-1.0, bias=end))
        kc_m.append(step(DV, e_prev[-2:] + gla_in, v.tensor_tensor, Kc[d], gkT[:, :, 0:S], E_ctx, ALU.mult))
        m = step(AC, gla_in + qc_m, a.activation, Ql, BT[d][:, :, S:2 * S], ACT.Exp)
        qc_m.append(step(DV, [m], v.tensor_tensor, Qc[d], gqT, Ql, ALU.mult))
    attc_m = []
    for s_ in range(2):
        for par in range(2):
            b, ps, free = gemm.take()
            for c in range(2):
                pm = products(free + kc_m + qc_m, [(ps[:, c * S:(c + 1) * S], Kc[d][hp(par), c, s_ * P:(s_ + 1) * P], Qc[d][hp(par), c, :])
                                                  for d in range(2)])
            mk = step(AC, [pm], a.copy, attC[:, s_, par], ps.rearrange("p (c s) -> p c s", c=2))
            give(b, [mk])
            attc_m.append(mk)
    att_w = fence()
    for e in (DV, AC, GP):
        e.wait(att_w)
    prev = {}
    for par in range(2):
        b, ps, free = gemm.take()
        for tile in range(2):
            for c in range(2):
                at = (2 * tile + c) * P
                pm = products(free + kept, [(ps[:, at:at + P], gkT[hp(par), c, S + tile * P:S + (tile + 1) * P],
                                            gqT[hp(par), c, tile * P:(tile + 1) * P])])
        mk = step(AC, [pm] + BT_m, a.activation, attG[:, par].rearrange("p t c q -> p (t c q)"), ps, ACT.Copy, scale=2.0)
        give(b, [mk])
        prev[par] = mk
    zl = step(GP, [], g.memset, arena[:, base - 6 * 512:base], 0.0)
    lev_free = [[zl], [zl]]
    n_lev = 0
    lev_pool = Pool([0, 1, 2, 3, 6, 7])
    cross_m = []
    for hsize in GLA_LEVELS + [128]:
        nblk = 128 // hsize
        for d in range(2):
            k = n_lev % 2
            n_lev += 1
            E_, Q_, K_ = lev[3 * k:3 * k + 3]
            sp3 = lambda x_: x_.rearrange("p c (n two s) -> p c n two s", two=2, s=hsize)
            Bv = sp3(BT[d][:, :, S:2 * S])
            Ev, Qv, Kv, qv, kv = sp3(E_), sp3(Q_), sp3(K_), sp3(gqT), sp3(gkT[:, :, S:2 * S])
            th, sh = (1, 0) if d == 0 else (0, 1)
            seam = (Bv[:, :, :, 0, hsize - 1] if d == 0 else Bv[:, :, :, 1, 0]).unsqueeze(3).to_broadcast([P, 2, nblk, hsize])
            m1 = step(GP, lev_free[k], g.tensor_tensor, Ev[:, :, :, th, :], Bv[:, :, :, th, :], seam, ALU.subtract)
            m2 = step(GP, lev_free[k], g.tensor_tensor, Ev[:, :, :, sh, :], seam, Bv[:, :, :, sh, :], ALU.subtract)
            m3 = step(AC, [m1, m2], a.activation, E_, E_, ACT.Exp)
            m4 = step(DV, [m3] + lev_free[k], v.tensor_tensor, Qv[:, :, :, th, :], qv[:, :, :, th, :], Ev[:, :, :, th, :], ALU.mult)
            m5 = step(GP, [m3], g.tensor_tensor, Kv[:, :, :, sh, :], kv[:, :, :, sh, :], Ev[:, :, :, sh, :], ALU.mult)
            for par in range(2):
                b, ps, free = lev_pool.take()
                for tile in range(2 if hsize < 128 else 1):
                    s0, t0 = (tile * P, tile * P) if hsize < 128 else (sh * P, th * P)
                    for c in range(2):
                        at = (2 * tile + c) * P
                        pm = products(free + [m4, m5], [(ps[:, at:at + P], K_[hp(par), c, s0:s0 + P], Q_[hp(par), c, t0:t0 + P])])
                if hsize < 128:
                    mi = 7 * d + GLA_LEVELS.index(hsize)
                    mask = gla_mask[:, mi * P:(mi + 1) * P].unsqueeze(1).to_broadcast([P, 4, P])
                    mk = step(DV, [pm, prev[par]] + misc_m, v.copy_predicated, attG[:, par].rearrange("p t c q -> p (t c) q"), mask,
                              ps.rearrange("p (h q) -> p h q", h=4))
                    prev[par] = mk
                else:
                    mk = step(DV, [pm], v.tensor_copy, attX[:, sh, par], ps[:, 0:2 * P].rearrange("p (c q) -> p c q", c=2))
                    cross_m.append(mk)
                give(b, [mk])
            lev_free[k] = [pm]
    att_m = attc_m + cross_m + [prev[0], prev[1]]
    g_m = {}
    for i in range(2):
        b, ps, free = gemm.take()
        for h in range(4):
            par, c = h % 2, h // 2
            keys = [(attC[:, s_, par, c, i * P:(i + 1) * P], s_) for s_ in range(2)]
            keys += [(attG[:, par, i, c, :], 2 + i), (attX[:, 1 - i, par, c, :], 3 - i)]
            terms = [(ps[:, h * P:(h + 1) * P], att, gv_tm[:, s_, h * P:(h + 1) * P]) for att, s_ in keys]
            pm = products(free + att_m + kept, terms)
        mk = step(DV, [pm], v.tensor_copy, cat[:, i, 0:512], ps)
        give(b, [mk])
        g_m[i] = [mk]
    for i in range(2):
        g_m[i] = head_norm(cat[:, i, 0:512], 4, 128, g_m[i], xn[:, i, 0:512], (DV, v))
    dbg("gla", cat[:, :, 0:512], g_m[0] + g_m[1])

    f = fence_all()
    for i in range(4):
        probs_free[i], probsT_free[i] = f, f
    base = 2 * D
    nqT, base = carve(base, 4, S)
    nkT, base = carve(base, 4, 512)
    nv, base = carve(base, 4, 512)
    nab, base = carve(base, 2, 8, S)
    nab_m = [load(AC, "na_bias", nab, ins["na_bias"], f)]
    kept = []
    project_fm(gemm, "nq", uT, u_all, S, S, range(4), plain, copy_out(lambda ft: nqT[:, ft, :], NA_D ** -0.5))
    project_fm(gemm, "nk", uT, u_all, 0, 512, range(4), plain, copy_out_v(lambda ft: nkT[:, ft, :]))
    project_tm(gemm, "nv", uT, lambda i: um[i], all4, copy_out_v(lambda i: nv[:, i, :]))
    bias_marks = nab_m
    n_m = {0: [], 1: []}
    attention([0, 1], 8, lambda h, qt: nqT[hp(h % 2), h // 2, qt * P:(qt + 1) * P], lambda h, n: nkT[hp(h % 2), h // 2, 0:n],
              lambda qt: 512, lambda h, j: nv[:, j, 64 * h:64 * h + 64], kept,
              finish_to(lambda qt: cat[:, qt, 512:1024], lambda qt: n_m[qt]), bias=lambda h, qt: nab[:, qt, h, :], b0=S, nbias=S)
    dbg("na", cat[:, :, 512:1024], n_m[0] + n_m[1])
    f = fence_all()
    catT_m = gated_cat_T(1, [2, 3], 2, cat, {i: g_m[i] + n_m[i] for i in range(2)}, col("gla_norm"), None)
    Hm = gate_and_out(["out10", "out11"], [0, 1], 2, uT, catT_m, Hm, None)

    f = fence_all()
    r, rm, _ = rstd_of([H[:, i, :] for i in lat], D, [Hm[2], Hm[3]])
    outs = []
    for i in range(2):
        mk = step(DV, [rm] + row_m["final_norm"], v.scalar_tensor_tensor, xn[:, i, :], H[:, 2 + i, :], r[:, i:i + 1],
                  rowbuf[:, 0, :], ALU.mult, ALU.mult)
        outs.append(load(SP, f"out{i}", out[i * P:(i + 1) * P, :], xn[:, i, :], [mk]))
    SP.wait(outs + list(loads.values()))


def _t5_bucket(rel):
    half = NUM_BUCKETS // 2
    max_exact = half // 2
    sign = np.where(rel > 0, half, 0)
    n = np.abs(rel)
    nf = np.maximum(n, 1).astype(np.float32)
    large = max_exact + (np.log(nf / np.float32(max_exact)) / np.float32(math.log(MAX_DISTANCE / max_exact))
                         * np.float32(half - max_exact)).astype(np.int32)
    large = np.minimum(large, half - 1)
    return sign + np.where(n < max_exact, n, large)


def _constants():
    i = np.arange(P)
    s, t_ = i[:, None], i[None, :]
    f = lambda c: np.where(c, 1.0, 0.0).astype(np.float32)
    tri_u, tri_l = f(s <= t_), f(s >= t_)
    one = np.ones((P, P), np.float32)
    parts = {"ident": f(s == t_), "ones": one, "tri_u": tri_u, "tri_l": tri_l, "tri_u16": tri_u / 16, "ones16a": one / 16,
             "ones16b": one / 16, "tri_l16": tri_l / 16, "neg_u": np.where(s <= t_, 0, NEG), "neg_l": np.where(s >= t_, 0, NEG)}
    sq = np.concatenate([parts[n] for n in SQ], 1).astype(np.float32)
    rel = np.arange(384)[None, :] - 128 - np.arange(P)[:, None]
    count = sum(((rel % dil == 0) & (np.abs(rel) <= dil * (window // (2 * dil)))).astype(np.int64) for window, dil in DILATED)
    lnc = np.where(count > 0, np.log(np.maximum(count, 1)), 0.0).astype(np.float32)
    selneg = np.zeros((4, 4, P), np.float32)
    sel2 = np.zeros((2, 2, P), np.float32)
    for h in range(4):
        selneg[h, h] = -1.0
    for r in range(2):
        sel2[r, r] = 1.0
    masks = []
    for d in range(2):
        for hs in GLA_LEVELS:
            same = (s // (2 * hs)) == (t_ // (2 * hs))
            sh, th = (s // hs) % 2, (t_ // hs) % 2
            masks.append(same & ((sh == 0) & (th == 1) if d == 0 else (sh == 1) & (th == 0)))
    tt = np.arange(S)
    inv = 1.0 / (np.float32(10000.0) ** (np.arange(PAIRS, dtype=np.float32) / PAIRS))
    ang = np.concatenate([(tt // GRID_W)[:, None] * inv, (tt % GRID_W)[:, None] * inv], -1)
    cs = np.stack([np.cos(ang), np.sin(ang)], 1).astype(np.float32)
    rope = np.ascontiguousarray(cs.reshape(2, P, 2, 16).transpose(1, 0, 2, 3))
    return {"sq": sq, "lnc": lnc, "selneg": selneg.reshape(4, 4 * P), "sel2": sel2.reshape(2, 2 * P),
            "gla_mask": np.concatenate(masks, 1).astype(np.float32), "rope": rope}, rel, count


def _layout(i):
    c, rel, count = _constants()
    w = lambda n: np.ascontiguousarray(i[n][0] if i[n].ndim == 3 else i[n])
    dev = dict(c)
    for n in ("w_in", "w_o", "w_up", "w_down", "w_ple_proj", "w_ple_gate"):
        dev[n] = w(n)
    qa = dev["w_in"][:, :WA].reshape(D, NKVA, NHA // NKVA, HD).transpose(0, 2, 1, 3).reshape(D, WA)
    dev["w_in"] = np.concatenate([qa, dev["w_in"][:, WA:]], 1)
    for n in ("l0_w_mod", "l0_w_in", "l0_w_out", "l1_w_mod", "l1_w_in", "l1_w_out"):
        dev[n] = w(n + "_2")
    dev["w_uq"], dev["w_ukv"] = w("l0_mla_w_uq_2"), w("l0_mla_w_ukv_2")
    dev["x"], dev["ctx"] = i["x"][0], i["ctx_2"][0]
    dev["pT"] = np.ascontiguousarray(i["p"][0, 0].T)

    def columns(vec):
        return np.asarray(vec).reshape(-1, P).T

    conv_w = np.concatenate([columns(i["l0_mlstm_conv_w_2"][j]) for j in range(3)], 1)
    cc = np.stack([columns(i["c_ctx_2"]), columns(i["c_2"][0])], 2).reshape(P, 16)
    vecs = {"g_pre_mix": i["g_pre_mix"], "g_out_a": i["g_out_a"], "g_out_b": i["g_out_b"], "g_pre_mlp": i["g_pre_mlp"],
            "l0_norm": i["l0_norm_2"], "l1_norm": i["l1_norm_2"], "l0_b_mod": i["l0_b_mod_2"], "l1_b_mod": i["l1_b_mod_2"],
            "q_norm": i["l0_mla_q_norm_2"], "kv_norm": i["l0_mla_kv_norm_2"], "h_norm": i["l0_mlstm_norm_2"],
            "gla_norm": i["l1_gla_norm_2"], "conv_b": i["l0_mlstm_conv_b_2"]}
    dev["cols"] = np.concatenate([columns(vecs[n]) if n in vecs else (conv_w if n == "conv_w" else cc) for n in COLS], 1)
    dev["rows"] = np.stack([i["g_post_mix"][0], i["g_post_mlp"][0], i["b_ple_gate"][0], i["g_post_ple"][0],
                            i["l0_b_mod_2"][2 * D:], i["l1_b_mod_2"][2 * D:], i["final_norm_2"]])
    gates = np.stack([i["l0_mlstm_b_i_2"], i["l0_mlstm_b_f_2"]], 1).reshape(-1)
    dev["small_rows"] = np.concatenate([i["sink_a"][0], gates])
    table = i["rel_bias_table"]
    bias = table[_t5_bucket(rel)].transpose(0, 2, 1).copy()
    keep = np.zeros(bias.shape, bool)
    keep[:, 0:8] = (np.abs(rel) <= WINDOW_A)[:, None]
    keep[:, 8:16] = (count > 0)[:, None]
    bias[~keep] = NEG
    dev["bias_t5"] = bias
    wg = np.zeros((2 * GLA_RANK + 1, 512), np.float32)
    for d in range(2):
        wg[d * GLA_RANK:(d + 1) * GLA_RANK, d * 256:(d + 1) * 256] = i["l1_gla_w_gate_2"][d]
        wg[2 * GLA_RANK, d * 256:(d + 1) * 256] = i["l1_gla_b_gate_2"][d]
    dev["wgate"] = wg
    tok = np.arange(S)
    r, cc_ = tok // GRID_W, tok % GRID_W
    kh = min(NA_KH, ROWS)
    r0 = np.clip(r - kh // 2, 0, ROWS - kh)
    c0 = np.clip(cc_ - NA_KW // 2, 0, GRID_W - NA_KW)
    inside = ((r[None, :] >= r0[:, None]) & (r[None, :] < r0[:, None] + kh)
              & (cc_[None, :] >= c0[:, None]) & (cc_[None, :] < c0[:, None] + NA_KW))
    dr = np.where(inside, r[None, :] - r[:, None] + NA_KH - 1, 0)
    dc = np.where(inside, cc_[None, :] - cc_[:, None] + NA_KW - 1, 0)
    nb = i["l1_na_rpb_2"][:, dr, dc].copy()
    nb[:, ~inside] = NEG
    dev["na_bias"] = np.ascontiguousarray(nb.reshape(NA_H, 2, P, S).transpose(2, 1, 0, 3))
    return {n: np.ascontiguousarray(x_) for n, x_ in dev.items()}


def kernel(**inputs):
    import concourse.bacc as bacc
    from concourse.bass_utils import run_bass_kernel_spmd

    dev = _layout({n: np.asarray(x_) for n, x_ in inputs.items()})
    nc = bacc.Bacc("TRN2", target_bir_lowering=False, num_devices=1)
    aps = {n: nc.dram_tensor("in_" + n, x_.shape, mybir.dt.from_np(x_.dtype), kind="ExternalInput").ap() for n, x_ in dev.items()}
    out = nc.dram_tensor("out_h", (S, D), F32, kind="ExternalOutput").ap()
    build(nc, aps, out)
    r = run_bass_kernel_spmd(nc, [{"in_" + n: x_ for n, x_ in dev.items()}], core_ids=[0])
    return r.results[0]["out_h"].reshape(1, S, D)
```

```python
import math
from contextlib import ExitStack

import numpy as np
import concourse.bass as bass
from concourse import mybir

ALU = mybir.AluOpType
ACT = mybir.ActivationFunctionType
F32 = mybir.dt.float32
F32R = mybir.dt.float32r
U8 = mybir.dt.uint8
AX_X = mybir.AxisListType.X

P = 128
D = 1024
KT = D // P
S = 256
EPS = 1e-6
NEG = -1e30
BANK = 512

HD = 64
NHA, NKVA, NHB = 8, 2, 8
WINDOW_A = 128
DILATED = ((128, 1), (512, 4), (2048, 16))
WA, KVA, WB = NHA * HD, NKVA * HD, NHB * HD
D_FF = 4 * D
PLE = 256
NUM_BUCKETS, MAX_DISTANCE = 32, 1024

GRID_W = 64
ROWS = S // GRID_W
MLA_H, Q_RANK, KV_RANK, NOPE, ROPE, MLA_V = 8, 384, 256, 64, 32, 64
QK = NOPE + ROPE
PAIRS = ROPE // 4
ML_H, ML_D = 4, 128
GLA_H, GLA_DK, GLA_DV, GLA_RANK, GLA_TAU = 4, 64, 128, 16, 16.0
NA_H, NA_D, NA_KH, NA_KW = 8, 64, 8, 16
E_SIZES = (Q_RANK, KV_RANK, ROPE, 512, 512, 512, 512, 4 * ML_H, 1024)
O_SIZES = (256, 256, 512, 2 * GLA_RANK, 512, 512, 512, 1024)
E_OFF = [sum(E_SIZES[:i]) for i in range(len(E_SIZES) + 1)]
O_OFF = [sum(O_SIZES[:i]) for i in range(len(O_SIZES) + 1)]
GLA_LEVELS = [1 << i for i in range(7)]

COLS = {}
_n = 0
for _name, _w in (("g_pre_mix", 8), ("g_out_a", 4), ("g_out_b", 4), ("g_pre_mlp", 8), ("l0_norm", 8),
                  ("l1_norm", 8), ("l0_b_mod", 24), ("l1_b_mod", 24), ("q_norm", 3), ("kv_norm", 2),
                  ("h_norm", 4), ("gla_norm", 4), ("conv_b", 8), ("conv_w", 24), ("c", 16)):
    COLS[_name] = (_n, _w)
    _n += _w
NCOLS = _n
ROWS_ORDER = ("g_post_mix", "g_post_mlp", "b_ple_gate", "g_post_ple", "l0_b_gate", "l1_b_gate", "final_norm")
SQ = {n: i for i, n in enumerate(("ident", "ones", "tri_u", "tri_l", "tri_u16", "ones16b", "tri_l16", "neg_u", "neg_l"))}


class Engine:

    def __init__(self, e, sem):
        self.e, self.sem, self.count, self.seen = e, sem, 0, {}

    def wait(self, marks):
        for sem, value in marks:
            if self.seen.get(id(sem), 0) < value:
                self.e.wait_ge(sem, value)
                self.seen[id(sem)] = value

    def last(self):
        return [(self.sem, self.count)] if self.count else []


def step(eng, after, method, *args, **kw):
    eng.wait(after)
    method(*args, **kw).then_inc(eng.sem, 1)
    eng.count += 1
    return (eng.sem, eng.count)


def build(nc, ins, out, dump=None):
    ctx = ExitStack()
    with ctx:
        _build(nc, ctx, ins, out, dump)


def _build(nc, ctx, ins, out, dump):
    def sb(name, shape, dt=F32):
        return ctx.enter_context(nc.sbuf_tensor(name, shape, dt))

    def new_sem(name):
        return ctx.enter_context(nc.semaphore(name))

    PE = Engine(nc.tensor, new_sem("pe_done"))
    DV = Engine(nc.vector, new_sem("dve_done"))
    AC = Engine(nc.scalar, new_sem("act_done"))
    GP = Engine(nc.gpsimd, new_sem("pool_done"))
    SP = Engine(nc.sync, new_sem("sp_done"))
    COMPUTE = (PE, DV, AC, GP)
    v, a, g, t = nc.vector, nc.scalar, nc.gpsimd, nc.tensor

    sq = sb("sq", [P, len(SQ) * P])
    cols = sb("cols", [P, NCOLS])
    sel4 = sb("sel4", [4, 2 * P])
    gla_mask = sb("gla_mask", [P, 14 * P], U8)
    rope = sb("rope", [P, 2, 2, 2 * PAIRS])
    small_rows = sb("small_rows", [P, 8 + 16])
    H = sb("H", [P, 4, D])
    uT = (sb("uT_hi", [P, KT, 512], F32R), sb("uT_lo", [P, KT, 512], F32R))
    CH = 2048
    NRAW = 2
    wraw = sb("wraw", [P, NRAW, CH])
    w_hi, w_lo = sb("w_hi", [P, 2, CH], F32R), sb("w_lo", [P, 2, CH], F32R)
    presplit = sb("presplit", [P, 2, 512])
    rowbuf = sb("rowbuf", [P, 2, D])
    probs = sb("probs", [P, 4, 512])
    probsT = sb("probsT", [P, 4, 512])
    xn = sb("xn", [P, 2, D])
    stats = sb("stats", [P, 900])
    ARENA = 13000
    arena = sb("arena", [P, ARENA])
    banks = ctx.enter_context(nc.psum_tensor("banks", [P, 8, BANK], F32))

    def sqc(name):
        i = SQ[name]
        return sq[:, i * P:(i + 1) * P]

    ident = sqc("ident")

    def col(name, j0=0, n=None):
        c0, w = COLS[name]
        return cols[:, c0 + j0:c0 + (w if n is None else j0 + n)]

    stat_at = [0]

    def stat(n=1):
        stat_at[0] += n
        assert stat_at[0] <= 900, stat_at
        return stats[:, stat_at[0] - n:stat_at[0]]

    def carve(base, *shape):
        n = int(np.prod(shape))
        assert base + n <= ARENA, (base, n)
        view = arena[:, base:base + n]
        if len(shape) == 2:
            view = view.rearrange("p (a b) -> p a b", a=shape[0])
        elif len(shape) == 3:
            view = view.rearrange("p (a b c) -> p a b c", a=shape[0], b=shape[1])
        elif len(shape) == 4:
            view = view.rearrange("p (a b c d) -> p a b c d", a=shape[0], b=shape[1], c=shape[2])
        return view, base + n

    def bc(ap, n):
        return ap.unsqueeze(len(ap.shape)).to_broadcast(list(ap.shape) + [n])

    bank_free = [[] for _ in range(8)]

    class Pool:

        def __init__(self, which):
            self.which, self.n = list(which), 0

        def take(self):
            b = self.which[self.n % len(self.which)]
            self.n += 1
            free = bank_free[b]
            assert free is not None, b
            bank_free[b] = None
            return b, banks[:, b, :], free

    def give(b, marks):
        bank_free[b] = list(marks)

    loads = {}
    def load(eng, name, dst, src, after=(), sem=None):
        eng.wait(after)
        s_ = sem or new_sem("ld_" + name)
        eng.e.dma_start(dst, src).then_inc(s_, 16)
        loads[name] = (s_, 16)
        return (s_, 16)

    def kview(w, k0, k1, c0, c1):
        return w[k0 * P:k1 * P, c0:c1].rearrange("(k p) n -> p k n", p=P)

    chunks = []

    def chunk(name, *parts):
        chunks.append((name, parts))

    def chunk_tm(name, w, c0, c1, extra=None):
        for k in range(2):
            parts = [(w, 4 * k, 4 * k + 4, c0, c1)]
            if extra:
                parts.append((w, 4 * k, 4 * k + 4) + extra)
            chunk(f"{name}.{k}", *parts)

    def chunk_fm(name, w, c0, c1):
        for k in range((c1 - c0 + 255) // 256):
            chunk(f"{name}.{k}", (w, 0, 8, c0 + 256 * k, min(c1, c0 + 256 * k + 256)))

    n_mod = [0]
    MODS = [(layer, c) for layer in range(2) for c in range(6)]

    def chunk_mods(n):
        for _ in range(n):
            layer, c = MODS[n_mod[0] // 2]
            k = n_mod[0] % 2
            chunk(f"mod{n_mod[0]}", (f"l{layer}_w_mod", 4 * k, 4 * k + 4, 512 * c, 512 * c + 512))
            n_mod[0] += 1

    FILL = {"attA": 6, "attB": 6, "o": 0, "mix": 0, "mlp": 0, "ple": 0, "mla": 10, "cat": 2}
    chunk_fm("qa", "w_in", 0, 512)
    chunk("kva", ("w_in", 0, 8, 512, 768))
    chunk_fm("qb", "w_in", 768, 1280)
    chunk_fm("kb", "w_in", 1280, 1792)
    chunk_tm("vb", "w_in", 1792, 2304)
    chunk_mods(FILL["attA"] + FILL["attB"] + FILL["o"])
    for c in range(2):
        chunk_tm(f"wo{c}", "w_o", c * 512, c * 512 + 512)
    chunk_mods(FILL["mix"])
    for c in range(8):
        chunk_fm(f"up{c}", "w_up", c * 512, c * 512 + 512)
        if c:
            for h in range(2):
                chunk(f"down{c - 1}{h}", ("w_down", 4 * c - 4, 4 * c, h * 512, h * 512 + 512))
    for h in range(2):
        chunk(f"down7{h}", ("w_down", 28, 32, h * 512, h * 512 + 512))
    chunk("ple", ("w_ple_proj", 0, 2, 0, 1024))
    chunk_mods(FILL["mlp"])
    for c in range(2):
        chunk_tm(f"pg{c}", "w_ple_gate", c * 512, c * 512 + 512)
    chunk_mods(FILL["ple"])
    eo = E_OFF
    chunk_tm("cq", "l0_w_in", eo[0], eo[1])
    chunk_tm("ckv", "l0_w_in", eo[1], eo[3], (eo[7], eo[8]))
    chunk("uq0", ("w_uq", 0, 3, 0, 512))
    chunk("uq1", ("w_uq", 0, 3, 512, 768))
    chunk("ukv", ("w_ukv", 0, 2, 0, 1024))
    chunk_mods(FILL["mla"])
    chunk_fm("mq", "l0_w_in", eo[3], eo[4])
    chunk_fm("mk", "l0_w_in", eo[4], eo[5])
    chunk_tm("mv", "l0_w_in", eo[5], eo[6])
    chunk_tm("mo", "l0_w_in", eo[6], eo[7])
    for c in range(2):
        chunk_tm(f"z0{c}", "l0_w_in", eo[8] + 512 * c, eo[8] + 512 * c + 512)
    chunk_mods(FILL["cat"])
    for c in range(2):
        chunk_tm(f"out0{c}", "l0_w_out", c * 512, c * 512 + 512)
    oo = O_OFF
    chunk_fm("gqk", "l1_w_in", 0, 512)
    chunk_tm("gv", "l1_w_in", oo[2], oo[3])
    chunk("ga", ("l1_w_in", 0, 8, oo[3], oo[3] + P))
    chunk_fm("nq", "l1_w_in", oo[4], oo[5])
    chunk_fm("nk", "l1_w_in", oo[5], oo[6])
    chunk_tm("nv", "l1_w_in", oo[6], oo[7])
    for c in range(2):
        chunk_tm(f"z1{c}", "l1_w_in", oo[7] + 512 * c, oo[7] + 512 * c + 512)
    for c in range(2):
        chunk_tm(f"out1{c}", "l1_w_out", c * 512, c * 512 + 512)
    PLAIN = {"uq0", "uq1", "ukv"}
    pair_slot = {}
    for i, (name, _) in enumerate(chunks):
        if name not in PLAIN:
            pair_slot[i] = len(pair_slot) % 2

    raw_sem = [new_sem(f"weights_in_slot{i}") for i in range(NRAW)]
    raw_count = [0] * NRAW
    landed = {}
    split_done = {}
    pair_free = [[], []]
    next_split = [0]

    def chunk_view(buf, i):
        parts = chunks[i][1]
        kt = parts[0][2] - parts[0][1]
        n = sum(p[4] - p[3] for p in parts)
        return buf[:, 0:kt * n].rearrange("p (k n) -> p k n", k=kt)

    def load_chunk(i, after):
        if i >= len(chunks):
            return
        SP.wait(after)
        k = i % NRAW
        view, at = chunk_view(wraw[:, k, :], i), 0
        for name, k0, k1, c0, c1 in chunks[i][1]:
            SP.e.dma_start(view[:, :, at:at + c1 - c0], kview(ins[name], k0, k1, c0, c1)).then_inc(raw_sem[k], 16)
            raw_count[k] += 16
            at += c1 - c0
        landed[i] = loads[f"slot{k}"] = (raw_sem[k], raw_count[k])

    def split_up_to(last):
        while next_split[0] < min(len(chunks), last + 1):
            i = next_split[0]
            if i in pair_slot:
                k = pair_slot[i]
                if pair_free[k] is None:
                    return
                raw, hi, lo = (chunk_view(x, i) for x in (wraw[:, i % NRAW, :], w_hi[:, k, :], w_lo[:, k, :]))
                mods = chunks[i][0].startswith("mod")
                E1, copy = (DV, v.tensor_copy) if mods else (AC, a.copy)
                E2, e2 = (GP, g) if mods else (DV, v)
                m1 = step(E1, [landed[i]] + pair_free[k], copy, hi, raw)
                m2 = step(E2, [m1] + pair_free[k], e2.tensor_tensor, lo, raw, hi.bitcast(F32), ALU.subtract)
                split_done[i] = [m1, m2]
                pair_free[k] = None
                load_chunk(i + NRAW, [m1, m2])
            next_split[0] += 1

    chunk_at = [0]

    def weights(name):
        i = chunk_at[0]
        assert chunks[i][0] == name, (chunks[i][0], name)
        chunk_at[0] += 1
        if name in PLAIN:
            return chunk_view(wraw[:, i % NRAW, :], i), [landed[i]], i
        return [chunk_view(x[:, pair_slot[i], :], i) for x in (w_hi, w_lo)], split_done[i], i

    def used(i, mark):
        if i in pair_slot:
            pair_free[pair_slot[i]] = [mark]
        else:
            load_chunk(i + NRAW, [mark])
        split_up_to(i + 2)

    def products(after, terms):
        PE.wait(after)
        for i, (o, l, r) in enumerate(terms):
            m = t.matmul(o, l, r, start=(i == 0), stop=(i == len(terms) - 1))
        m.then_inc(PE.sem, 1)
        PE.count += 1
        return (PE.sem, PE.count)

    HALVES = ((0, 0), (0, 1), (1, 0))

    def project(pool, name, items, marks, operands, evac, kparts):
        taken = {}
        for kc in range(kparts):
            w, wm, i = weights(name if kparts == 1 else f"{name}.{kc}")
            kn = w[0].shape[1]
            for it in items:
                if kc == 0:
                    taken[it] = pool.take()
                b, ps, free = taken[it]
                PE.wait(wm + (list(free) + list(marks(it)) if kc == 0 else []))
                for k in range(kn):
                    o, l, r = operands(it, w, kc * kn + k, k)
                    for j, (x, y) in enumerate(HALVES):
                        m = t.matmul(ps[:, 0:o], l[x], r[y], start=(kc + k + j == 0), stop=(kc == kparts - 1 and k == kn - 1 and j == 2))
                m.then_inc(PE.sem, 1)
                PE.count += 1
                m = (PE.sem, PE.count)
                if kc == kparts - 1:
                    give(b, evac(it, ps, m))
            used(i, m)

    def project_tm(pool, name, src, marks, tiles, evac, n=512, kparts=2):
        def operands(tile, w, K, k):
            return n, [x[:, K, tile * P:(tile + 1) * P] for x in src], [x[:, k, 0:n] for x in w]
        project(pool, name, tiles, marks, operands, evac, kparts)

    def project_fm(pool, name, src, marks, t0, nt, fts, evac):
        for c in range(0, len(fts), 2):
            def operands(ft, w, K, k, c=c):
                return nt, [x[:, k, (ft - fts[c]) * P:(ft - fts[c] + 1) * P] for x in w], [x[:, K, t0:t0 + nt] for x in src]
            project(pool, f"{name}.{c // 2}", fts[c:c + 2], lambda ft: marks, operands, evac, 1)

    junk_mark = [[]]

    def rstd_of(srcs, width, after, junk=None):
        n = len(srcs)
        ss, r = stat(n), stat(n)
        ms = []
        for i, s_ in enumerate(srcs):
            j = junk if junk is not None else probs[:, 0:2, :].rearrange("p a b -> p (a b)")
            m = step(AC, list(after[i]) + junk_mark[0], a.activation, j[:, 0:width], s_, ACT.Square, accum_out=ss[:, i:i + 1])
            junk_mark[0] = [m]
            ms.append(m)
        m = step(GP, ms, g.tensor_scalar, ss, ss, 1.0 / width, EPS, ALU.mult, ALU.add)
        m = step(GP, [m], g.tensor_tensor, r, ss, minus_half[:, 0:1].to_broadcast([P, n]), ALU.pow)
        return r, m, ms

    xn_free = [[], []]
    xn_n = [0]

    pre_free = [[], []]
    pre_n = [0]

    def split(x, hi, lo, after, free):
        m1 = step(AC, list(after) + list(free), a.copy, hi, x)
        m2 = step(DV, [m1] + list(free), v.tensor_tensor, lo, x, hi.bitcast(F32), ALU.subtract)
        return [m1, m2]

    def into_T(pool, src, width, dst, tok, after, gain=None, shift=None, dst_free=()):
        marks, reads = [], []
        nj = width // P
        for j0 in range(0, nj, 4):
            nb = min(4, nj - j0)
            b, ps, free = pool.take()
            PE.wait(free + list(after))
            for j in range(nb):
                m = t.transpose(ps[:, j * P:(j + 1) * P], src[:, (j0 + j) * P:(j0 + j + 1) * P], ident)
            m.then_inc(PE.sem, 1)
            PE.count += 1
            m = (PE.sem, PE.count)
            reads = [m]
            psv = ps[:, 0:nb * P].rearrange("p (j q) -> p j q", j=nb)
            pair = isinstance(dst, tuple)
            if pair:
                k = pre_n[0] % 2
                pre_n[0] += 1
                d = presplit[:, k, 0:nb * P].rearrange("p (j q) -> p j q", j=nb)
                free = pre_free[k]
            else:
                d, free = dst[:, j0:j0 + nb, tok:tok + P], list(dst_free)
            if gain is None:
                m2 = step(DV, [m] + free, v.tensor_copy, d, psv)
            else:
                m2 = step(DV, [m] + free, v.tensor_tensor, d, psv, bc(gain[:, j0:j0 + nb], P), ALU.mult)
            give(b, [m2])
            if shift is not None:
                m2 = step(DV, [m2], v.tensor_tensor, d, d, bc(shift[:, j0:j0 + nb], P), ALU.add)
            if pair:
                hi, lo = (x[:, j0:j0 + nb, tok:tok + P] for x in dst)
                pre_free[k] = split(d, hi, lo, [m2], dst_free)
                marks += pre_free[k]
            else:
                marks.append(m2)
        return marks, reads

    def norm_into_T(pool, srcs, width, dst, toks, after, gain=None, shift=None, dst_free=(), defer=False):
        r, rm, _ = rstd_of(srcs, width, after)

        def rest():
            return norm_rest(pool, srcs, width, dst, toks, after, gain, shift, dst_free, r, rm)

        return rest if defer else rest()

    def norm_rest(pool, srcs, width, dst, toks, after, gain, shift, dst_free, r, rm):
        marks = {}
        for i, s_ in enumerate(srcs):
            k = xn_n[0] % 2
            xn_n[0] += 1
            x_ = xn[:, k, 0:width]
            m = step(DV, [rm] + list(after[i]) + xn_free[k], v.tensor_scalar, x_, s_, r[:, i:i + 1], None, ALU.mult)
            mk, rd = into_T(pool, x_, width, dst, toks[i], [m], gain(i) if gain else None,
                            shift(i) if shift else None, dst_free)
            xn_free[k] = rd
            marks[i] = mk
        return marks

    def fence():
        return [m for e in COMPUTE for m in e.last()]

    def fence_all():
        f = fence()
        for e in COMPUTE:
            e.wait(f)
        return f

    def dbg(name, ap, after):
        if dump is not None and name in dump:
            AC.wait(after)
            dump[name](a, ap, new_sem("dump_" + name), loads)

    x_m = [load(AC, "x", H[:, 2:4, :], ins["x"].rearrange("(t p) d -> p t d", p=P))]
    cols_m = [load(SP, "cols", cols[:, :], ins["cols"])]
    sq_m = [load(SP, "sq", sq[:, :], ins["sq"])]
    bias_t5, lnc_at = carve(0, 16, 384)
    lnc = probsT[:, 0, 0:384]
    for i in range(NRAW):
        load_chunk(i, [])
    row_m = {}

    def load_row(slot, name, after=()):
        i = ROWS_ORDER.index(name)
        row_m[name] = [load(GP, name, rowbuf[:, slot, :], ins["rows"][i, :].partition_broadcast(P), after)]
        return rowbuf[:, slot, :]

    minus_half = sb("minus_half", [P, 1])
    GP.wait([step(DV, [], v.memset, minus_half[:, :], -0.5)])
    eps_col = sb("eps_col", [P, 1])
    eps_m = step(DV, [], v.memset, eps_col[:, :], EPS)
    AC.wait([eps_m])
    one_col = sb("one_col", [P, 1])
    one_m = step(DV, [], v.memset, one_col[:, :], 1.0)
    AC.wait([one_m])

    gemm = Pool([0, 1, 2, 3, 6, 7])
    turn = Pool([4, 5])
    outp = Pool([6, 7])

    csilu = sb("csilu", [P, KT, 2])
    csplit = sb("csplit", [P, KT, 4], F32R)
    modrow = sb("modrow", [4, 512])
    mod_dram = [nc.dram_tensor(f"mod_rows{i}", (4, 3 * D), F32).ap() for i in range(2)]
    mod_at = [0]
    mod_bank = [None]
    mod_stored = {0: [], 1: []}
    modrow_free = [[]]

    def fill(pool, n):
        for _ in range(n):
            at = mod_at[0]
            mod_at[0] += 1
            layer, c = MODS[at // 2]
            k0 = 4 * (at % 2)
            w, wm, wi = weights(f"mod{at}")
            if k0 == 0:
                mod_bank[0] = pool.take()
            b, ps, free = mod_bank[0]
            PE.wait(wm + c_m + (free if k0 == 0 else []))
            for k in range(4):
                for y in range(2):
                    m = t.matmul(ps[0:4, :], csplit[:, k0 + k, :], w[y][:, k, :], start=(k0 + k + y == 0), stop=(k0 + k == 7 and y == 1))
            m.then_inc(PE.sem, 1)
            PE.count += 1
            pm = (PE.sem, PE.count)
            used(wi, pm)
            if k0:
                mk = step(DV, [pm] + modrow_free[0], v.tensor_copy, modrow[:, :], ps[0:4, :])
                give(b, [mk])
                st = load(GP, f"mod_out{layer}{c}", mod_dram[layer][:, 512 * c:512 * c + 512], modrow[:, :], [mk])
                modrow_free[0] = [st]
                mod_stored[layer].append(st)

    probs_free = [[] for _ in range(4)]
    probsT_free = [[] for _ in range(4)]
    att_n = [0]

    def attention(qtiles, heads, q, k, nk, val, marks, finish, bias=None, b0=0, nbias=0, sink=None, filler=None):
        scores = Pool([0, 1, 2])
        items = [(qt, h) for qt in qtiles for h in range(heads)]
        state = {}
        outs = {}
        rsum = {qt: stat(heads) for qt in qtiles}
        esink = {qt: stat(heads) for qt in qtiles} if sink is not None else None
        summed = {}

        def head_scores(qt, h):
            n = nk(qt)
            b, ps, free = scores.take()
            m = products(free + marks, [(ps[:, 0:n], q(h, qt), k(h, n))])
            mn = stat(1)
            if bias is not None and nbias == n:
                m = step(DV, [m] + bias_marks, v.tensor_tensor_reduce, ps[:, 0:n], ps[:, 0:n], bias(h, qt),
                         1.0, 3e38, ALU.add, ALU.min, mn)
            else:
                if bias is not None:
                    m = step(DV, [m] + bias_marks, v.tensor_tensor, ps[:, b0:b0 + nbias], ps[:, b0:b0 + nbias],
                             bias(h, qt), ALU.subtract)
                m = step(DV, [m], v.tensor_reduce, mn, ps[:, 0:n], AX_X, ALU.min)
            if sink is not None:
                m = step(DV, [m], v.tensor_scalar, mn, sink(h), -1.0, mn, ALU.mult, ALU.min)
            i = att_n[0] % 4
            att_n[0] += 1
            pr = probs[:, i, 0:n]
            me = step(AC, [m] + probs_free[i] + junk_mark[0], a.activation, pr, ps[:, 0:n], ACT.Exp, bias=mn, scale=-1.0,
                      accum_out=rsum[qt][:, h:h + 1])
            give(b, [me])
            summed[(qt, h)] = [me]
            if sink is not None:
                summed[(qt, h)].append(step(AC, [m], a.activation, esink[qt][:, h:h + 1], sink(h), ACT.Exp, bias=mn))
            state[(qt, h)] = (i, pr, me, n)

        def head_values(qt, h):
            i, pr, me, n = state.pop((qt, h))
            b, ps, free = turn.take()
            PE.wait(free + [me])
            for j in range(n // P):
                m = t.transpose(ps[:, j * P:(j + 1) * P], pr[:, j * P:(j + 1) * P], ident)
            m.then_inc(PE.sem, 1)
            PE.count += 1
            m = (PE.sem, PE.count)
            probs_free[i] = [m]
            pT = probsT[:, i, 0:n]
            if (h + qt) % 2:
                me = step(AC, [m] + probsT_free[i], a.copy, pT, ps[:, 0:n])
            else:
                me = step(DV, [m] + probsT_free[i], v.tensor_copy, pT, ps[:, 0:n])
            give(b, [me])
            state[(qt, h, "T")] = (i, pT, me, n)

        def head_out(qt, h):
            i, pT, me, n = state.pop((qt, h, "T"))
            if h % 4 == 0:
                outs[0] = outp.take()
            b, po, free = outs[0]
            m = products(free + [me] + marks, [(po[:, (h % 4) * P:(h % 4 + 1) * P], pT[:, j * P:(j + 1) * P], val(h, j))
                                              for j in range(n // P)])
            probsT_free[i] = [m]
            if h % 4 == 3:
                hs = range(h - 3, h + 1)
                r = rsum[qt][:, h - 3:h + 1]
                dm = [x for hh in hs for x in summed[(qt, hh)]]
                if sink is not None:
                    dm = [step(DV, dm, v.tensor_tensor, r, r, esink[qt][:, h - 3:h + 1], ALU.add)]
                dm = [step(DV, dm, v.reciprocal, r, r)]
                give(b, finish(qt, h // 4, po, [m] + dm, r))

        for n in range(len(items) + 4):
            if n < len(items):
                head_scores(*items[n])
            if 2 <= n < len(items) + 2:
                head_values(*items[n - 2])
            if n >= 4:
                head_out(*items[n - 4])
            if filler is not None:
                filler(n)
        for i in range(4):
            junk_mark[0] = junk_mark[0] + probs_free[i]

    bias_marks = []

    split_up_to(1)
    for e in (PE, DV):
        e.wait(sq_m + cols_m)

    base = 16 * 384
    qaT, base = carve(base, 4, S)
    kaT, base = carve(base, 1, S)
    qbT, base = carve(base, 4, S)
    kbT, base = carve(base, 4, S)
    va, base = carve(base, 2, 128)
    vb, base = carve(base, 2, 512)
    o_tm, base = carve(base, 2, D)
    mix, _ = carve(0, 2, D)

    lat = [2, 3]
    m = norm_into_T(turn, [H[:, i, :] for i in lat], D, uT, [0, P], [x_m, x_m], gain=lambda i: col("g_pre_mix"))
    u_m = m[0] + m[1]
    c_m = [step(AC, cols_m, a.activation, csilu[:, :, :].rearrange("p a b -> p (a b)"), col("c"), ACT.Silu)]
    c_m = split(csilu[:, :, :], csplit[:, :, 0:2], csplit[:, :, 2:4], c_m, [])

    GP.wait(split_done[0])
    bias_m = [load(GP, "bias_t5", bias_t5, ins["bias_t5"])]
    lnc_m = [load(GP, "lnc", lnc, ins["lnc"])]
    small_m = [load(GP, "small_rows", small_rows[:, :], ins["small_rows"].partition_broadcast(P))]
    ma = step(GP, bias_m, g.tensor_scalar, bias_t5[:, 0:8, :], bias_t5[:, 0:8, :], -1.0, None, ALU.mult)
    m = step(GP, bias_m + lnc_m, g.tensor_tensor, bias_t5[:, 8:16, :],
             lnc.unsqueeze(1).to_broadcast([P, 8, 384]), bias_t5[:, 8:16, :], ALU.subtract)
    bias_marks = [ma, m]
    probsT_free[0] = [m]
    mask_f32 = H[:, 0:2, :].rearrange("p a b -> p (a b)")[:, 0:14 * P]
    misc_m = [load(GP, "sel4", sel4[:, :], ins["sel4"]), load(GP, "gla_mask", mask_f32, ins["gla_mask"]), load(GP, "rope", rope[:, :, :, :], ins["rope"])]
    misc_m.append(step(GP, misc_m, g.tensor_copy, gla_mask[:, :], mask_f32))
    ctx_m = [load(GP, "ctx", H[:, 0:2, :], ins["ctx"].rearrange("(t p) d -> p t d", p=P), misc_m)]
    g_post_mix = load_row(0, "g_post_mix")
    g_post_mlp = load_row(1, "g_post_mlp")

    def copy_out(dst, scale=None):
        def f(i, ps, mk):
            d = dst(i)
            n = d.shape[-1]
            mk = step(AC, [mk], a.activation, d, ps[:, 0:n], ACT.Copy, scale=1.0 if scale is None else scale)
            kept.append(mk)
            return [mk]
        return f

    def copy_out_v(dst):
        def f(i, ps, mk):
            d = dst(i)
            mk = step(DV, [mk], v.tensor_copy, d, ps[:, 0:d.shape[-1]])
            kept.append(mk)
            return [mk]
        return f

    kept = []
    project_fm(gemm, "qa", uT, u_m, 0, S, range(4), copy_out(lambda ft: qaT[:, ft, :], -HD ** -0.5))
    w, wm, wi = weights("kva")
    for it in range(3):
        b, ps, free = gemm.take()
        PE.wait(free + wm + u_m)
        for k in range(KT):
            for j, (x, y) in enumerate(HALVES):
                l, r = (w[x][:, k, 0:P], uT[y][:, k, 0:S]) if it == 0 else (uT[x][:, k, (it - 1) * P:it * P], w[y][:, k, :])
                m = t.matmul(ps[:, 0:S], l, r, start=(k + j == 0), stop=(k == KT - 1 and j == 2))
        m.then_inc(PE.sem, 1)
        PE.count += 1
        d, src = (kaT[:, 0, :], ps[:, 0:S]) if it == 0 else (va[:, it - 1, :], ps[:, P:2 * P])
        mk = step(DV, PE.last(), v.tensor_copy, d, src)
        kept.append(mk)
        give(b, [mk])
    used(wi, PE.last()[0])
    project_fm(gemm, "qb", uT, u_m, 0, S, range(4), copy_out(lambda ft: qbT[:, ft, :], -HD ** -0.5))
    project_fm(gemm, "kb", uT, u_m, 0, S, range(4), copy_out_v(lambda ft: kbT[:, ft, :]))
    project_tm(gemm, "vb", uT, lambda i: u_m, [0, 1], copy_out_v(lambda i: vb[:, i, :]))
    proj_m = kept[:]

    o_marks = {0: [], 1: []}

    def finish_to(dst, out_marks, same_half=False):
        def f(qt, hg, po, mk, r):
            if same_half:
                dm = step(DV, mk, v.tensor_tensor, dst(qt)[:, hg * 256:(hg + 1) * 256].rearrange("p (h d) -> p h d", h=4),
                          po.rearrange("p (h x) -> p h x", h=4)[:, :, 64 * hg:64 * hg + 64], bc(r, 64), ALU.mult)
            else:
                d = dst(qt)[:, hg * 256:(hg + 1) * 256].rearrange("p (c e d) -> p c e d", c=2, e=2)
                po_, r_ = po.rearrange("p (c e x) -> p c e x", c=2, e=2), r.rearrange("p (c e) -> p c e", c=2)
                for e in range(2):
                    dm = step(DV, mk, v.tensor_tensor, d[:, :, e], po_[:, :, e, 64 * e:64 * e + 64], bc(r_[:, :, e], 64), ALU.mult)
            out_marks(qt).append(dm)
            return [dm]
        return f

    def t5(h, qt):
        return bias_t5[:, h, (128 if qt == 0 else 0):(128 if qt == 0 else 0) + S]

    hp = lambda h: slice(64 * h, 64 * h + 64)
    fill_bank = Pool([3])

    def spread(n, items):
        at = [round((j + 0.5) * items / n) for j in range(n)]
        return lambda i: fill(fill_bank, at.count(i))

    attention([0, 1], 8, lambda h, qt: qaT[hp(h // 4), h % 4, qt * P:(qt + 1) * P], lambda h, n: kaT[hp(h // 4), 0, 0:n],
              lambda qt: S, lambda h, j: va[:, j, :], proj_m + small_m,
              finish_to(lambda qt: o_tm[:, qt, 0:512], lambda qt: o_marks[qt], True), bias=t5, nbias=S,
              sink=lambda h: small_rows[:, h:h + 1], filler=spread(FILL["attA"], 18))
    pair_of = lambda h: slice(128 * (h // 2), 128 * (h // 2) + 128)
    attention([0, 1], 8, lambda h, qt: qbT[hp(h % 2), h // 2, qt * P:(qt + 1) * P], lambda h, n: kbT[hp(h % 2), h // 2, 0:n],
              lambda qt: S, lambda h, j: vb[:, j, pair_of(h)], proj_m,
              finish_to(lambda qt: o_tm[:, qt, 512:1024], lambda qt: o_marks[qt]), bias=lambda h, qt: t5(h + 8, qt), nbias=S,
              filler=spread(FILL["attB"], 18))
    fill(fill_bank, FILL["o"])
    dbg("o_tm", o_tm, o_marks[0] + o_marks[1])

    dead_u = PE.last()
    ob = [o_marks[0], o_marks[1]]
    m1 = norm_into_T(turn, [o_tm[:, i, 0:512] for i in range(2)], 512, tuple(x[:, 0:4, :] for x in uT), [0, P], ob,
                     gain=lambda i: col("g_out_a"), dst_free=dead_u)
    m2 = norm_into_T(turn, [o_tm[:, i, 512:1024] for i in range(2)], 512, tuple(x[:, 4:8, :] for x in uT), [0, P], ob,
                     gain=lambda i: col("g_out_b"), dst_free=dead_u)
    oT_m = [m1[0] + m2[0], m1[1] + m2[1]]

    def project_1024(names, srcT, src_marks, tiles, evac):
        for c, name in enumerate(names):
            project_tm(gemm, name, srcT, src_marks, tiles, lambda i, ps, mk, c=c: evac(i, c, ps, mk))

    def half(ap, c):
        return ap[:, c * 512:(c + 1) * 512]

    def residual_norm(src, src_marks, gain, gain_marks):
        r, rm, _ = rstd_of([src[:, i, :] for i in range(2)], D, [src_marks[i] for i in range(2)])
        res = []
        for i in range(2):
            mk = step(DV, [rm] + src_marks[i] + gain_marks, v.scalar_tensor_tensor, src[:, i, :], src[:, i, :],
                      r[:, i:i + 1], gain, ALU.mult, ALU.mult)
            res.append([step(GP, [mk], g.tensor_tensor, H[:, 2 + i, :], H[:, 2 + i, :], src[:, i, :], ALU.add)])
        return res

    mix_marks = [[], []]
    bias_dead = DV.last()

    def mix_evac(i, c, ps, mk):
        mk = step(DV if c else AC, [mk] + bias_dead, v.tensor_copy if c else a.copy, half(mix[:, i, :], c), ps)
        mix_marks[i].append(mk)
        return [mk]

    project_1024(["wo0", "wo1"], uT, lambda i: oT_m[i], [0, 1], mix_evac)
    fill(fill_bank, FILL["mix"])
    h_m = residual_norm(mix, mix_marks, g_post_mix, row_m["g_post_mix"])
    b_ple = load_row(0, "b_ple_gate", DV.last())
    dbg("h1", H[:, 2:4, :], h_m[0] + h_m[1])

    dead = PE.last()
    m = norm_into_T(turn, [H[:, i, :] for i in lat], D, uT, [0, P], h_m, gain=lambda i: col("g_pre_mlp"), dst_free=dead)
    v_m = m[0] + m[1]
    hidden = [tuple(x[:, 4 * k:4 * k + 4, S:2 * S] for x in uT) for k in range(2)]
    relu, _ = carve(2 * D, 4, 512)
    relu_free = [fence() for _ in range(4)]
    hidden_free = [[], []]
    mix_dead = fence()
    up_pool = Pool([4, 5, 6, 7])
    down = {(i, h): banks[:, 2 * i + h, :] for i in range(2) for h in range(2)}
    hid_m = {}
    down_free = [m for b in range(4) for m in bank_free[b]]
    mix_marks = [[], []]
    for c in range(9):
        if c < 8:
            sl = c % 2
            hm = []
            for kc in range(2):
                w, wm, wi = weights(f"up{c}.{kc}")
                b, ps, free = up_pool.take()
                for f in range(2):
                    PE.wait(free + wm + v_m)
                    for k in range(KT):
                        for j, (x, y) in enumerate(HALVES):
                            m = t.matmul(ps[:, f * S:(f + 1) * S], w[x][:, k, f * P:(f + 1) * P], uT[y][:, k, 0:S],
                                         start=(k + j == 0), stop=(k == KT - 1 and j == 2))
                m.then_inc(PE.sem, 1)
                PE.count += 1
                pm = (PE.sem, PE.count)
                rk = (2 * c + kc) % 4
                rl = relu[:, rk, :]
                rm = step(AC, [pm] + relu_free[rk], a.activation, rl, ps, ACT.Relu)
                give(b, [rm])
                sm = step(GP, [rm], g.tensor_tensor, rl, rl, rl, ALU.mult)
                hi, lo = (x[:, 2 * kc:2 * kc + 2, :] for x in hidden[sl])
                relu_free[rk] = split(rl.rearrange("p (f s) -> p f s", f=2), hi, lo, [sm], hidden_free[sl])
                hm += relu_free[rk]
                used(wi, pm)
            hid_m[c] = hm
        if c:
            hi, lo = hidden[(c - 1) % 2]
            for h in range(2):
                w, wm, wi = weights(f"down{c - 1}{h}")
                for i in range(2):
                    PE.wait(wm + hid_m[c - 1] + (down_free if c == 1 else []))
                    for k in range(4):
                        for j, (x, y) in enumerate(HALVES):
                            m = t.matmul(down[(i, h)], (hi, lo)[x][:, k, i * P:(i + 1) * P], w[y][:, k, :],
                                         start=(c == 1 and k + j == 0), stop=(c == 8 and k == 3 and j == 2))
                    m.then_inc(PE.sem, 1)
                    PE.count += 1
                    pm = (PE.sem, PE.count)
                    if c == 8:
                        mk = step(DV if i else AC, [pm] + mix_dead, v.tensor_copy if i else a.copy, half(mix[:, i, :], h), down[(i, h)])
                        give(2 * i + h, [mk])
                        mix_marks[i].append(mk)
                used(wi, pm)
            hidden_free[(c - 1) % 2] = [pm]
    h_m = residual_norm(mix, mix_marks, g_post_mlp, row_m["g_post_mlp"])
    g_post_ple = load_row(1, "g_post_ple", DV.last())
    dbg("h2", H[:, 2:4, :], h_m[0] + h_m[1])

    pf, base = carve(2 * D, 2, S)
    gate_tm, base = carve(base, 2, D)
    ple_tm, base = carve(base, 2, D)
    arena_free = fence()
    pT = tuple(x[:, 0:2, S:2 * S] for x in uT)
    pT_m = split(pf, pT[0], pT[1], [load(AC, "pT", pf, ins["pT"].rearrange("(k p) t -> p k t", p=P), arena_free)], arena_free)
    w, wm, wi = weights("ple")
    ple_marks = [[], []]
    for i in range(2):
        for c in range(2):
            b, ps, free = gemm.take()
            PE.wait(free + wm + pT_m)
            for k in range(2):
                for j, (x, y) in enumerate(HALVES):
                    m = t.matmul(ps, pT[x][:, k, i * P:(i + 1) * P], w[y][:, k, c * 512:c * 512 + 512],
                                 start=(k + j == 0), stop=(k == 1 and j == 2))
            m.then_inc(PE.sem, 1)
            PE.count += 1
            mk = step(AC, PE.last() + arena_free, a.copy, half(ple_tm[:, i, :], c), ps)
            give(b, [mk])
            ple_marks[i].append(mk)
    used(wi, PE.last()[0])
    fill(gemm, FILL["mlp"])
    hT_m = []
    for i in range(2):
        mk, _ = into_T(turn, H[:, 2 + i, :], D, uT, i * P, h_m[i], dst_free=dead)
        hT_m.append(mk)
    mix_marks = [[], []]

    def gate_evac(i, c, ps, mk):
        gsl = half(gate_tm[:, i, :], c)
        m1 = step(DV, [mk] + row_m["b_ple_gate"], v.tensor_tensor, gsl, ps, half(b_ple, c), ALU.add)
        m2 = step(AC, [m1], a.activation, gsl, gsl, ACT.Sigmoid)
        mix_marks[i].append(step(GP, [m2] + ple_marks[i] + arena_free, g.tensor_tensor, half(mix[:, i, :], c), gsl,
                                 half(ple_tm[:, i, :], c), ALU.mult))
        return [m1]

    project_1024(["pg0", "pg1"], uT, lambda i: hT_m[i], [0, 1], gate_evac)
    fill(gemm, FILL["ple"])
    h_m = residual_norm(mix, mix_marks, g_post_ple, row_m["g_post_ple"])
    dbg("h3", H[:, 2:4, :], h_m[0] + h_m[1])

    row_free = fence()
    gateB = {0: rowbuf[:, 0, :], 1: rowbuf[:, 1, :]}
    mod_shift, mod_gain = sb("mod_shift", [P, KT, 2]), sb("mod_gain", [P, KT, 2])
    mod_sum = sb("mod_sum", [P, 32])

    def modulation(layer, streams, readers):
        back = probsT[0:64, 0, 0:P]
        src = mod_dram[layer][:, 0:2 * D].rearrange("r (j q) -> r j q", q=P)
        bm = []
        for r in range(4):
            bm.append(load(AC, f"mod_cols{layer}{r}", probsT[16 * r:16 * r + 16, 0, 0:P], src[r], mod_stored[layer] + readers))
        rows = probsT[0:4, 1:3, :].rearrange("p a b -> p (a b)")
        gm = [load(AC, f"mod_gates{layer}", rows, mod_dram[layer][:, 2 * D:3 * D], mod_stored[layer] + readers)]
        bg = xn[:, 0, :]
        bgm = [load(AC, f"b_gate{layer}", bg, ins["rows"][ROWS_ORDER.index(f"l{layer}_b_gate"), :].partition_broadcast(P), readers)]
        b, ps, free = turn.take()
        PE.wait(free + bm)
        m = t.transpose(ps[:, 0:64], back, sq[0:64, 0:64])
        m.then_inc(PE.sem, 1)
        PE.count += 1
        m = step(DV, PE.last() + readers, v.tensor_copy, mod_sum[:, :], ps[:, 0:32])
        m = step(DV, [m], v.tensor_tensor, mod_sum[:, :], mod_sum[:, :], ps[:, 32:64], ALU.add)
        give(b, [m])
        sums = mod_sum[:, :].rearrange("p (r c j) -> p c j r", r=2, c=2)
        ms = step(DV, [m], v.tensor_tensor, mod_shift[:, :, :], sums[:, 0], bc(col(f"l{layer}_b_mod", 0, 8), 2), ALU.add)
        m = step(DV, [m], v.tensor_tensor, mod_gain[:, :, :], sums[:, 1], bc(col(f"l{layer}_b_mod", 8, 8), 2), ALU.add)
        m = step(DV, [m], v.tensor_scalar, mod_gain[:, :, :], mod_gain[:, :, :], 1.0, None, ALU.add)
        m = step(DV, [m], v.tensor_tensor, mod_gain[:, :, :], mod_gain[:, :, :], bc(col(f"l{layer}_norm"), 2), ALU.mult)
        gates = []
        for r in streams:
            for c in range(2):
                b, ps, free = gemm.take()
                pm = products(free + gm + misc_m, [(ps, sel4[:, r * P:(r + 1) * P], rows[:, c * 512:(c + 1) * 512])])
                m2 = step(DV, [pm] + readers + bgm, v.tensor_tensor, half(gateB[r], c), ps, half(bg, c), ALU.add)
                give(b, [m2])
                gates.append(m2)
        probsT_free[0] = probsT_free[1] = probsT_free[2] = PE.last()
        xn_free[0] = gates[-1:]
        return [ms, m], gates

    def modulated_norm(tiles, marks, mod_m, dst_free):
        stream = lambda tile: 0 if tile < 2 else 1
        m = norm_into_T(turn, [H[:, i, :] for i in tiles], D, uT, [i * P for i in tiles],
                        [marks[i] + mod_m for i in tiles],
                        gain=lambda i: mod_gain[:, :, stream(tiles[i])],
                        shift=lambda i: mod_shift[:, :, stream(tiles[i])], dst_free=dst_free)
        return {tile: m[i] for i, tile in enumerate(tiles)}

    def gate_and_out(names, tiles, tile0, catT, cat_marks, H_marks, release):
        res = {i: [] for i in tiles}

        def evac(i, c, ps, mk):
            k = (2 * c + i) % 4
            tile = i + tile0
            tmp = probsT[:, k, :]
            m1 = step(DV, [mk] + probsT_free[k] + gates_m, v.tensor_tensor, tmp, ps, half(gateB[0 if tile < 2 else 1], c), ALU.mult)
            m2 = step(GP, [m1] + H_marks[tile], g.tensor_tensor, half(H[:, tile, :], c), half(H[:, tile, :], c), tmp, ALU.add)
            probsT_free[k] = [m2]
            res[i].append(m2)
            return [m1]

        project_1024(names, catT, lambda i: cat_marks[i], tiles, evac)
        return {i + tile0: res[i] for i in tiles}

    mod_m, gates_m = modulation(0, [0, 1], row_free)
    ctx_marks = {0: ctx_m, 1: ctx_m, 2: h_m[0], 3: h_m[1]}
    um = modulated_norm([0, 1, 2, 3], ctx_marks, mod_m, PE.last())
    u_all = [x for i in range(4) for x in um[i]]
    stage0 = fence_all()
    all4 = range(4)
    a_tm, base = carve(0, 4, 512)
    qT, base = carve(base, 8, 512)
    kT, base = carve(base, 8, 512)
    v_tm, base = carve(base, 4, 512)
    kr_tm, base = carve(base, 4, ROPE)
    q_tm = xn[:, 0, 0:8 * QK].rearrange("p (h d) -> p h d", h=8)
    k_tm = xn[:, 1, 0:8 * QK].rearrange("p (h d) -> p h d", h=8)
    g_tm = sb("g_tm", [P, 4, 16])
    rtmp = sb("rtmp", [P, 4, 128])

    kr_m, gt_m, cq_raw, ckv_raw = {}, {}, {}, {}
    cq_tm, _ = carve(0, 4, Q_RANK)
    ckv_tm, _ = carve(4 * 512 + 16 * 512, 4, KV_RANK)
    cqT, _ = carve(4 * 512 + 8 * 512, 3, 512)
    ckvT, _ = carve(4 * 512 + 8 * 512 + 3 * 512, 2, 512)

    def cq_evac(i, ps, mk):
        cq_raw[i] = [step(AC, [mk], a.copy, cq_tm[:, i, :], ps[:, 0:Q_RANK])]
        return cq_raw[i]

    project_tm(gemm, "cq", uT, lambda i: um[i], all4, cq_evac, n=Q_RANK)
    cq_m = norm_into_T(turn, [cq_tm[:, i, :] for i in all4], Q_RANK, cqT, [i * P for i in all4], [cq_raw[i] for i in all4],
                       gain=lambda _: col("q_norm"), defer=True)

    def ckv_evac(i, ps, mk):
        m1 = step(DV, [mk], v.tensor_copy, kr_tm[:, i, :], ps[:, KV_RANK:KV_RANK + ROPE])
        m2 = step(DV, [mk] + small_m, v.tensor_tensor, g_tm[:, i, :], ps[:, KV_RANK + ROPE:KV_RANK + ROPE + 16],
                  small_rows[:, 8:24], ALU.add)
        m3 = step(AC, [m2], a.copy, ckv_tm[:, i, :], ps[:, 0:KV_RANK])
        kr_m[i], gt_m[i], ckv_raw[i] = [m1], m2, [m3]
        return [m3]

    project_tm(gemm, "ckv", uT, lambda i: um[i], all4, ckv_evac, n=KV_RANK + ROPE + 16)
    cq_m = cq_m()
    ckv_m = norm_into_T(turn, [ckv_tm[:, i, :] for i in all4], KV_RANK, ckvT, [i * P for i in all4], [ckv_raw[i] for i in all4],
                        gain=lambda _: col("kv_norm"))

    rt_free = [[]]

    def rotate(view, nh, tile, after):
        y = view.rearrange("p h (a two c) -> p h a two c", a=2, two=2)
        y1, y2 = y[:, :, :, 0, :], y[:, :, :, 1, :]

        def table(which):
            x_ = rope[:, tile, which, :].rearrange("p (a c) -> p a c", a=2)
            return x_.unsqueeze(1).to_broadcast([P, nh, 2, PAIRS])

        tmp = [rtmp[:, j, 0:nh * 16].rearrange("p (h a c) -> p h a c", h=nh, a=2) for j in range(4)]
        ms = []
        for j, (y_, w_) in enumerate(((y1, 0), (y2, 1), (y2, 0), (y1, 1))):
            ms.append(step(GP, after + rt_free[0] + misc_m, g.tensor_tensor, tmp[j], y_, table(w_), ALU.mult))
        m1 = step(GP, ms, g.tensor_tensor, y1, tmp[0], tmp[1], ALU.subtract)
        m2 = step(GP, ms, g.tensor_tensor, y2, tmp[2], tmp[3], ALU.add)
        rt_free[0] = [m1, m2]
        return [m1, m2]

    def heads_into_T(src, dst, tile, after):
        res = []
        for hh in range(2):
            b, ps, free = turn.take()
            PE.wait(free + after)
            for j in range(4):
                m = t.transpose(ps[0:QK, j * P:(j + 1) * P], src[:, 4 * hh + j, :], ident)
            m.then_inc(PE.sem, 1)
            PE.count += 1
            d = dst[0:QK, 4 * hh:4 * hh + 4, tile * P:(tile + 1) * P]
            psv = ps[0:QK, :].rearrange("p (j q) -> p j q", j=4)
            mk = step(DV, PE.last(), v.tensor_copy, d, psv) if hh else step(AC, PE.last(), a.copy, d, psv)
            give(b, [mk])
            res.append(mk)
        return res, PE.last()

    wq = [weights("uq0"), weights("uq1")]
    q_free, qT_m = xn_free[0] + xn_free[1], []
    for i in all4:
        qf = q_tm.rearrange("p a b -> p (a b)")
        ms = []
        for c0, n, (w, wm, wi) in ((0, 512, wq[0]), (512, 256, wq[1])):
            b, ps, free = gemm.take()
            pm = products(free + wm + cq_m[i], [(ps[:, 0:n], cqT[:, k, i * P:(i + 1) * P], w[:, k, 0:n]) for k in range(3)])
            mk = step(AC, [pm] + q_free, a.activation, qf[:, c0:c0 + n], ps[:, 0:n], ACT.Copy, scale=-QK ** -0.5)
            give(b, [mk])
            ms.append(mk)
        if i >= 2:
            ms = ms + rotate(q_tm[:, :, NOPE:QK], 8, i - 2, ms)
        mk, q_free = heads_into_T(q_tm, qT, i, ms)
        qT_m += mk
    used(wq[0][2], pm)
    used(wq[1][2], pm)
    w, wm, wi = weights("ukv")
    k_free, kv_m = xn_free[0] + xn_free[1], []
    for i in all4:
        ms = []
        for hh in range(2):
            b, ps, free = gemm.take()
            pm = products(free + wm + ckv_m[i], [(ps, ckvT[:, k, i * P:(i + 1) * P], w[:, k, hh * 512:hh * 512 + 512]) for k in range(2)])
            kvv = ps.rearrange("p (h d) -> p h d", h=4)
            m1 = step(DV, [pm] + k_free, v.tensor_copy, k_tm[:, 4 * hh:4 * hh + 4, 0:NOPE], kvv[:, :, 0:NOPE])
            m2 = step(AC, [m1], a.copy, v_tm[:, i, hh * 256:hh * 256 + 256].rearrange("p (h d) -> p h d", h=4), kvv[:, :, NOPE:])
            give(b, [m1, m2])
            kv_m.append(m2)
            ms.append(m1)
        krv = kr_tm[:, i, :].unsqueeze(1)
        if i >= 2:
            kr_m[i] = kr_m[i] + rotate(krv, 1, i - 2, kr_m[i])
        ms.append(step(DV, kr_m[i] + k_free, v.tensor_copy, k_tm[:, :, NOPE:QK], krv.to_broadcast([P, 8, ROPE])))
        mk, k_free = heads_into_T(k_tm, kT, i, ms + [pm])
        kv_m += mk
    used(wi, pm)
    xn_free[0] = xn_free[1] = PE.last()
    cat_free = fence()
    for e in (DV, AC):
        e.wait(cat_free)
    a_m = {i: [] for i in all4}
    bias_marks = []
    attention(all4, 8, lambda h, qt: qT[0:QK, h, qt * P:(qt + 1) * P], lambda h, n: kT[0:QK, h, 0:n],
              lambda qt: 256 if qt < 2 else 512, lambda h, j: v_tm[:, j, pair_of(h)], qT_m + kv_m,
              finish_to(lambda qt: a_tm[:, qt, :], lambda qt: a_m[qt]), filler=spread(FILL["mla"], 34))
    dbg("mla", a_tm, fence())

    stage1 = fence_all()
    h_tm, base = carve(4 * 512, 4, 512)
    mlT = []
    for _ in range(2):
        w_, base = carve(base, 4, 512)
        mlT.append(w_)
    mv, base = carve(base, 4, 4, 132)
    dec, base = carve(base, 2, 512)
    selneg = arena[0:4, base:base + 4 * P]
    selneg_m = [load(AC, "selneg", selneg, ins["selneg"], stage1)]
    base += 4 * P
    pads = [h_tm[:, k, :] for k in ()]
    b2 = 4 * 512
    for _ in range(2):
        w_, b2 = carve(b2, 2, 384)
        pads.append(w_)
    assert b2 <= 8 * 512
    pads = pads * 2
    Mrow = xn
    glog, gb, ga_ = sb("glog", [P, 4, 2, 4]), sb("gb", [P, 4, 2, 4]), sb("ga_", [P, 4, 2, 4])
    gem = sb("gem", [P, 4, 2, 4])
    ml_m = [[], []]
    for which, name in enumerate(("mq", "mk")):
        def conv_evac(ft, ps, mk, which=which):
            d = mlT[which][:, ft, :]
            cw = col("conv_w").rearrange("p (j f) -> p j f", j=3)
            f = 4 * which + ft
            dr, pr = (x_.rearrange("p (r s) -> p r s", r=2) for x_ in (d, ps))
            m = step(DV, [mk], v.tensor_scalar, d, ps, cw[:, 1, f:f + 1], col("conv_b", f, 1), ALU.mult, ALU.add)
            m = step(DV, [m], v.scalar_tensor_tensor, dr[:, :, 1:S], pr[:, :, 0:S - 1], cw[:, 0, f:f + 1], dr[:, :, 1:S], ALU.mult, ALU.add)
            m = step(DV, [m], v.scalar_tensor_tensor, dr[:, :, 0:S - 1], pr[:, :, 1:S], cw[:, 2, f:f + 1], dr[:, :, 0:S - 1], ALU.mult, ALU.add)
            ml_m[which].append(step(AC, [m], a.activation, d, d, ACT.Silu))
            return [m]
        project_fm(gemm, name, uT, u_all, 0, 512, range(4), conv_evac)
    mv_ones = step(GP, [], g.memset, mv[:, :, :, 128:129], 1.0)
    mv_m = [mv_ones]

    def mv_evac(i, ps, mk):
        mk = step(DV, [mk], v.tensor_copy, mv[:, i, :, 0:128], ps.rearrange("p (h d) -> p h d", h=4))
        mv_m.append(mk)
        return [mk]

    project_tm(gemm, "mv", uT, lambda i: um[i], all4, mv_evac)
    def log_sigmoid(x_, tmp, dst, after):
        m = step(AC, after, a.activation, tmp, x_, ACT.Abs)
        m = step(AC, [m], a.activation, tmp, tmp, ACT.Exp, scale=-1.0)
        m = step(AC, [m], a.activation, tmp, tmp, ACT.Ln, bias=one_col[:, 0:1])
        return step(DV, [m] + list(after), v.scalar_tensor_tensor, dst, x_, 0.0, tmp, ALU.min, ALU.subtract)

    gv5 = g_tm[:, :, :].rearrange("p t (d w h) -> p t d w h", d=2, w=2)
    gtm = list(gt_m.values())
    ftmp = rtmp[:, 0, 0:32].rearrange("p (t d h) -> p t d h", t=4, d=2)
    fin = rtmp[:, 1, 0:32].rearrange("p (t d h) -> p t d h", t=4, d=2)
    m = step(DV, gtm + rt_free[0], v.tensor_copy, fin, gv5[:, :, :, 1, :])
    fl = lambda x_: x_.rearrange("p t d h -> p (t d h)")
    lf_m = log_sigmoid(rtmp[:, 1, 0:32], rtmp[:, 0, 0:32], fl(glog[:, :, :, :]), [m])
    b, ps, free = gemm.take()
    gbp = ps[:, 0:32].rearrange("p (t d h) -> p t d h", t=4, d=2)
    for i in all4:
        for d in range(2):
            if d == 0:
                src = [(j, "ones") for j in range(i)] + [(i, "tri_u")]
            elif i < 2:
                src = [(i, "tri_l")] + [(j, "ones") for j in range(i + 1, 2)]
            else:
                src = [(0, "ones"), (1, "ones"), (i, "tri_l")] + [(j, "ones") for j in range(i + 1, 4)]
            pm = products(free + [lf_m], [(gbp[:, i, d, :], sqc(n_), glog[:, j, d, :]) for j, n_ in src])
    bm = step(DV, [pm], v.tensor_copy, gb[:, :, :, :], gbp)
    give(b, [bm])
    am = step(DV, [bm], v.tensor_tensor, ga_[:, :, :, :], gv5[:, :, :, 0, :], gb[:, :, :, :], ALU.subtract)
    zm = step(GP, [], g.memset, arena[0:4, 4 * 512:4 * 512 + 2 * 768], 0.0)
    for d in range(2):
        b, ps, free = gemm.take()
        PE.wait(free + [am])
        for i in all4:
            m = t.transpose(ps[0:4, i * P:(i + 1) * P], ga_[:, i, d, :], ident)
        m.then_inc(PE.sem, 1)
        PE.count += 1
        lo = 128 if d == 0 else 0
        own = pads[2 * d:2 * d + 2]
        if d:
            zm = step(GP, Mm, g.memset, arena[0:4, 4 * 512:4 * 512 + 2 * 768], 0.0)
        m = step(DV, PE.last() + [zm], v.tensor_copy, own[0][0:4, :, lo:lo + S], ps[0:4, :].rearrange("p (r s) -> p r s", r=2))
        give(b, [m])
        cur = 0
        for sh in (1, 2, 4, 8, 16, 32, 64, 128):
            s_ = own[cur][0:4]
            o_ = own[1 - cur][0:4]
            off = lo - sh if d == 0 else sh
            m = step(DV, [m], v.tensor_tensor, o_[:, :, lo:lo + S], s_[:, :, lo:lo + S], s_[:, :, off:off + S], ALU.max)
            cur = 1 - cur
        s_ = own[cur][0:4]
        carry = s_[:, 0, lo + S - 1:lo + S] if d == 0 else s_[:, 0, lo:lo + 1]
        m1 = step(DV, [m], v.tensor_scalar, Mrow[0:4, d, 0:S], s_[:, 0, lo:lo + S], 0.0, None, ALU.max)
        m2 = step(DV, [m], v.tensor_scalar, Mrow[0:4, d, S:2 * S], s_[:, 1, lo:lo + S], carry, 0.0, ALU.max, ALU.max)
        if d == 0:
            Mm = [m1, m2]
        else:
            Mm = Mm + [m1, m2]
    b, ps, free = gemm.take()
    PE.wait(free + Mm)
    mtp = ps[:, 0:32].rearrange("p (t d h) -> p t d h", t=4, d=2)
    for i in all4:
        for d in range(2):
            m = t.transpose(mtp[:, i, d, :], Mrow[0:4, d, i * P:(i + 1) * P], sq[0:4, 0:4])
    m.then_inc(PE.sem, 1)
    PE.count += 1
    m = step(DV, PE.last(), v.tensor_tensor, gem[:, :, :, :], mtp, gb[:, :, :, :], ALU.add)
    give(b, [m])
    m = step(DV, [m], v.tensor_scalar, gem[:, :, :, :], gem[:, :, :, :], -1.0, 80.0, ALU.mult, ALU.min)
    em_m = step(AC, [m], a.activation, fl(gem[:, :, :, :]), fl(gem[:, :, :, :]), ACT.Exp)
    pads_dead = fence()
    DV.wait(pads_dead)
    dbg("gem", gem[:, :, :, :], [em_m])

    reach = {0: [[0, 1, 2, 3], [1, 2, 3], [2, 3], [3]], 1: [[0, 2, 3], [0, 1, 2, 3], [2], [2, 3]]}
    ranges = {0: [[(0, 4)], [(1, 4)], [(2, 4)], [(3, 4)]], 1: [[(0, 1), (2, 4)], [(0, 4)], [(2, 3)], [(2, 4)]]}
    nd_m = []
    prod_free = [[], []]
    dec_free = [[], []]
    wl_free = [[] for _ in range(4)]
    prodP = [probs, probsT]
    ap = Pool([0, 1])
    sp_ = Pool([2, 3, 4, 5])
    hp_ = Pool([6, 7])
    all_in = ml_m[0] + ml_m[1] + mv_m
    wtmp_free = [[], []]
    for h in range(ML_H):
        decs = []
        for d in range(2):
            b, ps, free = ap.take()
            pm = products(free + Mm + selneg_m, [(ps, selneg[:, h * P:(h + 1) * P], Mrow[0:4, d, 0:512])])
            dm = step(DV, [pm] + dec_free[d], v.tensor_tensor, dec[:, d, :].rearrange("p (j q) -> p j q", j=4),
                      ps.rearrange("p (j q) -> p j q", j=4),
                      sqc("neg_u" if d == 0 else "neg_l").unsqueeze(1).to_broadcast([P, 4, P]), ALU.add)
            decs.append((b, ps, pm, dm))
        st = []
        for s_ in range(4):
            b, ps, free = sp_.take()
            c0 = 0 if s_ < 2 else 256
            pm = products(free + all_in, [(ps[:, c0:512], mlT[1][:, h, s_ * P:(s_ + 1) * P], mlT[0][:, h, c0:512])])
            st.append((b, ps, pm, []))
        pmk = {}
        for d in range(2):
            bD, psD, pmD, dmD = decs[d]
            readers = []
            for s_ in range(4):
                wl = xn[:, (2 * d + s_) % 2, 512:1024]
                wk = (2 * d + s_) % 2
                ems = []
                for (c0, c1) in ranges[d][s_]:
                    for (x0, x1) in ((c0, min(c1, s_)), (max(c0, s_ + 1), c1)):
                        if x0 < x1:
                            m = step(AC, [dmD, am] + wtmp_free[wk], a.activation, wl[:, x0 * P:x1 * P], psD[:, x0 * P:x1 * P],
                                     ACT.Exp, bias=ga_[:, s_, d, h:h + 1])
                            ems.append(m)
                            readers.append(m)
                m = step(AC, [dmD, am] + wtmp_free[wk], a.activation, wl[:, s_ * P:(s_ + 1) * P], dec[:, d, s_ * P:(s_ + 1) * P],
                         ACT.Exp, bias=ga_[:, s_, d, h:h + 1])
                ems.append(m)
                dlast = m
                b, ps, pm, rd = st[s_]
                for (c0, c1) in ranges[d][s_]:
                    m = step(DV, ems + [pm] + prod_free[d], v.scalar_tensor_tensor, prodP[d][:, s_, c0 * P:c1 * P],
                             ps[:, c0 * P:c1 * P], ML_D ** -0.5, wl[:, c0 * P:c1 * P], ALU.mult, ALU.mult)
                    rd.append(m)
                wtmp_free[wk] = [m]
                pmk[(d, s_)] = m
            dec_free[d] = [dlast]
            give(bD, readers + [dmD])
        for b, ps, pm, rd in st:
            give(b, rd)
        for i in all4:
            b, ps, free = hp_.take()
            for d in range(2):
                srcs = [s_ for s_ in range(4) if i in reach[d][s_]]
                m = products(free + [pmk[(d, s_)] for s_ in srcs],
                             [(ps[:, d * 132:d * 132 + 129], prodP[d][:, s_, i * P:(i + 1) * P], mv[:, s_, h, 0:129]) for s_ in srcs])
            den = ps[:, 0:264].rearrange("p (d w) -> p d w", d=2)[:, :, 128]
            r_ = stat(2)
            mk = step(DV, [m], v.tensor_scalar, r_, den, -1.0, None, ALU.mult)
            mk = step(DV, [mk], v.tensor_tensor, r_, r_, den, ALU.max)
            mk = step(DV, [mk, em_m], v.tensor_tensor, r_, r_, gem[:, i, :, h], ALU.max)
            mk = step(DV, [mk], v.reciprocal, r_, r_)
            hd = h_tm[:, i, h * P:(h + 1) * P]
            mk = step(DV, [mk], v.tensor_scalar, hd, ps[:, 0:128], r_[:, 0:1], None, ALU.mult)
            mk = step(DV, [mk], v.scalar_tensor_tensor, hd, ps[:, 132:260], r_[:, 1:2], hd, ALU.mult, ALU.add)
            give(b, [mk])
            nd_m.append(mk)
        prod_free = [[m], [m]]

    sig_stage = fence()
    hm_m = {}

    def mo_evac(i, ps, mk):
        k = i % 4
        m1 = step(AC, [mk] + sig_stage, a.activation, probs[:, k, :], ps, ACT.Sigmoid)
        hm_m[i] = [step(DV, [m1] + nd_m, v.tensor_tensor, h_tm[:, i, :], h_tm[:, i, :], probs[:, k, :], ALU.mult)]
        return [m1]

    project_tm(gemm, "mo", uT, lambda i: um[i], all4, mo_evac)
    def head_norm(ap_, n, width, after, sq_buf, eng):
        E_, e_ = eng
        view = ap_.rearrange("p (h w) -> p h w", h=n)
        sqv = sq_buf.rearrange("p (h w) -> p h w", h=n)
        ss = stat(n)
        m = step(E_, after, e_.tensor_tensor, sqv, view, view, ALU.mult)
        m = step(DV, [m], v.tensor_reduce, ss, sqv, AX_X, ALU.add)
        m = step(GP, [m], g.tensor_scalar, ss, ss, 1.0 / width, EPS, ALU.mult, ALU.add)
        m = step(GP, [m], g.tensor_tensor, ss, ss, minus_half[:, 0:1].to_broadcast([P, n]), ALU.pow)
        return [step(E_, [m], e_.tensor_tensor, view, view, bc(ss, width), ALU.mult)]

    for i in all4:
        hm_m[i] = head_norm(h_tm[:, i, :], 4, 128, hm_m[i], probsT[:, i, :], (DV, v) if i % 2 else (GP, g))
    dbg("hm", h_tm, fence())

    def gated_cat_T(layer, tiles, tile0, halves, cat_m, gains):
        res = {i - tile0: [] for i in tiles}
        zm = {}
        for c in range(2):
            def z_evac(i, ps, mk, c=c):
                k = i % 4
                tmp = probs[:, k, :]
                m1 = step(AC, [mk] + probs_free[k] + junk_mark[0], a.activation, tmp, ps, ACT.Silu)
                x_ = halves[c][:, i - tile0, :]
                m2 = step(GP if i % 2 else DV, [m1] + cat_m[i - tile0], (g if i % 2 else v).tensor_tensor, x_, x_, tmp, ALU.mult)
                probs_free[k] = [m2]
                zm[(i, c)] = m2
                return [m1]
            project_tm(gemm, f"z{layer}{c}", uT, lambda i: um[i], tiles, z_evac)
        dead = PE.last()
        if layer == 0:
            fill(gemm, FILL["cat"])
        for i in tiles:
            for c in range(2):
                mk, _ = into_T(turn, halves[c][:, i - tile0, :], 512, tuple(x[:, 4 * c:4 * c + 4, :] for x in uT),
                               (i - tile0) * P, [zm[(i, c)]], gain=gains[c], dst_free=dead)
                res[i - tile0] += mk
        return res

    f = fence_all()
    for i in range(4):
        probs_free[i], probsT_free[i] = f, f
    catT_m = gated_cat_T(0, all4, 0, (a_tm, h_tm), {i: a_m[i] + hm_m[i] for i in all4}, (None, col("h_norm")))
    Hm = gate_and_out(["out00", "out01"], all4, 0, uT, catT_m, ctx_marks, None)
    dbg("h4", H[:, :, :], fence())

    f = fence_all()
    mod_m, gates_m = modulation(1, [1], f)
    load_row(0, "final_norm", f)
    um = modulated_norm([0, 1, 2, 3], Hm, mod_m, f)
    u_all = [x for i in range(4) for x in um[i]]
    g_out, base = carve(0, 2, 512)
    gkT, base = carve(base, 2, 512)
    gqT, base = carve(base, 2, S)
    gv_tm, base = carve(base, 4, 512)
    BT = []
    for _ in range(2):
        w_, base = carve(base, 2, 512)
        BT.append(w_)
    lg, lg_end = carve(base, 4, 2, 256)
    gaT = arena[0:2 * GLA_RANK + 1, lg_end:lg_end + 512]
    wgate = arena[0:2 * GLA_RANK + 1, lg_end + 512:lg_end + 1024]
    wgate_m = [load(AC, "wgate", wgate, ins["wgate"], f)]
    attG, base = carve(base, 2, 2, 2, P)
    attX, base = carve(base, 2, 2, 2, P)
    attC, base = carve(base, 2, 2, 2, S)
    lev = []
    for k in range(2):
        lev.append(xn[:, k, 0:512].rearrange("p (c s) -> p c s", c=2))
        for _ in range(2):
            w_, base = carve(base, 2, S)
            lev.append(w_)
    kept = []
    kept_q = []

    scale_q = copy_out(lambda ft: gqT[:, ft, :], GLA_DK ** -0.5)
    keep_k = copy_out(lambda ft: gkT[:, ft - 2, :])
    project(gemm, "gqk.0", (0, 1), lambda _: u_all,
            lambda ft, w, K, k: (S, [x[:, k, ft * P:(ft + 1) * P] for x in w], [x[:, K, S:2 * S] for x in uT]), scale_q, 1)
    project(gemm, "gqk.1", (2, 3), lambda _: u_all,
            lambda ft, w, K, k: (512, [x[:, k, (ft - 2) * P:(ft - 1) * P] for x in w], [x[:, K, :] for x in uT]), keep_k, 1)
    project_tm(gemm, "gv", uT, lambda i: um[i], all4, copy_out_v(lambda i: gv_tm[:, i, :]))
    gone = step(DV, [], v.memset, gaT[2 * GLA_RANK:2 * GLA_RANK + 1, :], 1.0)

    def ga_evac(_, ps, mk):
        ga_marks.append(step(DV, [mk], v.tensor_copy, gaT[0:32, :], ps[0:32, :]))
        return ga_marks

    ga_marks = []
    project(gemm, "ga", (0,), lambda _: u_all, lambda _, w, K, k: (512, [x[:, k, :] for x in w], [x[:, K, :] for x in uT]), ga_evac, 1)
    gaT_m = ga_marks[0]
    lg_m = {}
    for i in all4:
        b, ps, free = gemm.take()
        pm = products(free + [gaT_m, gone] + wgate_m, [(ps, gaT[:, i * P:(i + 1) * P], wgate)])
        lg_m[i] = log_sigmoid(ps, probs[:, i, :], lg[:, i, :, :].rearrange("p d c -> p (d c)"), [pm])
        give(b, [lg_m[i]])
    BT_m = []
    for d in range(2):
        for dt_ in range(2):
            b, ps, free = gemm.take()
            for r in range(2):
                o_ = ps[:, r * S:(r + 1) * S]
                full = sq[:, SQ["tri_u16" if d == 0 else "ones16b"] * P:][:, 0:2 * P]
                first, second = (2 * r, 2 * r + 1) if d == 0 else (2 * r + 1, 2 * r)
                tri = sqc("tri_u16" if d == 0 else "tri_l16")
                sub = o_[:, P:2 * P] if d == 0 else o_[:, 0:P]
                pm = products(free + [lg_m[2 * r], lg_m[2 * r + 1]],
                              [(o_, lg[:, first, d, dt_ * P:(dt_ + 1) * P], full), (sub, lg[:, second, d, dt_ * P:(dt_ + 1) * P], tri)])
            mk = step(AC if dt_ else DV, [pm], a.copy if dt_ else v.tensor_copy, BT[d][:, dt_, :], ps)
            give(b, [mk])
            BT_m.append(mk)
    dbg("BT", BT[0], BT_m)
    gla_in = kept + BT_m
    E_ctx, Kc = lev[0], [lev[1], lev[2]]
    Ql, Qc = lev[3], [lev[4], lev[5]]
    qc_m, kc_m = [], []
    e_prev = []
    for d in range(2):
        for dt_ in range(2):
            end = BT[d][:, dt_, S - 1:S] if d == 0 else BT[d][:, dt_, 0:1]
            e_prev.append(step(AC, gla_in + kc_m + qc_m, a.activation, E_ctx[:, dt_, :], BT[d][:, dt_, 0:S], ACT.Exp, scale=-1.0, bias=end))
        kc_m.append(step(DV, e_prev[-2:] + gla_in, v.tensor_tensor, Kc[d], gkT[:, :, 0:S], E_ctx, ALU.mult))
        m = step(AC, gla_in + qc_m, a.activation, Ql, BT[d][:, :, S:2 * S], ACT.Exp)
        qc_m.append(step(DV, [m], v.tensor_tensor, Qc[d], gqT, Ql, ALU.mult))
    attc_m = []
    for s_ in range(2):
        for par in range(2):
            b, ps, free = gemm.take()
            for c in range(2):
                pm = products(free + kc_m + qc_m, [(ps[:, c * S:(c + 1) * S], Kc[d][hp(par), c, s_ * P:(s_ + 1) * P], Qc[d][hp(par), c, :])
                                                  for d in range(2)])
            mk = step(AC, [pm], a.copy, attC[:, s_, par], ps.rearrange("p (c s) -> p c s", c=2))
            give(b, [mk])
            attc_m.append(mk)
    att_w = fence()
    for e in (DV, AC, GP):
        e.wait(att_w)
    prev = {}
    for par in range(2):
        b, ps, free = gemm.take()
        for tile in range(2):
            for c in range(2):
                at = (2 * tile + c) * P
                pm = products(free + kept, [(ps[:, at:at + P], gkT[hp(par), c, S + tile * P:S + (tile + 1) * P],
                                            gqT[hp(par), c, tile * P:(tile + 1) * P])])
        mk = step(AC, [pm] + BT_m, a.activation, attG[:, par].rearrange("p t c q -> p (t c q)"), ps, ACT.Copy, scale=2.0)
        give(b, [mk])
        prev[par] = mk
    zl = step(GP, [], g.memset, arena[:, base - 4 * 512:base], 0.0)
    lev_free = [[zl], [zl]]
    n_lev = 0
    lev_pool = Pool([0, 1, 2, 3, 6, 7])
    cross_m = []
    for hsize in GLA_LEVELS + [128]:
        nblk = 128 // hsize
        for d in range(2):
            k = n_lev % 2
            n_lev += 1
            E_, Q_, K_ = lev[3 * k:3 * k + 3]
            sp3 = lambda x_: x_.rearrange("p c (n two s) -> p c n two s", two=2, s=hsize)
            Bv = sp3(BT[d][:, :, S:2 * S])
            Ev, Qv, Kv, qv, kv = sp3(E_), sp3(Q_), sp3(K_), sp3(gqT), sp3(gkT[:, :, S:2 * S])
            th, sh = (1, 0) if d == 0 else (0, 1)
            seam = (Bv[:, :, :, 0, hsize - 1] if d == 0 else Bv[:, :, :, 1, 0]).unsqueeze(3).to_broadcast([P, 2, nblk, hsize])
            m1 = step(GP, lev_free[k], g.tensor_tensor, Ev[:, :, :, th, :], Bv[:, :, :, th, :], seam, ALU.subtract)
            m2 = step(GP, lev_free[k], g.tensor_tensor, Ev[:, :, :, sh, :], seam, Bv[:, :, :, sh, :], ALU.subtract)
            m3 = step(AC, [m1, m2], a.activation, E_, E_, ACT.Exp)
            m4 = step(DV, [m3] + lev_free[k], v.tensor_tensor, Qv[:, :, :, th, :], qv[:, :, :, th, :], Ev[:, :, :, th, :], ALU.mult)
            m5 = step(GP, [m3], g.tensor_tensor, Kv[:, :, :, sh, :], kv[:, :, :, sh, :], Ev[:, :, :, sh, :], ALU.mult)
            for par in range(2):
                b, ps, free = lev_pool.take()
                for tile in range(2 if hsize < 128 else 1):
                    s0, t0 = (tile * P, tile * P) if hsize < 128 else (sh * P, th * P)
                    for c in range(2):
                        at = (2 * tile + c) * P
                        pm = products(free + [m4, m5], [(ps[:, at:at + P], K_[hp(par), c, s0:s0 + P], Q_[hp(par), c, t0:t0 + P])])
                if hsize < 128:
                    mi = 7 * d + GLA_LEVELS.index(hsize)
                    mask = gla_mask[:, mi * P:(mi + 1) * P].unsqueeze(1).to_broadcast([P, 4, P])
                    mk = step(DV, [pm, prev[par]] + misc_m, v.copy_predicated, attG[:, par].rearrange("p t c q -> p (t c) q"), mask,
                              ps.rearrange("p (h q) -> p h q", h=4))
                    prev[par] = mk
                else:
                    mk = step(DV, [pm], v.tensor_copy, attX[:, sh, par], ps[:, 0:2 * P].rearrange("p (c q) -> p c q", c=2))
                    cross_m.append(mk)
                give(b, [mk])
            lev_free[k] = [pm]
    att_m = attc_m + cross_m + [prev[0], prev[1]]
    g_m = {}
    for i in range(2):
        b, ps, free = gemm.take()
        for h in range(4):
            par, c = h % 2, h // 2
            keys = [(attC[:, s_, par, c, i * P:(i + 1) * P], s_) for s_ in range(2)]
            keys += [(attG[:, par, i, c, :], 2 + i), (attX[:, 1 - i, par, c, :], 3 - i)]
            terms = [(ps[:, h * P:(h + 1) * P], att, gv_tm[:, s_, h * P:(h + 1) * P]) for att, s_ in keys]
            pm = products(free + att_m + kept, terms)
        mk = step(DV, [pm], v.tensor_copy, g_out[:, i, :], ps)
        give(b, [mk])
        g_m[i] = [mk]
    for i in range(2):
        g_m[i] = head_norm(g_out[:, i, :], 4, 128, g_m[i], probs[:, i, :], (DV, v))
    dbg("gla", g_out, g_m[0] + g_m[1])

    f = fence_all()
    for i in range(4):
        probs_free[i], probsT_free[i] = f, f
    na_out, base = carve(2 * 512, 2, 512)
    nqT, base = carve(base, 4, S)
    nkT, base = carve(base, 4, 512)
    nv, base = carve(base, 4, 512)
    nab, base = carve(base, 2, 8, S)
    nab_m = [load(AC, "na_bias", nab, ins["na_bias"], f)]
    kept = []
    project_fm(gemm, "nq", uT, u_all, S, S, range(4), copy_out(lambda ft: nqT[:, ft, :], -NA_D ** -0.5))
    project_fm(gemm, "nk", uT, u_all, 0, 512, range(4), copy_out_v(lambda ft: nkT[:, ft, :]))
    project_tm(gemm, "nv", uT, lambda i: um[i], all4, copy_out_v(lambda i: nv[:, i, :]))
    bias_marks = nab_m
    n_m = {0: [], 1: []}
    attention([0, 1], 8, lambda h, qt: nqT[hp(h % 2), h // 2, qt * P:(qt + 1) * P], lambda h, n: nkT[hp(h % 2), h // 2, 0:n],
              lambda qt: 512, lambda h, j: nv[:, j, pair_of(h)], kept,
              finish_to(lambda qt: na_out[:, qt, :], lambda qt: n_m[qt]), bias=lambda h, qt: nab[:, qt, h, :], b0=S, nbias=S)
    dbg("na", na_out, n_m[0] + n_m[1])
    f = fence_all()
    catT_m = gated_cat_T(1, [2, 3], 2, (g_out, na_out), {i: g_m[i] + n_m[i] for i in range(2)},
                         (col("gla_norm"), None))
    Hm = gate_and_out(["out10", "out11"], [0, 1], 2, uT, catT_m, Hm, None)

    f = fence_all()
    r, rm, _ = rstd_of([H[:, i, :] for i in lat], D, [Hm[2], Hm[3]])
    outs = []
    for i in range(2):
        mk = step(DV, [rm] + row_m["final_norm"], v.scalar_tensor_tensor, xn[:, i, :], H[:, 2 + i, :], r[:, i:i + 1],
                  rowbuf[:, 0, :], ALU.mult, ALU.mult)
        outs.append(load(SP, f"out{i}", out[i * P:(i + 1) * P, :], xn[:, i, :], [mk]))
    SP.wait(outs + list(loads.values()))


def _t5_bucket(rel):
    half = NUM_BUCKETS // 2
    max_exact = half // 2
    sign = np.where(rel > 0, half, 0)
    n = np.abs(rel)
    nf = np.maximum(n, 1).astype(np.float32)
    large = max_exact + (np.log(nf / np.float32(max_exact)) / np.float32(math.log(MAX_DISTANCE / max_exact))
                         * np.float32(half - max_exact)).astype(np.int32)
    large = np.minimum(large, half - 1)
    return sign + np.where(n < max_exact, n, large)


def _constants():
    i = np.arange(P)
    s, t_ = i[:, None], i[None, :]
    f = lambda c: np.where(c, 1.0, 0.0).astype(np.float32)
    tri_u, tri_l = f(s <= t_), f(s >= t_)
    one = np.ones((P, P), np.float32)
    parts = {"ident": f(s == t_), "ones": one, "tri_u": tri_u, "tri_l": tri_l, "tri_u16": tri_u / 16, "ones16b": one / 16, "tri_l16": tri_l / 16, "neg_u": np.where(s <= t_, 0, NEG), "neg_l": np.where(s >= t_, 0, NEG)}
    sq = np.concatenate([parts[n] for n in SQ], 1).astype(np.float32)
    rel = np.arange(384)[None, :] - 128 - np.arange(P)[:, None]
    count = sum(((rel % dil == 0) & (np.abs(rel) <= dil * (window // (2 * dil)))).astype(np.int64) for window, dil in DILATED)
    lnc = np.where(count > 0, -np.log(np.maximum(count, 1)), 0.0).astype(np.float32)
    selneg = np.zeros((4, 4, P), np.float32)
    sel4 = np.zeros((4, 2, P), np.float32)
    for h in range(4):
        selneg[h, h] = -1.0
    for r in range(2):
        sel4[r, r] = sel4[r + 2, r] = 1.0
    masks = []
    for d in range(2):
        for hs in GLA_LEVELS:
            same = (s // (2 * hs)) == (t_ // (2 * hs))
            sh, th = (s // hs) % 2, (t_ // hs) % 2
            masks.append(same & ((sh == 0) & (th == 1) if d == 0 else (sh == 1) & (th == 0)))
    tt = np.arange(S)
    inv = 1.0 / (np.float32(10000.0) ** (np.arange(PAIRS, dtype=np.float32) / PAIRS))
    ang = np.concatenate([(tt // GRID_W)[:, None] * inv, (tt % GRID_W)[:, None] * inv], -1)
    cs = np.stack([np.cos(ang), np.sin(ang)], 1).astype(np.float32)
    rope = np.ascontiguousarray(cs.reshape(2, P, 2, 16).transpose(1, 0, 2, 3))
    return {"sq": sq, "lnc": lnc, "selneg": selneg.reshape(4, 4 * P), "sel4": sel4.reshape(4, 2 * P),
            "gla_mask": np.concatenate(masks, 1).astype(np.float32), "rope": rope}, rel, count


def _layout(i):
    c, rel, count = _constants()
    w = lambda n: np.ascontiguousarray(i[n][0] if i[n].ndim == 3 else i[n])
    dev = dict(c)
    for n in ("w_in", "w_o", "w_up", "w_down", "w_ple_proj", "w_ple_gate"):
        dev[n] = w(n)
    qa = dev["w_in"][:, :WA].reshape(D, NKVA, NHA // NKVA, HD).transpose(0, 2, 1, 3).reshape(D, WA)
    dev["w_in"] = np.concatenate([qa, dev["w_in"][:, WA:]], 1)
    for n in ("l0_w_mod", "l0_w_in", "l0_w_out", "l1_w_mod", "l1_w_in", "l1_w_out"):
        dev[n] = w(n + "_2")
    dev["w_uq"], dev["w_ukv"] = w("l0_mla_w_uq_2"), w("l0_mla_w_ukv_2")
    dev["x"], dev["ctx"] = i["x"][0], i["ctx_2"][0]
    dev["pT"] = np.ascontiguousarray(i["p"][0, 0].T)

    def columns(vec):
        return np.asarray(vec).reshape(-1, P).T

    conv_w = np.concatenate([columns(i["l0_mlstm_conv_w_2"][j]) for j in range(3)], 1)
    cc = np.stack([columns(i["c_ctx_2"]), columns(i["c_2"][0])], 2).reshape(P, 16)
    vecs = {"g_pre_mix": i["g_pre_mix"], "g_out_a": i["g_out_a"], "g_out_b": i["g_out_b"], "g_pre_mlp": i["g_pre_mlp"],
            "l0_norm": i["l0_norm_2"], "l1_norm": i["l1_norm_2"], "l0_b_mod": i["l0_b_mod_2"], "l1_b_mod": i["l1_b_mod_2"],
            "q_norm": i["l0_mla_q_norm_2"], "kv_norm": i["l0_mla_kv_norm_2"], "h_norm": i["l0_mlstm_norm_2"],
            "gla_norm": i["l1_gla_norm_2"], "conv_b": i["l0_mlstm_conv_b_2"]}
    dev["cols"] = np.concatenate([columns(vecs[n]) if n in vecs else (conv_w if n == "conv_w" else cc) for n in COLS], 1)
    dev["rows"] = np.stack([i["g_post_mix"][0], i["g_post_mlp"][0], i["b_ple_gate"][0], i["g_post_ple"][0],
                            i["l0_b_mod_2"][2 * D:], i["l1_b_mod_2"][2 * D:], i["final_norm_2"]])
    gates = np.stack([i["l0_mlstm_b_i_2"], i["l0_mlstm_b_f_2"]], 1).reshape(-1)
    dev["small_rows"] = np.concatenate([i["sink_a"][0], gates])
    table = i["rel_bias_table"]
    bias = table[_t5_bucket(rel)].transpose(0, 2, 1).copy()
    keep = np.zeros(bias.shape, bool)
    keep[:, 0:8] = (np.abs(rel) <= WINDOW_A)[:, None]
    keep[:, 8:16] = (count > 0)[:, None]
    bias[~keep] = NEG
    dev["bias_t5"] = bias
    wg = np.zeros((2 * GLA_RANK + 1, 512), np.float32)
    for d in range(2):
        wg[d * GLA_RANK:(d + 1) * GLA_RANK, d * 256:(d + 1) * 256] = i["l1_gla_w_gate_2"][d]
        wg[2 * GLA_RANK, d * 256:(d + 1) * 256] = i["l1_gla_b_gate_2"][d]
    dev["wgate"] = wg
    tok = np.arange(S)
    r, cc_ = tok // GRID_W, tok % GRID_W
    kh = min(NA_KH, ROWS)
    r0 = np.clip(r - kh // 2, 0, ROWS - kh)
    c0 = np.clip(cc_ - NA_KW // 2, 0, GRID_W - NA_KW)
    inside = ((r[None, :] >= r0[:, None]) & (r[None, :] < r0[:, None] + kh)
              & (cc_[None, :] >= c0[:, None]) & (cc_[None, :] < c0[:, None] + NA_KW))
    dr = np.where(inside, r[None, :] - r[:, None] + NA_KH - 1, 0)
    dc = np.where(inside, cc_[None, :] - cc_[:, None] + NA_KW - 1, 0)
    nb = i["l1_na_rpb_2"][:, dr, dc].copy()
    nb[:, ~inside] = NEG
    dev["na_bias"] = np.ascontiguousarray(nb.reshape(NA_H, 2, P, S).transpose(2, 1, 0, 3))
    return {n: np.ascontiguousarray(x_) for n, x_ in dev.items()}


def kernel(**inputs):
    import concourse.bacc as bacc
    from concourse.bass_utils import run_bass_kernel_spmd

    dev = _layout({n: np.asarray(x_) for n, x_ in inputs.items()})
    nc = bacc.Bacc("TRN2", target_bir_lowering=False, num_devices=1)
    aps = {n: nc.dram_tensor("in_" + n, x_.shape, mybir.dt.from_np(x_.dtype), kind="ExternalInput").ap() for n, x_ in dev.items()}
    out = nc.dram_tensor("out_h", (S, D), F32, kind="ExternalOutput").ap()
    build(nc, aps, out)
    r = run_bass_kernel_spmd(nc, [{"in_" + n: x_ for n, x_ in dev.items()}], core_ids=[0])
    return r.results[0]["out_h"].reshape(1, S, D)
```

```python
import math
from contextlib import ExitStack

import numpy as np
import concourse.bass as bass
from concourse import mybir

ALU = mybir.AluOpType
ACT = mybir.ActivationFunctionType
F32 = mybir.dt.float32
F32R = mybir.dt.float32r
U8 = mybir.dt.uint8
AX_X = mybir.AxisListType.X

P = 128
D = 1024
KT = D // P
S = 256
EPS = 1e-6
NEG = -1e30
BANK = 512

HD = 64
NHA, NKVA, NHB = 8, 2, 8
WINDOW_A = 128
DILATED = ((128, 1), (512, 4), (2048, 16))
WA, KVA, WB = NHA * HD, NKVA * HD, NHB * HD
D_FF = 4 * D
PLE = 256
NUM_BUCKETS, MAX_DISTANCE = 32, 1024

GRID_W = 64
ROWS = S // GRID_W
MLA_H, Q_RANK, KV_RANK, NOPE, ROPE, MLA_V = 8, 384, 256, 64, 32, 64
QK = NOPE + ROPE
PAIRS = ROPE // 4
ML_H, ML_D = 4, 128
GLA_H, GLA_DK, GLA_DV, GLA_RANK, GLA_TAU = 4, 64, 128, 16, 16.0
NA_H, NA_D, NA_KH, NA_KW = 8, 64, 8, 16
E_SIZES = (Q_RANK, KV_RANK, ROPE, 512, 512, 512, 512, 4 * ML_H, 1024)
O_SIZES = (256, 256, 512, 2 * GLA_RANK, 512, 512, 512, 1024)
E_OFF = [sum(E_SIZES[:i]) for i in range(len(E_SIZES) + 1)]
O_OFF = [sum(O_SIZES[:i]) for i in range(len(O_SIZES) + 1)]
GLA_LEVELS = [1 << i for i in range(7)]

COLS = {}
_n = 0
for _name, _w in (("g_pre_mix", 8), ("g_out_a", 4), ("g_out_b", 4), ("g_pre_mlp", 8), ("l0_norm", 8),
                  ("l1_norm", 8), ("l0_b_mod", 24), ("l1_b_mod", 24), ("q_norm", 3), ("kv_norm", 2),
                  ("h_norm", 4), ("gla_norm", 4), ("conv_b", 8), ("conv_w", 24), ("c", 16)):
    COLS[_name] = (_n, _w)
    _n += _w
NCOLS = _n
ROWS_ORDER = ("g_post_mix", "g_post_mlp", "b_ple_gate", "g_post_ple", "l0_b_gate", "l1_b_gate", "final_norm")
SQ = {n: i for i, n in enumerate(("ident", "ones", "tri_u", "tri_l", "tri_u16", "ones16b", "tri_l16", "neg_u", "neg_l"))}


class Engine:

    def __init__(self, e, sem):
        self.e, self.sem, self.count, self.seen = e, sem, 0, {}

    def wait(self, marks):
        for sem, value in marks:
            if self.seen.get(id(sem), 0) < value:
                self.e.wait_ge(sem, value)
                self.seen[id(sem)] = value

    def last(self):
        return [(self.sem, self.count)] if self.count else []


def step(eng, after, method, *args, **kw):
    eng.wait(after)
    method(*args, **kw).then_inc(eng.sem, 1)
    eng.count += 1
    return (eng.sem, eng.count)


def build(nc, ins, out, dump=None):
    ctx = ExitStack()
    with ctx:
        _build(nc, ctx, ins, out, dump)


def _build(nc, ctx, ins, out, dump):
    def sb(name, shape, dt=F32):
        return ctx.enter_context(nc.sbuf_tensor(name, shape, dt))

    def new_sem(name):
        return ctx.enter_context(nc.semaphore(name))

    PE = Engine(nc.tensor, new_sem("pe_done"))
    DV = Engine(nc.vector, new_sem("dve_done"))
    AC = Engine(nc.scalar, new_sem("act_done"))
    GP = Engine(nc.gpsimd, new_sem("pool_done"))
    SP = Engine(nc.sync, new_sem("sp_done"))
    COMPUTE = (PE, DV, AC, GP)
    v, a, g, t = nc.vector, nc.scalar, nc.gpsimd, nc.tensor

    sq = sb("sq", [P, len(SQ) * P])
    cols = sb("cols", [P, NCOLS])
    sel2 = sb("sel2", [2, 2 * P])
    gla_mask = sb("gla_mask", [P, 14 * P], U8)
    rope = sb("rope", [P, 2, 2, 2 * PAIRS])
    small_rows = sb("small_rows", [P, 8 + 16])
    H = sb("H", [P, 4, D])
    uT = (sb("uT_hi", [P, KT, 512], F32R), sb("uT_lo", [P, KT, 512], F32R))
    CH = 2048
    wraw = sb("wraw", [P, 2, CH])
    landing = [wraw[:, 0, :], wraw[:, 1, :], H[:, 0:2, :].rearrange("p a b -> p (a b)")]
    w_hi, w_lo = sb("w_hi", [P, 2, CH], F32R), sb("w_lo", [P, 2, CH], F32R)
    presplit = sb("presplit", [P, 2, 512])
    rowbuf = sb("rowbuf", [P, 2, D])
    probs = sb("probs", [P, 4, 512])
    probsT = sb("probsT", [P, 4, 512])
    xn = sb("xn", [P, 2, D])
    rtmp = sb("rtmp", [P, 4, 128])
    stats = sb("stats", [P, 900])
    ARENA = 13000
    arena = sb("arena", [P, ARENA])
    banks = ctx.enter_context(nc.psum_tensor("banks", [P, 8, BANK], F32))

    def sqc(name):
        i = SQ[name]
        return sq[:, i * P:(i + 1) * P]

    ident = sqc("ident")

    def col(name, j0=0, n=None):
        c0, w = COLS[name]
        return cols[:, c0 + j0:c0 + (w if n is None else j0 + n)]

    stat_at = [0]

    def stat(n=1):
        stat_at[0] += n
        assert stat_at[0] <= 900, stat_at
        return stats[:, stat_at[0] - n:stat_at[0]]

    def carve(base, *shape):
        n = int(np.prod(shape))
        assert base + n <= ARENA, (base, n)
        view = arena[:, base:base + n]
        if len(shape) == 2:
            view = view.rearrange("p (a b) -> p a b", a=shape[0])
        elif len(shape) == 3:
            view = view.rearrange("p (a b c) -> p a b c", a=shape[0], b=shape[1])
        elif len(shape) == 4:
            view = view.rearrange("p (a b c d) -> p a b c d", a=shape[0], b=shape[1], c=shape[2])
        return view, base + n

    def bc(ap, n):
        return ap.unsqueeze(len(ap.shape)).to_broadcast(list(ap.shape) + [n])

    bank_free = [[] for _ in range(8)]

    class Pool:

        def __init__(self, which):
            self.which, self.n = list(which), 0

        def take(self):
            b = self.which[self.n % len(self.which)]
            self.n += 1
            free = bank_free[b]
            assert free is not None, b
            bank_free[b] = None
            return b, banks[:, b, :], free

    def give(b, marks):
        bank_free[b] = list(marks)

    loads = {}
    def load(eng, name, dst, src, after=(), sem=None):
        eng.wait(after)
        s_ = sem or new_sem("ld_" + name)
        eng.e.dma_start(dst, src).then_inc(s_, 16)
        loads[name] = (s_, 16)
        return (s_, 16)

    def kview(w, k0, k1, c0, c1):
        return w[k0 * P:k1 * P, c0:c1].rearrange("(k p) n -> p k n", p=P)

    chunks = []

    def chunk(name, *parts):
        chunks.append((name, parts))

    def chunk_tm(name, w, c0, c1, extra=None):
        for k in range(2):
            parts = [(w, 4 * k, 4 * k + 4, c0, c1)]
            if extra:
                parts.append((w, 4 * k, 4 * k + 4) + extra)
            chunk(f"{name}.{k}", *parts)

    def chunk_fm(name, w, c0, c1):
        for k in range((c1 - c0 + 255) // 256):
            chunk(f"{name}.{k}", (w, 0, 8, c0 + 256 * k, min(c1, c0 + 256 * k + 256)))

    n_mod = [0]
    MODS = [(layer, c) for layer in range(2) for c in range(6)]

    def chunk_mods(n):
        for _ in range(n):
            layer, c = MODS[n_mod[0] // 2]
            k = n_mod[0] % 2
            chunk(f"mod{n_mod[0]}", (f"l{layer}_w_mod", 4 * k, 4 * k + 4, 512 * c, 512 * c + 512))
            n_mod[0] += 1

    FILL = {"o": 2, "mix": 4, "mlp": 2, "ple": 4, "um": 4, "latent": 2, "gem": 2, "cat": 4, "end": 0}
    chunk_fm("qa", "w_in", 0, 512)
    chunk("kva", ("w_in", 0, 8, 512, 768))
    chunk_fm("qb", "w_in", 768, 1280)
    chunk_fm("kb", "w_in", 1280, 1792)
    chunk_tm("vb", "w_in", 1792, 2304)
    for c in range(2):
        chunk_tm(f"wo{c}", "w_o", c * 512, c * 512 + 512)
        if c == 0:
            chunk_mods(FILL["o"])
    for c in range(8):
        chunk_fm(f"up{c}", "w_up", c * 512, c * 512 + 512)
        if c == 0:
            chunk_mods(FILL["mix"])
        if c:
            for h in range(2):
                chunk(f"down{c - 1}{h}", ("w_down", 4 * c - 4, 4 * c, h * 512, h * 512 + 512))
    for h in range(2):
        chunk(f"down7{h}", ("w_down", 28, 32, h * 512, h * 512 + 512))
    chunk("ple", ("w_ple_proj", 0, 2, 0, 1024))
    for c in range(2):
        chunk_tm(f"pg{c}", "w_ple_gate", c * 512, c * 512 + 512)
        if c == 0:
            chunk_mods(FILL["mlp"])
    eo = E_OFF
    chunk_tm("cq", "l0_w_in", eo[0], eo[1])
    chunk_mods(FILL["ple"] + FILL["um"])
    chunk_tm("ckv", "l0_w_in", eo[1], eo[3], (eo[7], eo[8]))
    chunk_mods(FILL["latent"])
    chunk("uq0", ("w_uq", 0, 3, 0, 512))
    chunk("uq1", ("w_uq", 0, 3, 512, 768))
    chunk("ukv", ("w_ukv", 0, 2, 0, 1024))
    chunk_fm("mq", "l0_w_in", eo[3], eo[4])
    chunk_fm("mk", "l0_w_in", eo[4], eo[5])
    chunk_tm("mv", "l0_w_in", eo[5], eo[6])
    chunk_tm("mo", "l0_w_in", eo[6], eo[7])
    chunk_mods(FILL["gem"])
    for c in range(2):
        chunk_tm(f"z0{c}", "l0_w_in", eo[8] + 512 * c, eo[8] + 512 * c + 512)
    for c in range(2):
        chunk_tm(f"out0{c}", "l0_w_out", c * 512, c * 512 + 512)
        if c == 0:
            chunk_mods(FILL["cat"])
    oo = O_OFF
    chunk_fm("gqk", "l1_w_in", 0, 512)
    chunk_mods(FILL["end"])
    chunk_tm("gv", "l1_w_in", oo[2], oo[3])
    chunk("ga", ("l1_w_in", 0, 8, oo[3], oo[3] + P))
    chunk_fm("nq", "l1_w_in", oo[4], oo[5])
    chunk_fm("nk", "l1_w_in", oo[5], oo[6])
    chunk_tm("nv", "l1_w_in", oo[6], oo[7])
    for c in range(2):
        chunk_tm(f"z1{c}", "l1_w_in", oo[7] + 512 * c, oo[7] + 512 * c + 512)
    for c in range(2):
        chunk_tm(f"out1{c}", "l1_w_out", c * 512, c * 512 + 512)
    PLAIN = {"uq0", "uq1", "ukv"} | {f"mod{i}" for i in range(24)}
    pair_slot = {}
    for i, (name, _) in enumerate(chunks):
        if name not in PLAIN:
            pair_slot[i] = len(pair_slot) % 2

    in_first_block = [i for i, (name, _) in enumerate(chunks) if name == "pg1.1"][0] + 1
    raw_sem = [new_sem(f"weights_in_slot{i}") for i in range(3)]
    raw_count = [0] * 3
    raw_slot = {}
    landed = {}
    split_done = {}
    pair_free = [[], []]
    next_split = [0]

    def chunk_view(buf, i):
        parts = chunks[i][1]
        kt = parts[0][2] - parts[0][1]
        n = sum(p[4] - p[3] for p in parts)
        return buf[:, 0:kt * n].rearrange("p (k n) -> p k n", k=kt)

    def load_next(k, after):
        i = len(raw_slot)
        if i >= len(chunks) or (k == 2 and i >= in_first_block):
            return
        raw_slot[i] = k
        SP.wait(after)
        view, at = chunk_view(landing[k], i), 0
        for name, k0, k1, c0, c1 in chunks[i][1]:
            SP.e.dma_start(view[:, :, at:at + c1 - c0], kview(ins[name], k0, k1, c0, c1)).then_inc(raw_sem[k], 16)
            raw_count[k] += 16
            at += c1 - c0
        landed[i] = loads[f"slot{k}"] = (raw_sem[k], raw_count[k])

    def split_ready():
        while next_split[0] in raw_slot or (next_split[0] < len(chunks) and next_split[0] not in pair_slot):
            i = next_split[0]
            if i in pair_slot:
                k = pair_slot[i]
                if pair_free[k] is None:
                    return
                raw, hi, lo = (chunk_view(x, i) for x in (landing[raw_slot[i]], w_hi[:, k, :], w_lo[:, k, :]))
                m1 = step(AC, [landed[i]] + pair_free[k], a.copy, hi, raw)
                m2 = step(DV, [m1] + pair_free[k], v.tensor_tensor, lo, raw, hi.bitcast(F32), ALU.subtract)
                split_done[i] = [m1, m2]
                pair_free[k] = None
                load_next(raw_slot[i], [m1, m2])
            next_split[0] += 1

    number = {name: i for i, (name, _) in enumerate(chunks)}

    def weights(name):
        i = number[name]
        if name in PLAIN:
            return chunk_view(landing[raw_slot[i]], i), [landed[i]], i
        return [chunk_view(x[:, pair_slot[i], :], i) for x in (w_hi, w_lo)], split_done[i], i

    def used(i, mark, later=False):
        if i in pair_slot:
            pair_free[pair_slot[i]] = [mark]
        else:
            load_next(raw_slot[i], [mark])
        if not later:
            split_ready()

    def products(after, terms):
        PE.wait(after)
        for i, (o, l, r) in enumerate(terms):
            m = t.matmul(o, l, r, start=(i == 0), stop=(i == len(terms) - 1))
        m.then_inc(PE.sem, 1)
        PE.count += 1
        return (PE.sem, PE.count)

    HALVES = ((0, 0), (0, 1), (1, 0))

    def project(pool, name, items, marks, operands, evac, kparts):
        flush_mods()
        taken = {}
        for kc in range(kparts):
            w, wm, i = weights(name if kparts == 1 else f"{name}.{kc}")
            kn = w[0].shape[1]
            for it in items:
                if kc == 0:
                    taken[it] = pool.take()
                b, ps, free = taken[it]
                PE.wait(wm + (list(free) + list(marks(it)) if kc == 0 else []))
                for k in range(kn):
                    o, l, r = operands(it, w, kc * kn + k, k)
                    for j, (x, y) in enumerate(HALVES):
                        m = t.matmul(ps[:, 0:o], l[x], r[y], start=(kc + k + j == 0), stop=(kc == kparts - 1 and k == kn - 1 and j == 2))
                m.then_inc(PE.sem, 1)
                PE.count += 1
                m = (PE.sem, PE.count)
                if kc == kparts - 1:
                    give(b, evac(it, ps, m))
            used(i, m)

    def project_tm(pool, name, src, marks, tiles, evac, n=512, kparts=2):
        def operands(tile, w, K, k):
            return n, [x[:, K, tile * P:(tile + 1) * P] for x in src], [x[:, k, 0:n] for x in w]
        project(pool, name, tiles, marks, operands, evac, kparts)

    def project_fm(pool, name, src, marks, t0, nt, fts, evac):
        for c in range(0, len(fts), 2):
            def operands(ft, w, K, k, c=c):
                return nt, [x[:, k, (ft - fts[c]) * P:(ft - fts[c] + 1) * P] for x in w], [x[:, K, t0:t0 + nt] for x in src]
            project(pool, f"{name}.{c // 2}", fts[c:c + 2], lambda ft: marks, operands, evac, 1)

    junk_mark = [[]]

    def rstd_of(srcs, width, after, junk=None):
        n = len(srcs)
        ss, r = stat(n), stat(n)
        ms = []
        for i, s_ in enumerate(srcs):
            j = junk if junk is not None else probs[:, 0:2, :].rearrange("p a b -> p (a b)")
            m = step(AC, list(after[i]) + (junk_mark[0] if junk is None else ms[-1:]), a.activation, j[:, 0:width], s_, ACT.Square,
                     accum_out=ss[:, i:i + 1])
            if junk is None:
                junk_mark[0] = [m]
            ms.append(m)
        m = step(GP, ms, g.tensor_scalar, ss, ss, 1.0 / width, EPS, ALU.mult, ALU.add)
        m = step(GP, [m], g.tensor_tensor, r, ss, minus_half[:, 0:1].to_broadcast([P, n]), ALU.pow)
        return r, m, ms

    xn_free = [[], []]
    xn_n = [0]

    pre_free = [[], []]
    pre_n = [0]

    def split(x, hi, lo, after, free):
        m1 = step(AC, list(after) + list(free), a.copy, hi, x)
        m2 = step(DV, [m1] + list(free), v.tensor_tensor, lo, x, hi.bitcast(F32), ALU.subtract)
        return [m1, m2]

    pending_lo = []

    def flush_lo():
        while pending_lo:
            late, marks, lo, x, hi, after = pending_lo.pop()
            m = step(DV, after, v.tensor_tensor, lo, x, hi.bitcast(F32), ALU.subtract)
            late.append(m)
            marks.append(m)

    def into_T(pool, src, width, dst, tok, after, gain=None, shift=None, dst_free=(), hold=False):
        marks, reads = [], []
        nj = width // P
        for j0 in range(0, nj, 4):
            nb = min(4, nj - j0)
            b, ps, free = pool.take()
            PE.wait(free + list(after))
            for j in range(nb):
                m = t.transpose(ps[:, j * P:(j + 1) * P], src[:, (j0 + j) * P:(j0 + j + 1) * P], ident)
            m.then_inc(PE.sem, 1)
            PE.count += 1
            m = (PE.sem, PE.count)
            reads = [m]
            psv = ps[:, 0:nb * P].rearrange("p (j q) -> p j q", j=nb)
            pair = isinstance(dst, tuple)
            if pair:
                k = pre_n[0] % 2
                pre_n[0] += 1
                d = presplit[:, k, 0:nb * P].rearrange("p (j q) -> p j q", j=nb)
                free = pre_free[k]
            else:
                d, free = dst[:, j0:j0 + nb, tok:tok + P], list(dst_free)
            if shift is not None:
                for j in range(nb):
                    g_, s_ = gain[:, j0 + j:j0 + j + 1], shift[:, j0 + j:j0 + j + 1]
                    if j0:
                        m2 = step(AC, [m] + free, a.activation, d[:, j, :], psv[:, j, :], ACT.Identity, scale=g_, bias=s_)
                    else:
                        m2 = step(DV, [m] + free, v.tensor_scalar, d[:, j, :], psv[:, j, :], g_, s_, ALU.mult, ALU.add)
            elif gain is None:
                m2 = step(DV, [m] + free, v.tensor_copy, d, psv)
            else:
                m2 = step(DV, [m] + free, v.tensor_tensor, d, psv, bc(gain[:, j0:j0 + nb], P), ALU.mult)
            give(b, [m2])
            flush_lo()
            if pair:
                hi, lo = (x[:, j0:j0 + nb, tok:tok + P] for x in dst)
                m3 = step(AC, [m2] + list(dst_free), a.copy, hi, d)
                marks.append(m3)
                late = [m3]
                pre_free[k] = late
                pending_lo.append((late, marks, lo, d, hi, [m3] + list(dst_free)))
            else:
                marks.append(m2)
        if not hold:
            flush_lo()
        return marks, reads

    def norm_into_T(pool, srcs, width, dst, toks, after, gain=None, shift=None, dst_free=(), defer=False, junk=None):
        r, rm, _ = rstd_of(srcs, width, after, junk)

        def rest():
            return norm_rest(pool, srcs, width, dst, toks, after, gain, shift, dst_free, r, rm)

        return rest if defer else rest()

    def norm_rest(pool, srcs, width, dst, toks, after, gain, shift, dst_free, r, rm):
        marks, scaled = {}, {}

        def scale(i):
            k = xn_n[0] % 2
            xn_n[0] += 1
            x_ = xn[:, k, 0:width]
            ready = [rm] + list(after[i]) + xn_free[k]
            if i % 2:
                m = step(GP, ready, g.tensor_scalar, x_, srcs[i], r[:, i:i + 1], None, ALU.mult)
            else:
                m = step(AC, ready, a.activation, x_, srcs[i], ACT.Copy, scale=r[:, i:i + 1])
            scaled[i] = (k, x_, m)

        scale(0)
        for i in range(len(srcs)):
            if i + 1 < len(srcs):
                scale(i + 1)
            k, x_, m = scaled[i]
            marks[i], xn_free[k] = into_T(pool, x_, width, dst, toks[i], [m], gain(i) if gain else None,
                                          shift(i) if shift else None, dst_free, True)
        flush_lo()
        return marks

    def fence():
        return [m for e in COMPUTE for m in e.last()]

    def fence_all():
        f = fence()
        for e in (DV, AC, GP):
            e.wait(f)
        return f

    def dbg(name, ap, after):
        if dump is not None and name in dump:
            AC.wait(after)
            dump[name](a, ap, new_sem("dump_" + name), loads)

    x_m = [load(AC, "x", H[:, 2:4, :], ins["x"].rearrange("(t p) d -> p t d", p=P))]
    cols_m = [load(SP, "cols", cols[:, :], ins["cols"])]
    sq_m = [load(SP, "sq", sq[:, :], ins["sq"])]
    bias_t5, _ = carve(0, 16, 384)
    lnc = probsT[:, 0, 0:384]
    for i in range(3):
        load_next(i, x_m)
    row_m = {}

    def load_row(slot, name, after=()):
        i = ROWS_ORDER.index(name)
        row_m[name] = [load(GP, name, rowbuf[:, slot, :], ins["rows"][i, :].partition_broadcast(P), after)]
        return rowbuf[:, slot, :]

    minus_half = sb("minus_half", [P, 1])
    GP.wait([step(DV, [], v.memset, minus_half[:, :], -0.5)])
    eps_col = sb("eps_col", [P, 1])
    eps_m = step(DV, [], v.memset, eps_col[:, :], EPS)
    AC.wait([eps_m])
    one_col = sb("one_col", [P, 1])
    one_m = step(DV, [], v.memset, one_col[:, :], 1.0)
    AC.wait([one_m])

    gemm = Pool([0, 1, 2, 7])
    mod_pool = Pool([3, 6])
    turn = Pool([4, 5])
    outp = Pool([6, 7])
    up_pool = Pool([4, 5, 6, 7])

    csilu = sb("csilu", [P, KT, 2])
    modrow = sb("modrow", [2, 512])
    mod_dram = [nc.dram_tensor(f"mod_rows{i}", (2, 3 * D), F32).ap() for i in range(2)]
    mod_at = [0]
    mod_bank = [None]
    mod_stored = {0: [], 1: []}
    modrow_free = [[]]

    mod_pending = []

    def fill(n):
        if n:
            flush_mods()
        for _ in range(n):
            at = mod_at[0]
            mod_at[0] += 1
            layer, c = MODS[at // 2]
            k0 = 4 * (at % 2)
            w, wm, wi = weights(f"mod{at}")
            if k0 == 0:
                mod_bank[0] = mod_pool.take()
            b, ps, free = mod_bank[0]
            PE.wait(wm + c_m + (free if k0 == 0 else []))
            for k in range(4):
                m = t.matmul(ps[0:2, :], csilu[:, k0 + k, :], w[:, k, :], start=(k0 + k == 0), stop=(k0 + k == 7))
            m.then_inc(PE.sem, 1)
            PE.count += 1
            pm = (PE.sem, PE.count)
            used(wi, pm)
            if k0:
                mod_pending.append((layer, c, b, ps, pm))

    def flush_mods():
        while mod_pending:
            layer, c, b, ps, pm = mod_pending.pop(0)
            mk = step(DV, [pm] + modrow_free[0], v.tensor_copy, modrow[:, :], ps[0:2, :])
            give(b, [mk])
            st = load(GP, f"mod_out{layer}{c}", mod_dram[layer][:, 512 * c:512 * c + 512], modrow[:, :], [mk])
            modrow_free[0] = [st]
            mod_stored[layer].append(st)

    probs_free = [[] for _ in range(4)]
    probsT_free = [[] for _ in range(4)]
    att_n = [0]

    def attention(qtiles, heads, q, k, nk, val, marks, finish, bias=None, b0=0, nbias=0, sink=None, during=()):
        flush_mods()
        scores = Pool([0, 1, 2])
        items = [(qt, h) for qt in qtiles for h in range(heads)]
        state = {}
        outs = {}
        rsum = {qt: stat(heads) for qt in qtiles}
        esink = {qt: stat(heads) for qt in qtiles} if sink is not None else None
        summed = {}

        def head_scores(qt, h):
            n = nk(qt)
            b, ps, free = scores.take()
            m = products(free + marks, [(ps[:, 0:n], q(h, qt), k(h, n))])
            mn = stat(1)
            if bias is not None and nbias == n:
                m = step(DV, [m] + bias_marks, v.tensor_tensor_reduce, ps[:, 0:n], ps[:, 0:n], bias(h, qt),
                         1.0, 3e38, ALU.add, ALU.min, mn)
            else:
                if bias is not None:
                    m = step(DV, [m] + bias_marks, v.tensor_tensor, ps[:, b0:b0 + nbias], ps[:, b0:b0 + nbias],
                             bias(h, qt), ALU.subtract)
                m = step(DV, [m], v.tensor_reduce, mn, ps[:, 0:n], AX_X, ALU.min)
            if sink is not None:
                m = step(DV, [m], v.tensor_scalar, mn, sink(h), -1.0, mn, ALU.mult, ALU.min)
            i = att_n[0] % 4
            att_n[0] += 1
            pr = probs[:, i, 0:n]
            me = step(AC, [m] + probs_free[i] + junk_mark[0], a.activation, pr, ps[:, 0:n], ACT.Exp, bias=mn, scale=-1.0,
                      accum_out=rsum[qt][:, h:h + 1])
            give(b, [me])
            summed[(qt, h)] = [me]
            if sink is not None:
                summed[(qt, h)].append(step(AC, [m], a.activation, esink[qt][:, h:h + 1], sink(h), ACT.Exp, bias=mn))
            state[(qt, h)] = (i, pr, me, n)

        def head_values(qt, h):
            i, pr, me, n = state.pop((qt, h))
            b, ps, free = turn.take()
            PE.wait(free + [me])
            for j in range(n // P):
                m = t.transpose(ps[:, j * P:(j + 1) * P], pr[:, j * P:(j + 1) * P], ident)
            m.then_inc(PE.sem, 1)
            PE.count += 1
            m = (PE.sem, PE.count)
            probs_free[i] = [m]
            pT = probsT[:, i, 0:n]
            if (h + qt) % 2:
                me = step(AC, [m] + probsT_free[i], a.copy, pT, ps[:, 0:n])
            else:
                me = step(DV, [m] + probsT_free[i], v.tensor_copy, pT, ps[:, 0:n])
            give(b, [me])
            state[(qt, h, "T")] = (i, pT, me, n)

        def head_out(qt, h):
            i, pT, me, n = state.pop((qt, h, "T"))
            if h % 4 == 0:
                outs[0] = outp.take()
            b, po, free = outs[0]
            m = products(free + [me] + marks, [(po[:, (h % 4) * P:(h % 4 + 1) * P], pT[:, j * P:(j + 1) * P], val(h, j))
                                              for j in range(n // P)])
            probsT_free[i] = [m]
            if h % 4 == 3:
                hs = range(h - 3, h + 1)
                r = rsum[qt][:, h - 3:h + 1]
                dm = [x for hh in hs for x in summed[(qt, hh)]]
                if sink is not None:
                    dm = [step(DV, dm, v.tensor_tensor, r, r, esink[qt][:, h - 3:h + 1], ALU.add)]
                dm = [step(DV, dm, v.reciprocal, r, r)]
                give(b, finish(qt, h // 4, po, [m] + dm, r))

        for n in range(len(items) + 4):
            if n < len(items):
                head_scores(*items[n])
            if 2 <= n < len(items) + 2:
                head_values(*items[n - 2])
            if n >= 4:
                head_out(*items[n - 4])
            if n in during:
                during[n]()
        for i in range(4):
            junk_mark[0] = junk_mark[0] + probs_free[i]

    bias_marks = []

    for e in (PE, DV):
        e.wait(sq_m + cols_m)

    base = 16 * 384
    qaT, base = carve(base, 4, S)
    kaT, base = carve(base, 1, S)
    qbT, base = carve(base, 4, S)
    kbT, base = carve(base, 4, S)
    va, base = carve(base, 2, 128)
    vb, base = carve(base, 2, 512)
    o_tm, base = carve(base, 2, D)
    mix, _ = carve(0, 2, D)

    lat = [2, 3]
    m = norm_into_T(turn, [H[:, i, :] for i in lat], D, uT, [0, P], [x_m, x_m], gain=lambda i: col("g_pre_mix"))
    u_m = m[0] + m[1]
    split_ready()
    c_m = [step(AC, cols_m, a.activation, csilu[:, :, :].rearrange("p a b -> p (a b)"), col("c"), ACT.Silu)]

    GP.wait(split_done[0])
    bias_m = [load(GP, "bias_t5", bias_t5, ins["bias_t5"])]
    lnc_m = [load(GP, "lnc", lnc, ins["lnc"])]
    small_m = [load(GP, "small_rows", small_rows[:, :], ins["small_rows"].partition_broadcast(P))]
    ma = step(GP, bias_m, g.tensor_scalar, bias_t5[:, 0:8, :], bias_t5[:, 0:8, :], -1.0, None, ALU.mult)
    m = step(GP, bias_m + lnc_m, g.tensor_tensor, bias_t5[:, 8:16, :],
             lnc.unsqueeze(1).to_broadcast([P, 8, 384]), bias_t5[:, 8:16, :], ALU.subtract)
    bias_marks = [ma, m]
    probsT_free[0] = [m]
    mask_f32 = rowbuf[:, :, :].rearrange("p a b -> p (a b)")[:, 0:14 * P]
    misc_m = [load(GP, "sel2", sel2[:, :], ins["sel2"]), load(GP, "gla_mask", mask_f32, ins["gla_mask"]), load(GP, "rope", rope[:, :, :, :], ins["rope"])]
    misc_m.append(step(GP, misc_m, g.tensor_copy, gla_mask[:, :], mask_f32))
    GP.wait(misc_m)
    g_post_mix = load_row(0, "g_post_mix")
    g_post_mlp = load_row(1, "g_post_mlp")

    def copy_out(dst, scale=None):
        def f(i, ps, mk):
            d = dst(i)
            n = d.shape[-1]
            mk = step(AC, [mk], a.activation, d, ps[:, 0:n], ACT.Copy, scale=1.0 if scale is None else scale)
            kept.append(mk)
            return [mk]
        return f

    def copy_out_v(dst):
        def f(i, ps, mk):
            d = dst(i)
            mk = step(DV, [mk], v.tensor_copy, d, ps[:, 0:d.shape[-1]])
            kept.append(mk)
            return [mk]
        return f

    kept = []
    project_fm(gemm, "qa", uT, u_m, 0, S, range(4), copy_out(lambda ft: qaT[:, ft, :], -HD ** -0.5))
    w, wm, wi = weights("kva")
    for it in range(3):
        b, ps, free = gemm.take()
        PE.wait(free + wm + u_m)
        for k in range(KT):
            for j, (x, y) in enumerate(HALVES):
                l, r = (w[x][:, k, 0:P], uT[y][:, k, 0:S]) if it == 0 else (uT[x][:, k, (it - 1) * P:it * P], w[y][:, k, :])
                m = t.matmul(ps[:, 0:S], l, r, start=(k + j == 0), stop=(k == KT - 1 and j == 2))
        m.then_inc(PE.sem, 1)
        PE.count += 1
        d, src = (kaT[:, 0, :], ps[:, 0:S]) if it == 0 else (va[:, it - 1, :], ps[:, P:2 * P])
        mk = step(DV, PE.last(), v.tensor_copy, d, src)
        kept.append(mk)
        give(b, [mk])
    used(wi, PE.last()[0])
    project_fm(gemm, "qb", uT, u_m, 0, S, range(4), copy_out(lambda ft: qbT[:, ft, :], -HD ** -0.5))
    project_fm(gemm, "kb", uT, u_m, 0, S, range(4), copy_out_v(lambda ft: kbT[:, ft, :]))
    project_tm(gemm, "vb", uT, lambda i: u_m, [0, 1], copy_out_v(lambda i: vb[:, i, :]))
    proj_m = kept[:]
    proj_last = PE.last()

    o_marks = {0: [], 1: []}

    def finish_to(dst, out_marks, same_half=False):
        def f(qt, hg, po, mk, r):
            if same_half:
                dm = step(DV, mk, v.tensor_tensor, dst(qt)[:, hg * 256:(hg + 1) * 256].rearrange("p (h d) -> p h d", h=4),
                          po.rearrange("p (h x) -> p h x", h=4)[:, :, 64 * hg:64 * hg + 64], bc(r, 64), ALU.mult)
            else:
                d = dst(qt)[:, hg * 256:(hg + 1) * 256].rearrange("p (c e d) -> p c e d", c=2, e=2)
                po_, r_ = po.rearrange("p (c e x) -> p c e x", c=2, e=2), r.rearrange("p (c e) -> p c e", c=2)
                for e in range(2):
                    dm = step(DV, mk, v.tensor_tensor, d[:, :, e], po_[:, :, e, 64 * e:64 * e + 64], bc(r_[:, :, e], 64), ALU.mult)
            out_marks(qt).append(dm)
            return [dm]
        return f

    def t5(h, qt):
        return bias_t5[:, h, (128 if qt == 0 else 0):(128 if qt == 0 else 0) + S]

    hp = lambda h: slice(64 * h, 64 * h + 64)
    attention([0, 1], 8, lambda h, qt: qaT[hp(h // 4), h % 4, qt * P:(qt + 1) * P], lambda h, n: kaT[hp(h // 4), 0, 0:n],
              lambda qt: S, lambda h, j: va[:, j, :], proj_m + small_m,
              finish_to(lambda qt: o_tm[:, qt, 0:512], lambda qt: o_marks[qt], True), bias=t5, nbias=S,
              sink=lambda h: small_rows[:, h:h + 1])
    pair_of = lambda h: slice(128 * (h // 2), 128 * (h // 2) + 128)
    dead_u = proj_last
    a_marks = [list(o_marks[i]) for i in range(2)]
    m1 = {}

    def norm_a():
        m1[0] = norm_into_T(turn, [o_tm[:, i, 0:512] for i in range(2)], 512, tuple(x[:, 0:4, :] for x in uT), [0, P], a_marks,
                            gain=lambda i: col("g_out_a"), dst_free=dead_u, defer=True, junk=rtmp[:, :, :].rearrange("p a b -> p (a b)"))

    def norm_a_T():
        m1[0] = m1[0]()

    attention([0, 1], 8, lambda h, qt: qbT[hp(h % 2), h // 2, qt * P:(qt + 1) * P], lambda h, n: kbT[hp(h % 2), h // 2, 0:n],
              lambda qt: S, lambda h, j: vb[:, j, pair_of(h)], proj_m,
              finish_to(lambda qt: o_tm[:, qt, 512:1024], lambda qt: o_marks[qt]), bias=lambda h, qt: t5(h + 8, qt), nbias=S,
              during={5: norm_a, 9: norm_a_T})
    dbg("o_tm", o_tm, o_marks[0] + o_marks[1])

    fill(FILL["o"])
    m2 = norm_into_T(turn, [o_tm[:, i, 512:1024] for i in range(2)], 512, tuple(x[:, 4:8, :] for x in uT), [0, P], o_marks,
                     gain=lambda i: col("g_out_b"), dst_free=dead_u)
    oT_m = [m1[0][i] + m2[i] for i in range(2)]

    def project_1024(names, srcT, src_marks, tiles, evac):
        for c, name in enumerate(names):
            project_tm(gemm, name, srcT, src_marks, tiles, lambda i, ps, mk, c=c: evac(i, c, ps, mk))

    def half(ap, c):
        return ap[:, c * 512:(c + 1) * 512]

    def residual_norm(src, src_marks, gain, gain_marks):
        r, rm, _ = rstd_of([src[:, i, :] for i in range(2)], D, [src_marks[i] for i in range(2)])
        res = []
        for i in range(2):
            mk = step(DV, [rm] + src_marks[i] + gain_marks, v.scalar_tensor_tensor, src[:, i, :], src[:, i, :],
                      r[:, i:i + 1], gain, ALU.mult, ALU.mult)
            e, add = ((GP, g), (DV, v))[i]
            res.append([step(e, [mk], add.tensor_tensor, H[:, 2 + i, :], H[:, 2 + i, :], src[:, i, :], ALU.add)])
        return res

    mix_marks = [[], []]
    bias_dead = DV.last()

    def mix_evac(i, c, ps, mk):
        mk = step(DV if c else AC, [mk] + bias_dead, v.tensor_copy if c else a.copy, half(mix[:, i, :], c), ps)
        mix_marks[i].append(mk)
        return [mk]

    project_1024(["wo0", "wo1"], uT, lambda i: oT_m[i], [0, 1], mix_evac)
    fill(FILL["mix"])
    h_m = residual_norm(mix, mix_marks, g_post_mix, row_m["g_post_mix"])
    b_ple = load_row(0, "b_ple_gate", DV.last())
    dbg("h1", H[:, 2:4, :], h_m[0] + h_m[1])

    dead = PE.last()
    m = norm_into_T(turn, [H[:, i, :] for i in lat], D, uT, [0, P], h_m, gain=lambda i: col("g_pre_mlp"), dst_free=dead)
    v_m = m[0] + m[1]
    flush_mods()
    hidden = [tuple(x[:, 4 * k:4 * k + 4, S:2 * S] for x in uT) for k in range(2)]
    relu, _ = carve(2 * D, 4, 512)
    relu_free = [fence() for _ in range(4)]
    hidden_free = [[], []]
    mix_dead = fence()
    down = {(i, h): banks[:, 2 * i + h, :] for i in range(2) for h in range(2)}
    hid_m = {}
    down_free = [m for b in range(4) for m in bank_free[b]]
    mix_marks = [[], []]
    for c in range(9):
        if c < 8:
            sl = c % 2
            hm = []
            for kc in range(2):
                w, wm, wi = weights(f"up{c}.{kc}")
                b, ps, free = up_pool.take()
                for f in range(2):
                    PE.wait(free + wm + v_m)
                    for k in range(KT):
                        for j, (x, y) in enumerate(HALVES):
                            m = t.matmul(ps[:, f * S:(f + 1) * S], w[x][:, k, f * P:(f + 1) * P], uT[y][:, k, 0:S],
                                         start=(k + j == 0), stop=(k == KT - 1 and j == 2))
                m.then_inc(PE.sem, 1)
                PE.count += 1
                pm = (PE.sem, PE.count)
                rk = (2 * c + kc) % 4
                rl = relu[:, rk, :]
                rm = step(AC, [pm] + relu_free[rk], a.activation, rl, ps, ACT.Relu)
                give(b, [rm])
                sm = step(GP, [rm], g.tensor_tensor, rl, rl, rl, ALU.mult)
                used(wi, pm)
                hi, lo = (x[:, 2 * kc:2 * kc + 2, :] for x in hidden[sl])
                relu_free[rk] = split(rl.rearrange("p (f s) -> p f s", f=2), hi, lo, [sm], hidden_free[sl])
                hm += relu_free[rk]
            hid_m[c] = hm
        if c:
            hi, lo = hidden[(c - 1) % 2]
            for h in range(2):
                w, wm, wi = weights(f"down{c - 1}{h}")
                for i in range(2):
                    PE.wait(wm + hid_m[c - 1] + (down_free if c == 1 else []))
                    for k in range(4):
                        for j, (x, y) in enumerate(HALVES):
                            m = t.matmul(down[(i, h)], (hi, lo)[x][:, k, i * P:(i + 1) * P], w[y][:, k, :],
                                         start=(c == 1 and k + j == 0), stop=(c == 8 and k == 3 and j == 2))
                    m.then_inc(PE.sem, 1)
                    PE.count += 1
                    pm = (PE.sem, PE.count)
                    if c == 8:
                        mk = step(DV if i else AC, [pm] + mix_dead, v.tensor_copy if i else a.copy, half(mix[:, i, :], h), down[(i, h)])
                        give(2 * i + h, [mk])
                        mix_marks[i].append(mk)
                used(wi, pm)
            hidden_free[(c - 1) % 2] = [pm]
    fill(FILL["mlp"])
    h_m = residual_norm(mix, mix_marks, g_post_mlp, row_m["g_post_mlp"])
    g_post_ple = load_row(1, "g_post_ple", DV.last())
    dbg("h2", H[:, 2:4, :], h_m[0] + h_m[1])

    gateB = {0: rowbuf[:, 0, :], 1: rowbuf[:, 1, :]}
    mod_shift, mod_gain = sb("mod_shift", [P, KT, 2]), sb("mod_gain", [P, KT, 2])
    mod_sum = sb("mod_sum", [P, 32])

    def modulation_columns(layer, readers):
        flush_mods()
        back = rtmp[0:32, 0, :]
        src = mod_dram[layer][:, 0:2 * D].rearrange("r (j q) -> r j q", q=P)
        bm = []
        for r in range(2):
            bm.append(load(GP, f"mod_cols{layer}{r}", rtmp[16 * r:16 * r + 16, 0, :], src[r], mod_stored[layer][0:4] + readers))

        def rest():
            b, ps, free = turn.take()
            PE.wait(free + bm)
            m = t.transpose(ps[:, 0:32], back, sq[0:32, 0:32])
            m.then_inc(PE.sem, 1)
            PE.count += 1
            m = step(DV, PE.last() + readers, v.tensor_copy, mod_sum[:, :], ps[:, 0:32])
            give(b, [m])
            sums = mod_sum[:, :].rearrange("p (r c j) -> p c j r", r=2, c=2)
            ms = step(DV, [m], v.tensor_tensor, mod_shift[:, :, :], sums[:, 0], bc(col(f"l{layer}_b_mod", 0, 8), 2), ALU.add)
            m = step(DV, [m], v.tensor_tensor, mod_gain[:, :, :], sums[:, 1], bc(col(f"l{layer}_b_mod", 8, 8), 2), ALU.add)
            m = step(DV, [m], v.tensor_scalar, mod_gain[:, :, :], mod_gain[:, :, :], 1.0, None, ALU.add)
            m = step(DV, [m], v.tensor_tensor, mod_gain[:, :, :], mod_gain[:, :, :], bc(col(f"l{layer}_norm"), 2), ALU.mult)
            return [ms, m]

        return rest

    def load_gates(layer, readers):
        flush_mods()
        rows = probsT[0:2, 1:3, :].rearrange("p a b -> p (a b)")
        bg = probs[:, 2:4, :].rearrange("p a b -> p (a b)")
        gm = load(GP, f"mod_gates{layer}", rows, mod_dram[layer][:, 2 * D:3 * D], mod_stored[layer][4:6] + readers)
        bgm = load(GP, f"b_gate{layer}", bg, ins["rows"][ROWS_ORDER.index(f"l{layer}_b_gate"), :].partition_broadcast(P), readers)
        return rows, bg, gm, bgm

    def modulation_gates(layer, streams, loaded, readers):
        rows, bg, gm, bgm = loaded
        gates = []
        for r in streams:
            for c in range(2):
                b, ps, free = gemm.take()
                pm = products(free + [gm] + misc_m, [(ps, sel2[:, r * P:(r + 1) * P], rows[:, c * 512:(c + 1) * 512])])
                m2 = step(DV, [pm, bgm] + readers, v.tensor_tensor, half(gateB[r], c), ps, half(bg, c), ALU.add)
                give(b, [m2])
                gates.append(m2)
        for i in range(4):
            probsT_free[i], probs_free[i] = PE.last(), gates[-1:]
        return gates

    pf, base = carve(2 * D, 2, S)
    gate_tm, base = carve(base, 2, D)
    ple_tm, base = carve(base, 2, D)
    arena_free = fence()
    pT = tuple(x[:, 0:2, S:2 * S] for x in uT)
    pT_m = split(pf, pT[0], pT[1], [load(AC, "pT", pf, ins["pT"].rearrange("(k p) t -> p k t", p=P), arena_free)], arena_free)
    w, wm, wi = weights("ple")
    ple_marks = [[], []]
    for i in range(2):
        for c in range(2):
            b, ps, free = gemm.take()
            PE.wait(free + wm + pT_m)
            for k in range(2):
                for j, (x, y) in enumerate(HALVES):
                    m = t.matmul(ps, pT[x][:, k, i * P:(i + 1) * P], w[y][:, k, c * 512:c * 512 + 512],
                                 start=(k + j == 0), stop=(k == 1 and j == 2))
            m.then_inc(PE.sem, 1)
            PE.count += 1
            mk = step(AC, PE.last() + arena_free, a.copy, half(ple_tm[:, i, :], c), ps)
            give(b, [mk])
            ple_marks[i].append(mk)
    used(wi, PE.last()[0])
    hT_m = []
    for i in range(2):
        mk, _ = into_T(turn, H[:, 2 + i, :], D, uT, i * P, h_m[i], dst_free=dead)
        hT_m.append(mk)
    mix_marks = [[], []]

    def gate_evac(i, c, ps, mk):
        gsl = half(gate_tm[:, i, :], c)
        m1 = step(DV, [mk] + row_m["b_ple_gate"], v.tensor_tensor, gsl, ps, half(b_ple, c), ALU.add)
        m2 = step(AC, [m1], a.activation, gsl, gsl, ACT.Sigmoid)
        mix_marks[i].append(step(GP, [m2] + ple_marks[i] + arena_free, g.tensor_tensor, half(mix[:, i, :], c), gsl,
                                 half(ple_tm[:, i, :], c), ALU.mult))
        return [m1]

    project_1024(["pg0", "pg1"], uT, lambda i: hT_m[i], [0, 1], gate_evac)
    columns_0 = modulation_columns(0, [])
    fill(FILL["ple"])
    h_m = residual_norm(mix, mix_marks, g_post_ple, row_m["g_post_ple"])
    dbg("h3", H[:, 2:4, :], h_m[0] + h_m[1])

    def modulated_norm(tiles, marks, mod_m, dst_free):
        stream = lambda tile: 0 if tile < 2 else 1
        m = norm_into_T(turn, [H[:, i, :] for i in tiles], D, uT, [i * P for i in tiles],
                        [marks[i] + mod_m for i in tiles],
                        gain=lambda i: mod_gain[:, :, stream(tiles[i])],
                        shift=lambda i: mod_shift[:, :, stream(tiles[i])], dst_free=dst_free)
        return {tile: m[i] for i, tile in enumerate(tiles)}

    def gate_and_out(names, tiles, tile0, catT, cat_marks, H_marks):
        res = {i: [] for i in tiles}

        def evac(i, c, ps, mk):
            k = (2 * c + i) % 4
            tile = i + tile0
            tmp = probsT[:, k, :]
            m1 = step(DV, [mk] + probsT_free[k] + gates_m, v.tensor_tensor, tmp, ps, half(gateB[0 if tile < 2 else 1], c), ALU.mult)
            m2 = step(GP, [m1] + H_marks[tile], g.tensor_tensor, half(H[:, tile, :], c), half(H[:, tile, :], c), tmp, ALU.add)
            probsT_free[k] = [m2]
            res[i].append(m2)
            return [m1]

        project_1024(names, catT, lambda i: cat_marks[i], tiles, evac)
        return {i + tile0: res[i] for i in tiles}

    ctx_m = [load(AC, "ctx", H[:, 0:2, :], ins["ctx"].rearrange("(t p) d -> p t d", p=P), split_done[in_first_block - 1])]
    mod_m = columns_0()
    f = fence()
    loaded = load_gates(0, f)
    ctx_marks = {0: ctx_m, 1: ctx_m, 2: h_m[0], 3: h_m[1]}
    fill(FILL["um"])
    um = modulated_norm([0, 1, 2, 3], ctx_marks, mod_m, PE.last())
    u_all = [x for i in range(4) for x in um[i]]
    gates_m = modulation_gates(0, [0, 1], loaded, f)
    stage0 = fence_all()
    all4 = range(4)
    a_tm, base = carve(0, 4, 512)
    qT, base = carve(base, 8, 512)
    kT, base = carve(base, 8, 512)
    v_tm, base = carve(base, 4, 512)
    kr_tm, base = carve(base, 4, ROPE)
    q_tm = xn[:, 0, 0:8 * QK].rearrange("p (h d) -> p h d", h=8)
    k_tm = xn[:, 1, 0:8 * QK].rearrange("p (h d) -> p h d", h=8)
    g_tm = sb("g_tm", [P, 4, 16])

    kr_m, gt_m, cq_raw, ckv_raw = {}, {}, {}, {}
    cq_tm, _ = carve(0, 4, Q_RANK)
    ckv_tm, _ = carve(4 * 512 + 16 * 512, 4, KV_RANK)
    cqT, _ = carve(4 * 512 + 8 * 512, 3, 512)
    ckvT, _ = carve(4 * 512 + 8 * 512 + 3 * 512, 2, 512)

    def cq_evac(i, ps, mk):
        cq_raw[i] = [step(AC, [mk], a.copy, cq_tm[:, i, :], ps[:, 0:Q_RANK])]
        return cq_raw[i]

    project_tm(gemm, "cq", uT, lambda i: um[i], all4, cq_evac, n=Q_RANK)
    cq_m = norm_into_T(turn, [cq_tm[:, i, :] for i in all4], Q_RANK, cqT, [i * P for i in all4], [cq_raw[i] for i in all4],
                       gain=lambda _: col("q_norm"), defer=True)

    def ckv_evac(i, ps, mk):
        m1 = step(DV, [mk], v.tensor_copy, kr_tm[:, i, :], ps[:, KV_RANK:KV_RANK + ROPE])
        m2 = step(DV, [mk] + small_m, v.tensor_tensor, g_tm[:, i, :], ps[:, KV_RANK + ROPE:KV_RANK + ROPE + 16],
                  small_rows[:, 8:24], ALU.add)
        m3 = step(AC, [m2], a.copy, ckv_tm[:, i, :], ps[:, 0:KV_RANK])
        kr_m[i], gt_m[i], ckv_raw[i] = [m1], m2, [m3]
        return [m3]

    project_tm(gemm, "ckv", uT, lambda i: um[i], all4, ckv_evac, n=KV_RANK + ROPE + 16)
    fill(FILL["latent"])
    cq_m = cq_m()
    ckv_m = norm_into_T(turn, [ckv_tm[:, i, :] for i in all4], KV_RANK, ckvT, [i * P for i in all4], [ckv_raw[i] for i in all4],
                        gain=lambda _: col("kv_norm"))

    rt_free = [[]]

    def rotate(view, nh, tile, after):
        y = view.rearrange("p h (a two c) -> p h a two c", a=2, two=2)
        y1, y2 = y[:, :, :, 0, :], y[:, :, :, 1, :]

        def table(which):
            x_ = rope[:, tile, which, :].rearrange("p (a c) -> p a c", a=2)
            return x_.unsqueeze(1).to_broadcast([P, nh, 2, PAIRS])

        tmp = [rtmp[:, j, 0:nh * 16].rearrange("p (h a c) -> p h a c", h=nh, a=2) for j in range(4)]
        ms = []
        for j, (y_, w_) in enumerate(((y1, 0), (y2, 1), (y2, 0), (y1, 1))):
            ms.append(step(GP, after + rt_free[0] + misc_m, g.tensor_tensor, tmp[j], y_, table(w_), ALU.mult))
        m1 = step(GP, ms, g.tensor_tensor, y1, tmp[0], tmp[1], ALU.subtract)
        m2 = step(GP, ms, g.tensor_tensor, y2, tmp[2], tmp[3], ALU.add)
        rt_free[0] = [m1, m2]
        return [m1, m2]

    def heads_into_T(src, dst, tile, after):
        res = []
        for hh in range(2):
            b, ps, free = turn.take()
            PE.wait(free + after)
            for j in range(4):
                m = t.transpose(ps[0:QK, j * P:(j + 1) * P], src[:, 4 * hh + j, :], ident)
            m.then_inc(PE.sem, 1)
            PE.count += 1
            d = dst[0:QK, 4 * hh:4 * hh + 4, tile * P:(tile + 1) * P]
            psv = ps[0:QK, :].rearrange("p (j q) -> p j q", j=4)
            mk = step(DV, PE.last(), v.tensor_copy, d, psv) if hh else step(AC, PE.last(), a.copy, d, psv)
            give(b, [mk])
            res.append(mk)
        return res, PE.last()

    wq = [weights("uq0"), weights("uq1")]
    q_free, qT_m = xn_free[0] + xn_free[1], []
    for i in all4:
        qf = q_tm.rearrange("p a b -> p (a b)")
        ms = []
        for c0, n, (w, wm, wi) in ((0, 512, wq[0]), (512, 256, wq[1])):
            b, ps, free = gemm.take()
            pm = products(free + wm + cq_m[i], [(ps[:, 0:n], cqT[:, k, i * P:(i + 1) * P], w[:, k, 0:n]) for k in range(3)])
            mk = step(AC, [pm] + q_free, a.activation, qf[:, c0:c0 + n], ps[:, 0:n], ACT.Copy, scale=-QK ** -0.5)
            give(b, [mk])
            ms.append(mk)
        if i >= 2:
            ms = ms + rotate(q_tm[:, :, NOPE:QK], 8, i - 2, ms)
        mk, q_free = heads_into_T(q_tm, qT, i, ms)
        qT_m += mk
    used(wq[0][2], pm, True)
    used(wq[1][2], pm, True)
    w, wm, wi = weights("ukv")
    k_free, kv_m = xn_free[0] + xn_free[1], []
    for i in all4:
        ms = []
        for hh in range(2):
            b, ps, free = gemm.take()
            pm = products(free + wm + ckv_m[i], [(ps, ckvT[:, k, i * P:(i + 1) * P], w[:, k, hh * 512:hh * 512 + 512]) for k in range(2)])
            kvv = ps.rearrange("p (h d) -> p h d", h=4)
            m1 = step(DV, [pm] + k_free, v.tensor_copy, k_tm[:, 4 * hh:4 * hh + 4, 0:NOPE], kvv[:, :, 0:NOPE])
            m2 = step(AC, [m1], a.copy, v_tm[:, i, hh * 256:hh * 256 + 256].rearrange("p (h d) -> p h d", h=4), kvv[:, :, NOPE:])
            give(b, [m1, m2])
            kv_m.append(m2)
            ms.append(m1)
        krv = kr_tm[:, i, :].unsqueeze(1)
        if i >= 2:
            kr_m[i] = kr_m[i] + rotate(krv, 1, i - 2, kr_m[i])
        ms.append(step(DV, kr_m[i] + k_free, v.tensor_copy, k_tm[:, :, NOPE:QK], krv.to_broadcast([P, 8, ROPE])))
        mk, k_free = heads_into_T(k_tm, kT, i, ms + [pm])
        kv_m += mk
    used(wi, pm)
    xn_free[0] = xn_free[1] = PE.last()
    cat_free = fence()
    for e in (DV, AC):
        e.wait(cat_free)
    a_m = {i: [] for i in all4}
    bias_marks = []
    attention(all4, 8, lambda h, qt: qT[0:QK, h, qt * P:(qt + 1) * P], lambda h, n: kT[0:QK, h, 0:n],
              lambda qt: 256 if qt < 2 else 512, lambda h, j: v_tm[:, j, pair_of(h)], qT_m + kv_m,
              finish_to(lambda qt: a_tm[:, qt, :], lambda qt: a_m[qt]))
    dbg("mla", a_tm, fence())

    stage1 = fence_all()
    h_tm, base = carve(4 * 512, 4, 512)
    mlT = []
    for _ in range(2):
        w_, base = carve(base, 4, 512)
        mlT.append(w_)
    mv, base = carve(base, 4, 4, 132)
    dec, base = carve(base, 2, 512)
    selneg = arena[0:4, base:base + 4 * P]
    selneg_m = [load(AC, "selneg", selneg, ins["selneg"], stage1)]
    base += 4 * P
    pads = []
    b2 = 4 * 512
    for _ in range(2):
        w_, b2 = carve(b2, 2, 384)
        pads.append(w_)
    assert b2 <= 8 * 512
    pads = pads * 2
    Mrow = xn
    glog, gb, ga_ = sb("glog", [P, 4, 2, 4]), sb("gb", [P, 4, 2, 4]), sb("ga_", [P, 4, 2, 4])
    gem = sb("gem", [P, 4, 2, 4])
    ml_m = [[], []]
    def log_sigmoid(items):
        ms = [step(AC, after, a.activation, tmp, x_, ACT.Abs) for x_, tmp, _, after in items]
        ms = [step(AC, [m], a.activation, it[1], it[1], ACT.Exp, scale=-1.0) for m, it in zip(ms, items)]
        ms = [step(AC, [m], a.activation, it[1], it[1], ACT.Ln, bias=one_col[:, 0:1]) for m, it in zip(ms, items)]
        return [step(DV, [m] + list(after), v.scalar_tensor_tensor, dst, x_, 0.0, tmp, ALU.min, ALU.subtract)
                for m, (x_, tmp, dst, after) in zip(ms, items)]

    gv5 = g_tm[:, :, :].rearrange("p t (d w h) -> p t d w h", d=2, w=2)
    gtm = list(gt_m.values())
    ftmp = rtmp[:, 0, 0:32].rearrange("p (t d h) -> p t d h", t=4, d=2)
    fin = rtmp[:, 1, 0:32].rearrange("p (t d h) -> p t d h", t=4, d=2)
    m = step(DV, gtm + rt_free[0], v.tensor_copy, fin, gv5[:, :, :, 1, :])
    fl = lambda x_: x_.rearrange("p t d h -> p (t d h)")
    lf_m = log_sigmoid([(rtmp[:, 1, 0:32], rtmp[:, 0, 0:32], fl(glog[:, :, :, :]), [m])])[0]
    for which, name in enumerate(("mq", "mk")):
        def conv_evac(ft, ps, mk, which=which):
            d = mlT[which][:, ft, :]
            cw = col("conv_w").rearrange("p (j f) -> p j f", j=3)
            f = 4 * which + ft
            dr, pr = (x_.rearrange("p (r s) -> p r s", r=2) for x_ in (d, ps))
            m = step(DV, [mk], v.tensor_scalar, d, ps, cw[:, 1, f:f + 1], col("conv_b", f, 1), ALU.mult, ALU.add)
            m = step(DV, [m], v.scalar_tensor_tensor, dr[:, :, 1:S], pr[:, :, 0:S - 1], cw[:, 0, f:f + 1], dr[:, :, 1:S], ALU.mult, ALU.add)
            m = step(DV, [m], v.scalar_tensor_tensor, dr[:, :, 0:S - 1], pr[:, :, 1:S], cw[:, 2, f:f + 1], dr[:, :, 0:S - 1], ALU.mult, ALU.add)
            ml_m[which].append(step(AC, [m], a.activation, d, d, ACT.Silu))
            return [m]
        project_fm(gemm, name, uT, u_all, 0, 512, range(4), conv_evac)
    mv_ones = step(GP, [], g.memset, mv[:, :, :, 128:129], 1.0)
    mv_m = [mv_ones]

    def mv_evac(i, ps, mk):
        mk = step(DV, [mk], v.tensor_copy, mv[:, i, :, 0:128], ps.rearrange("p (h d) -> p h d", h=4))
        mv_m.append(mk)
        return [mk]

    b, ps, free = gemm.take()
    gbp = ps[:, 0:32].rearrange("p (t d h) -> p t d h", t=4, d=2)
    for i in all4:
        for d in range(2):
            if d == 0:
                src = [(j, "ones") for j in range(i)] + [(i, "tri_u")]
            elif i < 2:
                src = [(i, "tri_l")] + [(j, "ones") for j in range(i + 1, 2)]
            else:
                src = [(0, "ones"), (1, "ones"), (i, "tri_l")] + [(j, "ones") for j in range(i + 1, 4)]
            pm = products(free + [lf_m], [(gbp[:, i, d, :], sqc(n_), glog[:, j, d, :]) for j, n_ in src])
    bm = step(DV, [pm], v.tensor_copy, gb[:, :, :, :], gbp)
    give(b, [bm])
    am = step(DV, [bm], v.tensor_tensor, ga_[:, :, :, :], gv5[:, :, :, 0, :], gb[:, :, :, :], ALU.subtract)
    zm = step(GP, [], g.memset, arena[0:4, 4 * 512:4 * 512 + 2 * 768], 0.0)
    for d in range(2):
        b, ps, free = gemm.take()
        PE.wait(free + [am])
        for i in all4:
            m = t.transpose(ps[0:4, i * P:(i + 1) * P], ga_[:, i, d, :], ident)
        m.then_inc(PE.sem, 1)
        PE.count += 1
        lo = 128 if d == 0 else 0
        own = pads[2 * d:2 * d + 2]
        if d:
            zm = step(GP, Mm, g.memset, arena[0:4, 4 * 512:4 * 512 + 2 * 768], 0.0)
        m = step(DV, PE.last() + [zm], v.tensor_copy, own[0][0:4, :, lo:lo + S], ps[0:4, :].rearrange("p (r s) -> p r s", r=2))
        give(b, [m])
        cur = 0
        for sh in (1, 2, 4, 8, 16, 32, 64, 128):
            s_ = own[cur][0:4]
            o_ = own[1 - cur][0:4]
            off = lo - sh if d == 0 else sh
            m = step(DV, [m], v.tensor_tensor, o_[:, :, lo:lo + S], s_[:, :, lo:lo + S], s_[:, :, off:off + S], ALU.max)
            cur = 1 - cur
        s_ = own[cur][0:4]
        carry = s_[:, 0, lo + S - 1:lo + S] if d == 0 else s_[:, 0, lo:lo + 1]
        m1 = step(DV, [m], v.tensor_scalar, Mrow[0:4, d, 0:S], s_[:, 0, lo:lo + S], 0.0, None, ALU.max)
        m2 = step(DV, [m], v.tensor_scalar, Mrow[0:4, d, S:2 * S], s_[:, 1, lo:lo + S], carry, 0.0, ALU.max, ALU.max)
        if d == 0:
            Mm = [m1, m2]
        else:
            Mm = Mm + [m1, m2]
    project_tm(gemm, "mv", uT, lambda i: um[i], all4, mv_evac)
    fill(FILL["gem"])
    b, ps, free = gemm.take()
    PE.wait(free + Mm)
    mtp = ps[:, 0:32].rearrange("p (t d h) -> p t d h", t=4, d=2)
    for i in all4:
        for d in range(2):
            m = t.transpose(mtp[:, i, d, :], Mrow[0:4, d, i * P:(i + 1) * P], sq[0:4, 0:4])
    m.then_inc(PE.sem, 1)
    PE.count += 1
    m = step(DV, PE.last(), v.tensor_tensor, gem[:, :, :, :], mtp, gb[:, :, :, :], ALU.add)
    give(b, [m])
    m = step(DV, [m], v.tensor_scalar, gem[:, :, :, :], gem[:, :, :, :], -1.0, 80.0, ALU.mult, ALU.min)
    em_m = step(AC, [m], a.activation, fl(gem[:, :, :, :]), fl(gem[:, :, :, :]), ACT.Exp)
    pads_dead = fence()
    DV.wait(pads_dead)
    dbg("gem", gem[:, :, :, :], [em_m])

    reach = {0: [[0, 1, 2, 3], [1, 2, 3], [2, 3], [3]], 1: [[0, 2, 3], [0, 1, 2, 3], [2], [2, 3]]}
    ranges = {0: [[(0, 4)], [(1, 4)], [(2, 4)], [(3, 4)]], 1: [[(0, 1), (2, 4)], [(0, 4)], [(2, 3)], [(2, 4)]]}
    nd_m = []
    prod_free = [[], []]
    dec_free = [[], []]
    prodP = [probs, probsT]
    ap = Pool([0, 1])
    sp_ = Pool([2, 3, 4, 5])
    hp_ = Pool([6, 7])
    flush_mods()
    all_in = ml_m[0] + ml_m[1] + mv_m
    wtmp_free = [[], []]

    def head_front(h):
        decs = []
        for d in range(2):
            b, ps, free = ap.take()
            pm = products(free + Mm + selneg_m, [(ps, selneg[:, h * P:(h + 1) * P], Mrow[0:4, d, 0:512])])
            dm = step(DV, [pm] + dec_free[d], v.tensor_tensor, dec[:, d, :].rearrange("p (j q) -> p j q", j=4),
                      ps.rearrange("p (j q) -> p j q", j=4),
                      sqc("neg_u" if d == 0 else "neg_l").unsqueeze(1).to_broadcast([P, 4, P]), ALU.add)
            decs.append((b, ps, pm, dm))
        st = []
        for s_ in range(4):
            b, ps, free = sp_.take()
            c0 = 0 if s_ < 2 else 256
            pm = products(free + all_in, [(ps[:, c0:512], mlT[1][:, h, s_ * P:(s_ + 1) * P], mlT[0][:, h, c0:512])])
            st.append((b, ps, pm, []))
        return decs, st

    fronts = {0: head_front(0)}
    for h in range(ML_H):
        decs, st = fronts.pop(h)
        pmk = {}
        for d in range(2):
            bD, psD, pmD, dmD = decs[d]
            readers = []
            for s_ in range(4):
                wl = xn[:, (2 * d + s_) % 2, 512:1024]
                wk = (2 * d + s_) % 2
                ems = []
                for (c0, c1) in ranges[d][s_]:
                    for (x0, x1) in ((c0, min(c1, s_)), (max(c0, s_ + 1), c1)):
                        if x0 < x1:
                            m = step(AC, [dmD, am] + wtmp_free[wk], a.activation, wl[:, x0 * P:x1 * P], psD[:, x0 * P:x1 * P],
                                     ACT.Exp, bias=ga_[:, s_, d, h:h + 1])
                            ems.append(m)
                            readers.append(m)
                m = step(AC, [dmD, am] + wtmp_free[wk], a.activation, wl[:, s_ * P:(s_ + 1) * P], dec[:, d, s_ * P:(s_ + 1) * P],
                         ACT.Exp, bias=ga_[:, s_, d, h:h + 1])
                ems.append(m)
                dlast = m
                b, ps, pm, rd = st[s_]
                for (c0, c1) in ranges[d][s_]:
                    m = step(DV, ems + [pm] + prod_free[d], v.scalar_tensor_tensor, prodP[d][:, s_, c0 * P:c1 * P],
                             ps[:, c0 * P:c1 * P], ML_D ** -0.5, wl[:, c0 * P:c1 * P], ALU.mult, ALU.mult)
                    rd.append(m)
                wtmp_free[wk] = [m]
                pmk[(d, s_)] = m
            dec_free[d] = [dlast]
            give(bD, readers + [dmD])
        for b, ps, pm, rd in st:
            give(b, rd)
        if h + 1 < ML_H:
            fronts[h + 1] = head_front(h + 1)
        for i in all4:
            b, ps, free = hp_.take()
            for d in range(2):
                srcs = [s_ for s_ in range(4) if i in reach[d][s_]]
                m = products(free + [pmk[(d, s_)] for s_ in srcs],
                             [(ps[:, d * 132:d * 132 + 129], prodP[d][:, s_, i * P:(i + 1) * P], mv[:, s_, h, 0:129]) for s_ in srcs])
            den = ps[:, 0:264].rearrange("p (d w) -> p d w", d=2)[:, :, 128]
            r_ = stat(2)
            mk = step(DV, [m], v.tensor_scalar, r_, den, -1.0, None, ALU.mult)
            mk = step(DV, [mk], v.tensor_tensor, r_, r_, den, ALU.max)
            mk = step(DV, [mk, em_m], v.tensor_tensor, r_, r_, gem[:, i, :, h], ALU.max)
            mk = step(DV, [mk], v.reciprocal, r_, r_)
            hd = h_tm[:, i, h * P:(h + 1) * P]
            mk = step(DV, [mk], v.tensor_scalar, hd, ps[:, 0:128], r_[:, 0:1], None, ALU.mult)
            mk = step(DV, [mk], v.scalar_tensor_tensor, hd, ps[:, 132:260], r_[:, 1:2], hd, ALU.mult, ALU.add)
            give(b, [mk])
            nd_m.append(mk)
        prod_free = [[m], [m]]

    sig_stage = fence()
    hm_m = {}

    def mo_evac(i, ps, mk):
        k = i % 4
        m1 = step(AC, [mk] + sig_stage, a.activation, probs[:, k, :], ps, ACT.Sigmoid)
        hm_m[i] = [step(DV, [m1] + nd_m, v.tensor_tensor, h_tm[:, i, :], h_tm[:, i, :], probs[:, k, :], ALU.mult)]
        return [m1]

    project_tm(gemm, "mo", uT, lambda i: um[i], all4, mo_evac)
    def head_norm(ap_, n, width, after, sq_buf, eng):
        E_, e_ = eng
        view = ap_.rearrange("p (h w) -> p h w", h=n)
        sqv = sq_buf.rearrange("p (h w) -> p h w", h=n)
        ss = stat(n)
        m = step(E_, after, e_.tensor_tensor, sqv, view, view, ALU.mult)
        m = step(DV, [m], v.tensor_reduce, ss, sqv, AX_X, ALU.add)
        m = step(GP, [m], g.tensor_scalar, ss, ss, 1.0 / width, EPS, ALU.mult, ALU.add)
        m = step(GP, [m], g.tensor_tensor, ss, ss, minus_half[:, 0:1].to_broadcast([P, n]), ALU.pow)
        return [step(E_, [m], e_.tensor_tensor, view, view, bc(ss, width), ALU.mult)]

    for i in all4:
        hm_m[i] = head_norm(h_tm[:, i, :], 4, 128, hm_m[i], probsT[:, i, :], (DV, v) if i % 2 else (GP, g))
    dbg("hm", h_tm, fence())

    def gated_cat_T(layer, tiles, tile0, halves, cat_m, gains):
        res = {i - tile0: [] for i in tiles}
        zm = {}
        for c in range(2):
            def z_evac(i, ps, mk, c=c):
                k = i % 4
                tmp = probs[:, k, :]
                m1 = step(AC, [mk] + probs_free[k] + junk_mark[0], a.activation, tmp, ps, ACT.Silu)
                x_ = halves[c][:, i - tile0, :]
                m2 = step(GP if i % 2 else DV, [m1] + cat_m[i - tile0], (g if i % 2 else v).tensor_tensor, x_, x_, tmp, ALU.mult)
                probs_free[k] = [m2]
                zm[(i, c)] = m2
                return [m1]
            project_tm(gemm, f"z{layer}{c}", uT, lambda i: um[i], tiles, z_evac)
        dead = PE.last()
        if layer == 0:
            fill(FILL["cat"])
        for i in tiles:
            for c in range(2):
                mk, _ = into_T(turn, halves[c][:, i - tile0, :], 512, tuple(x[:, 4 * c:4 * c + 4, :] for x in uT),
                               (i - tile0) * P, [zm[(i, c)]], gain=gains[c], dst_free=dead)
                res[i - tile0] += mk
        return res

    f = fence_all()
    for i in range(4):
        probs_free[i], probsT_free[i] = f, f
    catT_m = gated_cat_T(0, all4, 0, (a_tm, h_tm), {i: a_m[i] + hm_m[i] for i in all4}, (None, col("h_norm")))
    columns_1 = modulation_columns(1, rt_free[0])
    Hm = gate_and_out(["out00", "out01"], all4, 0, uT, catT_m, ctx_marks)
    dbg("h4", H[:, :, :], fence())
    fill(FILL["end"])

    f = fence_all()
    mod_m = columns_1()
    loaded = load_gates(1, f)
    load_row(0, "final_norm", f)
    um = modulated_norm([0, 1, 2, 3], Hm, mod_m, f)
    u_all = [x for i in range(4) for x in um[i]]
    gates_m = modulation_gates(1, [1], loaded, f)
    g_out, base = carve(0, 2, 512)
    gkT, base = carve(base, 2, 512)
    gqT, base = carve(base, 2, S)
    gv_tm, base = carve(base, 4, 512)
    BT = []
    for _ in range(2):
        w_, base = carve(base, 2, 512)
        BT.append(w_)
    lg, lg_end = carve(base, 4, 2, 256)
    gaT = arena[0:2 * GLA_RANK + 1, lg_end:lg_end + 512]
    wgate = arena[0:2 * GLA_RANK + 1, lg_end + 512:lg_end + 1024]
    wgate_m = [load(AC, "wgate", wgate, ins["wgate"], f)]
    attG, base = carve(base, 2, 2, 2, P)
    attX, base = carve(base, 2, 2, 2, P)
    attC, base = carve(base, 2, 2, 2, S)
    lev = []
    for k in range(2):
        lev.append(xn[:, k, 0:512].rearrange("p (c s) -> p c s", c=2))
        for _ in range(2):
            w_, base = carve(base, 2, S)
            lev.append(w_)
    kept = []

    scale_q = copy_out(lambda ft: gqT[:, ft, :], GLA_DK ** -0.5)
    keep_k = copy_out(lambda ft: gkT[:, ft - 2, :])
    project(gemm, "gqk.0", (0, 1), lambda _: u_all,
            lambda ft, w, K, k: (S, [x[:, k, ft * P:(ft + 1) * P] for x in w], [x[:, K, S:2 * S] for x in uT]), scale_q, 1)
    project(gemm, "gqk.1", (2, 3), lambda _: u_all,
            lambda ft, w, K, k: (512, [x[:, k, (ft - 2) * P:(ft - 1) * P] for x in w], [x[:, K, :] for x in uT]), keep_k, 1)
    project_tm(gemm, "gv", uT, lambda i: um[i], all4, copy_out_v(lambda i: gv_tm[:, i, :]))
    gone = step(DV, [], v.memset, gaT[2 * GLA_RANK:2 * GLA_RANK + 1, :], 1.0)

    def ga_evac(_, ps, mk):
        ga_marks.append(step(DV, [mk], v.tensor_copy, gaT[0:32, :], ps[0:32, :]))
        return ga_marks

    ga_marks = []
    project(gemm, "ga", (0,), lambda _: u_all, lambda _, w, K, k: (512, [x[:, k, :] for x in w], [x[:, K, :] for x in uT]), ga_evac, 1)
    gaT_m = ga_marks[0]
    lg_m = {}
    gate_ps = {}
    for i in all4:
        b, ps, free = gemm.take()
        pm = products(free + [gaT_m, gone] + wgate_m, [(ps, gaT[:, i * P:(i + 1) * P], wgate)])
        gate_ps[i] = (b, ps, pm)
    done = log_sigmoid([(gate_ps[i][1], probs[:, i, :], lg[:, i, :, :].rearrange("p d c -> p (d c)"), [gate_ps[i][2]]) for i in all4])
    for i in all4:
        lg_m[i] = done[i]
        give(gate_ps[i][0], [lg_m[i]])
    BT_m = []
    for d in range(2):
        for dt_ in range(2):
            b, ps, free = gemm.take()
            for r in range(2):
                o_ = ps[:, r * S:(r + 1) * S]
                full = sq[:, SQ["tri_u16" if d == 0 else "ones16b"] * P:][:, 0:2 * P]
                first, second = (2 * r, 2 * r + 1) if d == 0 else (2 * r + 1, 2 * r)
                tri = sqc("tri_u16" if d == 0 else "tri_l16")
                sub = o_[:, P:2 * P] if d == 0 else o_[:, 0:P]
                pm = products(free + [lg_m[2 * r], lg_m[2 * r + 1]],
                              [(o_, lg[:, first, d, dt_ * P:(dt_ + 1) * P], full), (sub, lg[:, second, d, dt_ * P:(dt_ + 1) * P], tri)])
            mk = step(AC if dt_ else DV, [pm], a.copy if dt_ else v.tensor_copy, BT[d][:, dt_, :], ps)
            give(b, [mk])
            BT_m.append(mk)
    dbg("BT", BT[0], BT_m)
    gla_in = kept + BT_m
    E_ctx, Kc = lev[0], [lev[1], lev[2]]
    Ql, Qc = lev[3], [lev[4], lev[5]]
    qc_m, kc_m = [], []
    e_prev = []
    for d in range(2):
        for dt_ in range(2):
            end = BT[d][:, dt_, S - 1:S] if d == 0 else BT[d][:, dt_, 0:1]
            e_prev.append(step(AC, gla_in + kc_m + qc_m, a.activation, E_ctx[:, dt_, :], BT[d][:, dt_, 0:S], ACT.Exp, scale=-1.0, bias=end))
        kc_m.append(step(DV, e_prev[-2:] + gla_in, v.tensor_tensor, Kc[d], gkT[:, :, 0:S], E_ctx, ALU.mult))
        m = step(AC, gla_in + qc_m, a.activation, Ql, BT[d][:, :, S:2 * S], ACT.Exp)
        qc_m.append(step(DV, [m], v.tensor_tensor, Qc[d], gqT, Ql, ALU.mult))
    attc_m = []
    for s_ in range(2):
        for par in range(2):
            b, ps, free = gemm.take()
            for c in range(2):
                pm = products(free + kc_m + qc_m, [(ps[:, c * S:(c + 1) * S], Kc[d][hp(par), c, s_ * P:(s_ + 1) * P], Qc[d][hp(par), c, :])
                                                  for d in range(2)])
            mk = step(AC, [pm], a.copy, attC[:, s_, par], ps.rearrange("p (c s) -> p c s", c=2))
            give(b, [mk])
            attc_m.append(mk)
    att_w = fence()
    for e in (DV, AC, GP):
        e.wait(att_w)
    prev = {}
    for par in range(2):
        b, ps, free = gemm.take()
        for tile in range(2):
            for c in range(2):
                at = (2 * tile + c) * P
                pm = products(free + kept, [(ps[:, at:at + P], gkT[hp(par), c, S + tile * P:S + (tile + 1) * P],
                                            gqT[hp(par), c, tile * P:(tile + 1) * P])])
        mk = step(AC, [pm] + BT_m, a.activation, attG[:, par].rearrange("p t c q -> p (t c q)"), ps, ACT.Copy, scale=2.0)
        give(b, [mk])
        prev[par] = mk
    zl = step(GP, [], g.memset, arena[:, base - 4 * 512:base], 0.0)
    lev_free = [[zl], [zl]]
    lev_pool = Pool([0, 1, 2, 3, 6, 7])
    cross_m = []
    blocks = [(hsize, d) for hsize in GLA_LEVELS + [128] for d in range(2)]

    def level_operands(n):
        hsize, d = blocks[n]
        nblk, k = 128 // hsize, n % 2
        E_, Q_, K_ = lev[3 * k:3 * k + 3]
        sp3 = lambda x_: x_.rearrange("p c (n two s) -> p c n two s", two=2, s=hsize)
        Bv = sp3(BT[d][:, :, S:2 * S])
        Ev, Qv, Kv, qv, kv = sp3(E_), sp3(Q_), sp3(K_), sp3(gqT), sp3(gkT[:, :, S:2 * S])
        th, sh = (1, 0) if d == 0 else (0, 1)
        seam = (Bv[:, :, :, 0, hsize - 1] if d == 0 else Bv[:, :, :, 1, 0]).unsqueeze(3).to_broadcast([P, 2, nblk, hsize])
        m1 = step(GP, lev_free[k], g.tensor_tensor, Ev[:, :, :, th, :], Bv[:, :, :, th, :], seam, ALU.subtract)
        m2 = step(GP, lev_free[k], g.tensor_tensor, Ev[:, :, :, sh, :], seam, Bv[:, :, :, sh, :], ALU.subtract)
        m3 = step(AC, [m1, m2], a.activation, E_, E_, ACT.Exp)
        m4 = step(DV, [m3] + lev_free[k], v.tensor_tensor, Qv[:, :, :, th, :], qv[:, :, :, th, :], Ev[:, :, :, th, :], ALU.mult)
        m5 = step(GP, [m3], g.tensor_tensor, Kv[:, :, :, sh, :], kv[:, :, :, sh, :], Ev[:, :, :, sh, :], ALU.mult)
        return Q_, K_, [m4, m5]

    ahead = level_operands(0)
    for n, (hsize, d) in enumerate(blocks):
        Q_, K_, ready = ahead
        th, sh = (1, 0) if d == 0 else (0, 1)
        banked = []
        for par in range(2):
            b, ps, free = lev_pool.take()
            for tile in range(2 if hsize < 128 else 1):
                s0, t0 = (tile * P, tile * P) if hsize < 128 else (sh * P, th * P)
                for c in range(2):
                    at = (2 * tile + c) * P
                    pm = products(free + ready, [(ps[:, at:at + P], K_[hp(par), c, s0:s0 + P], Q_[hp(par), c, t0:t0 + P])])
            banked.append((b, ps, pm))
        lev_free[n % 2] = [pm]
        if n + 1 < len(blocks):
            ahead = level_operands(n + 1)
        for par, (b, ps, pm) in enumerate(banked):
            if hsize < 128:
                mi = 7 * d + GLA_LEVELS.index(hsize)
                mask = gla_mask[:, mi * P:(mi + 1) * P].unsqueeze(1).to_broadcast([P, 4, P])
                mk = step(DV, [pm, prev[par]] + misc_m, v.copy_predicated, attG[:, par].rearrange("p t c q -> p (t c) q"), mask,
                          ps.rearrange("p (h q) -> p h q", h=4))
                prev[par] = mk
            else:
                mk = step(DV, [pm], v.tensor_copy, attX[:, sh, par], ps[:, 0:2 * P].rearrange("p (c q) -> p c q", c=2))
                cross_m.append(mk)
            give(b, [mk])
    att_m = attc_m + cross_m + [prev[0], prev[1]]
    g_m = {}
    for i in range(2):
        b, ps, free = gemm.take()
        for h in range(4):
            par, c = h % 2, h // 2
            keys = [(attC[:, s_, par, c, i * P:(i + 1) * P], s_) for s_ in range(2)]
            keys += [(attG[:, par, i, c, :], 2 + i), (attX[:, 1 - i, par, c, :], 3 - i)]
            terms = [(ps[:, h * P:(h + 1) * P], att, gv_tm[:, s_, h * P:(h + 1) * P]) for att, s_ in keys]
            pm = products(free + att_m + kept, terms)
        mk = step(DV, [pm], v.tensor_copy, g_out[:, i, :], ps)
        give(b, [mk])
        g_m[i] = [mk]
    for i in range(2):
        g_m[i] = head_norm(g_out[:, i, :], 4, 128, g_m[i], probs[:, i, :], (DV, v))
    dbg("gla", g_out, g_m[0] + g_m[1])

    f = fence_all()
    for i in range(4):
        probs_free[i], probsT_free[i] = f, f
    na_out, base = carve(2 * 512, 2, 512)
    nqT, base = carve(base, 4, S)
    nkT, base = carve(base, 4, 512)
    nv, base = carve(base, 4, 512)
    nab, base = carve(base, 2, 8, S)
    nab_m = [load(AC, "na_bias", nab, ins["na_bias"], f)]
    kept = []
    project_fm(gemm, "nq", uT, u_all, S, S, range(4), copy_out(lambda ft: nqT[:, ft, :], -NA_D ** -0.5))
    project_fm(gemm, "nk", uT, u_all, 0, 512, range(4), copy_out_v(lambda ft: nkT[:, ft, :]))
    project_tm(gemm, "nv", uT, lambda i: um[i], all4, copy_out_v(lambda i: nv[:, i, :]))
    bias_marks = nab_m
    n_m = {0: [], 1: []}
    attention([0, 1], 8, lambda h, qt: nqT[hp(h % 2), h // 2, qt * P:(qt + 1) * P], lambda h, n: nkT[hp(h % 2), h // 2, 0:n],
              lambda qt: 512, lambda h, j: nv[:, j, pair_of(h)], kept,
              finish_to(lambda qt: na_out[:, qt, :], lambda qt: n_m[qt]), bias=lambda h, qt: nab[:, qt, h, :], b0=S, nbias=S)
    dbg("na", na_out, n_m[0] + n_m[1])
    f = fence_all()
    catT_m = gated_cat_T(1, [2, 3], 2, (g_out, na_out), {i: g_m[i] + n_m[i] for i in range(2)},
                         (col("gla_norm"), None))
    Hm = gate_and_out(["out10", "out11"], [0, 1], 2, uT, catT_m, Hm)

    f = fence_all()
    r, rm, _ = rstd_of([H[:, i, :] for i in lat], D, [Hm[2], Hm[3]])
    outs = []
    for i in range(2):
        mk = step(DV, [rm] + row_m["final_norm"], v.scalar_tensor_tensor, xn[:, i, :], H[:, 2 + i, :], r[:, i:i + 1],
                  rowbuf[:, 0, :], ALU.mult, ALU.mult)
        outs.append(load(SP, f"out{i}", out[i * P:(i + 1) * P, :], xn[:, i, :], [mk]))
    SP.wait(outs + list(loads.values()))


def _t5_bucket(rel):
    half = NUM_BUCKETS // 2
    max_exact = half // 2
    sign = np.where(rel > 0, half, 0)
    n = np.abs(rel)
    nf = np.maximum(n, 1).astype(np.float32)
    large = max_exact + (np.log(nf / np.float32(max_exact)) / np.float32(math.log(MAX_DISTANCE / max_exact))
                         * np.float32(half - max_exact)).astype(np.int32)
    large = np.minimum(large, half - 1)
    return sign + np.where(n < max_exact, n, large)


def _constants():
    i = np.arange(P)
    s, t_ = i[:, None], i[None, :]
    f = lambda c: np.where(c, 1.0, 0.0).astype(np.float32)
    tri_u, tri_l = f(s <= t_), f(s >= t_)
    one = np.ones((P, P), np.float32)
    parts = {"ident": f(s == t_), "ones": one, "tri_u": tri_u, "tri_l": tri_l, "tri_u16": tri_u / 16, "ones16b": one / 16, "tri_l16": tri_l / 16, "neg_u": np.where(s <= t_, 0, NEG), "neg_l": np.where(s >= t_, 0, NEG)}
    sq = np.concatenate([parts[n] for n in SQ], 1).astype(np.float32)
    rel = np.arange(384)[None, :] - 128 - np.arange(P)[:, None]
    count = sum(((rel % dil == 0) & (np.abs(rel) <= dil * (window // (2 * dil)))).astype(np.int64) for window, dil in DILATED)
    lnc = np.where(count > 0, -np.log(np.maximum(count, 1)), 0.0).astype(np.float32)
    selneg = np.zeros((4, 4, P), np.float32)
    sel2 = np.zeros((2, 2, P), np.float32)
    for h in range(4):
        selneg[h, h] = -1.0
    for r in range(2):
        sel2[r, r] = 1.0
    masks = []
    for d in range(2):
        for hs in GLA_LEVELS:
            same = (s // (2 * hs)) == (t_ // (2 * hs))
            sh, th = (s // hs) % 2, (t_ // hs) % 2
            masks.append(same & ((sh == 0) & (th == 1) if d == 0 else (sh == 1) & (th == 0)))
    tt = np.arange(S)
    inv = 1.0 / (np.float32(10000.0) ** (np.arange(PAIRS, dtype=np.float32) / PAIRS))
    ang = np.concatenate([(tt // GRID_W)[:, None] * inv, (tt % GRID_W)[:, None] * inv], -1)
    cs = np.stack([np.cos(ang), np.sin(ang)], 1).astype(np.float32)
    rope = np.ascontiguousarray(cs.reshape(2, P, 2, 16).transpose(1, 0, 2, 3))
    return {"sq": sq, "lnc": lnc, "selneg": selneg.reshape(4, 4 * P), "sel2": sel2.reshape(2, 2 * P),
            "gla_mask": np.concatenate(masks, 1).astype(np.float32), "rope": rope}, rel, count


def _layout(i):
    c, rel, count = _constants()
    w = lambda n: np.ascontiguousarray(i[n][0] if i[n].ndim == 3 else i[n])
    dev = dict(c)
    for n in ("w_in", "w_o", "w_up", "w_down", "w_ple_proj", "w_ple_gate"):
        dev[n] = w(n)
    qa = dev["w_in"][:, :WA].reshape(D, NKVA, NHA // NKVA, HD).transpose(0, 2, 1, 3).reshape(D, WA)
    dev["w_in"] = np.concatenate([qa, dev["w_in"][:, WA:]], 1)
    for n in ("l0_w_mod", "l0_w_in", "l0_w_out", "l1_w_mod", "l1_w_in", "l1_w_out"):
        dev[n] = w(n + "_2")
    dev["w_uq"], dev["w_ukv"] = w("l0_mla_w_uq_2"), w("l0_mla_w_ukv_2")
    dev["x"], dev["ctx"] = i["x"][0], i["ctx_2"][0]
    dev["pT"] = np.ascontiguousarray(i["p"][0, 0].T)

    def columns(vec):
        return np.asarray(vec).reshape(-1, P).T

    conv_w = np.concatenate([columns(i["l0_mlstm_conv_w_2"][j]) for j in range(3)], 1)
    cc = np.stack([columns(i["c_ctx_2"]), columns(i["c_2"][0])], 2).reshape(P, 16)
    vecs = {"g_pre_mix": i["g_pre_mix"], "g_out_a": i["g_out_a"], "g_out_b": i["g_out_b"], "g_pre_mlp": i["g_pre_mlp"],
            "l0_norm": i["l0_norm_2"], "l1_norm": i["l1_norm_2"], "l0_b_mod": i["l0_b_mod_2"], "l1_b_mod": i["l1_b_mod_2"],
            "q_norm": i["l0_mla_q_norm_2"], "kv_norm": i["l0_mla_kv_norm_2"], "h_norm": i["l0_mlstm_norm_2"],
            "gla_norm": i["l1_gla_norm_2"], "conv_b": i["l0_mlstm_conv_b_2"]}
    dev["cols"] = np.concatenate([columns(vecs[n]) if n in vecs else (conv_w if n == "conv_w" else cc) for n in COLS], 1)
    dev["rows"] = np.stack([i["g_post_mix"][0], i["g_post_mlp"][0], i["b_ple_gate"][0], i["g_post_ple"][0],
                            i["l0_b_mod_2"][2 * D:], i["l1_b_mod_2"][2 * D:], i["final_norm_2"]])
    gates = np.stack([i["l0_mlstm_b_i_2"], i["l0_mlstm_b_f_2"]], 1).reshape(-1)
    dev["small_rows"] = np.concatenate([i["sink_a"][0], gates])
    table = i["rel_bias_table"]
    bias = table[_t5_bucket(rel)].transpose(0, 2, 1).copy()
    keep = np.zeros(bias.shape, bool)
    keep[:, 0:8] = (np.abs(rel) <= WINDOW_A)[:, None]
    keep[:, 8:16] = (count > 0)[:, None]
    bias[~keep] = NEG
    dev["bias_t5"] = bias
    wg = np.zeros((2 * GLA_RANK + 1, 512), np.float32)
    for d in range(2):
        wg[d * GLA_RANK:(d + 1) * GLA_RANK, d * 256:(d + 1) * 256] = i["l1_gla_w_gate_2"][d]
        wg[2 * GLA_RANK, d * 256:(d + 1) * 256] = i["l1_gla_b_gate_2"][d]
    dev["wgate"] = wg
    tok = np.arange(S)
    r, cc_ = tok // GRID_W, tok % GRID_W
    kh = min(NA_KH, ROWS)
    r0 = np.clip(r - kh // 2, 0, ROWS - kh)
    c0 = np.clip(cc_ - NA_KW // 2, 0, GRID_W - NA_KW)
    inside = ((r[None, :] >= r0[:, None]) & (r[None, :] < r0[:, None] + kh)
              & (cc_[None, :] >= c0[:, None]) & (cc_[None, :] < c0[:, None] + NA_KW))
    dr = np.where(inside, r[None, :] - r[:, None] + NA_KH - 1, 0)
    dc = np.where(inside, cc_[None, :] - cc_[:, None] + NA_KW - 1, 0)
    nb = i["l1_na_rpb_2"][:, dr, dc].copy()
    nb[:, ~inside] = NEG
    dev["na_bias"] = np.ascontiguousarray(nb.reshape(NA_H, 2, P, S).transpose(2, 1, 0, 3))
    return {n: np.ascontiguousarray(x_) for n, x_ in dev.items()}


def kernel(**inputs):
    import concourse.bacc as bacc
    from concourse.bass_utils import run_bass_kernel_spmd

    dev = _layout({n: np.asarray(x_) for n, x_ in inputs.items()})
    nc = bacc.Bacc("TRN2", target_bir_lowering=False, num_devices=1)
    aps = {n: nc.dram_tensor("in_" + n, x_.shape, mybir.dt.from_np(x_.dtype), kind="ExternalInput").ap() for n, x_ in dev.items()}
    out = nc.dram_tensor("out_h", (S, D), F32, kind="ExternalOutput").ap()
    build(nc, aps, out)
    r = run_bass_kernel_spmd(nc, [{"in_" + n: x_ for n, x_ in dev.items()}], core_ids=[0])
    return r.results[0]["out_h"].reshape(1, S, D)
```
